# Optimizing a Trainium2 kernel written in Bass

```python
import jax, jax.numpy as jnp
from jax import lax
import numpy as np

D_MODEL = 1024
BATCH = 1
SEQ = 512
DEPTH = 2

CTX_LEN = 256
GRID_W = 64

RWKV_HEAD_DIM = 64
RWKV_DIM = D_MODEL
RWKV_HEADS = RWKV_DIM // RWKV_HEAD_DIM
DECAY_LORA = 64
ICLR_LORA = 64
GATE_LORA = 128
CONV_DIM = D_MODEL // 2
CONV_WIDTH = 31
SGU_DIM = D_MODEL // 2
SGU_GROUPS = 8
CHUNK = 128
D_FF = ((8 * D_MODEL // 3 + 255) // 256) * 256
N_BRANCH = 3
NORM_EPS = 1e-6
LN_EPS = 1e-5
GN_EPS = 64e-5

OFF_R = 0
OFF_K = OFF_R + RWKV_DIM
OFF_V = OFF_K + RWKV_DIM
OFF_WF = OFF_V + RWKV_DIM
OFF_WB = OFF_WF + DECAY_LORA
OFF_AF = OFF_WB + DECAY_LORA
OFF_AB = OFF_AF + ICLR_LORA
OFF_G = OFF_AB + ICLR_LORA
RWKV_COLS = OFF_G + GATE_LORA
OFF_CONV = RWKV_COLS
OFF_SGU = OFF_CONV + 2 * CONV_DIM
OFF_GATE = OFF_SGU + 2 * SGU_DIM
P_IN = OFF_GATE + N_BRANCH * D_MODEL

kernel_name = "hybrid_rwkv7_conformer_sgu_prefix_dit"

def _standardize(x, eps):
    xf = x.astype(jnp.float32)
    xc = xf - jnp.mean(xf, -1, keepdims=True)
    return xc * lax.rsqrt(jnp.mean(xc * xc, -1, keepdims=True) + eps)

def rms_norm(x, g):
    xf = x.astype(jnp.float32)
    y = xf * lax.rsqrt(jnp.mean(xf * xf, -1, keepdims=True) + NORM_EPS)
    return (y * g.astype(jnp.float32)).astype(x.dtype)

def layer_norm(x, g, b):
    return (_standardize(x, LN_EPS) * g + b).astype(x.dtype)

def modulate(h, shift, scale):
    return h * (1 + scale) + shift

def short_conv(z, w):
    zp = jnp.pad(z, ((0, 0), (1, 1), (0, 0)))
    return zp[:, :-2] * w[0] + zp[:, 1:-1] * w[1] + zp[:, 2:] * w[2]

def to_heads(t):
    B, T = t.shape[:2]
    return t.astype(jnp.float32).reshape(B, T, RWKV_HEADS, RWKV_HEAD_DIM)

def rwkv_inputs(z, w0, w_up, a0, a_up, k_k, k_a):
    k = z[..., OFF_K:OFF_V]
    v = to_heads(z[..., OFF_V:OFF_WF])
    kk = to_heads(k * k_k)
    kk = kk * lax.rsqrt(jnp.maximum(jnp.sum(kk * kk, -1, keepdims=True), 1e-24))
    kf = k.astype(jnp.float32)
    dirs = []
    for d, (ow, oa) in enumerate(((OFF_WF, OFF_AF), (OFF_WB, OFF_AB))):
        lw = (w0[d] + jnp.tanh(z[..., ow:ow + DECAY_LORA]) @ w_up[d]).astype(jnp.float32)
        decay = jnp.exp(-jnp.exp(-jax.nn.softplus(-lw) - 0.5))
        a = jax.nn.sigmoid((a0[d] + z[..., oa:oa + ICLR_LORA] @ a_up[d]).astype(jnp.float32))
        k_d = kf * (1.0 + (a - 1.0) * k_a.astype(jnp.float32))
        dirs.append((to_heads(decay), to_heads(k_d), kk * to_heads(a)))
    return to_heads(k), v, kk, dirs

def wkv_scan(S0, decay, k, v, kk, kka, r, reverse):
    want_y = r is not None

    def step(S, inp):
        w_t, k_t, v_t, kk_t, kka_t = inp[:5]
        sa = jnp.einsum('bhvk,bhk->bhv', S, kk_t)
        S = (S * w_t[:, :, None, :] - sa[..., None] * kka_t[:, :, None, :]
             + v_t[..., None] * k_t[:, :, None, :])
        y = jnp.einsum('bhvk,bhk->bhv', S, inp[5]) if want_y else None
        return S, y

    seq = (decay, k, v, kk, kka) + ((r,) if want_y else ())
    xs = tuple(jnp.swapaxes(t, 0, 1) for t in seq)
    S, ys = lax.scan(step, S0, xs, reverse=reverse)
    return S, (jnp.swapaxes(ys, 0, 1) if want_y else None)

def rwkv_output(y, r, k, v, gz, gn_g, gn_b, r_k, g_up, w_out, dtype):
    B, T = y.shape[:2]
    yn = _standardize(y, GN_EPS).reshape(B, T, RWKV_DIM) * gn_g + gn_b
    bonus = jnp.sum(r * k * r_k.reshape(RWKV_HEADS, RWKV_HEAD_DIM), -1, keepdims=True) * v
    g = jax.nn.sigmoid(gz) @ g_up
    return ((yn + bonus.reshape(B, T, RWKV_DIM)).astype(dtype) * g) @ w_out

def conformer_branch(z, dw, dw_b, ln_g, ln_b, w_out, grid, horizontal):
    u = z[..., :CONV_DIM] * jax.nn.sigmoid(z[..., CONV_DIM:])
    B, T, C = u.shape
    if grid:
        u4 = u.reshape(B, T // GRID_W, GRID_W, C)
        w = dw[None, :, None, :] if horizontal else dw[:, None, None, :]
    else:
        u4 = u.reshape(B, 1, T, C)
        w = dw[None, :, None, :]
    y = lax.conv_general_dilated(u4, w.astype(u4.dtype), (1, 1), 'SAME',
                                 dimension_numbers=('NHWC', 'HWIO', 'NHWC'),
                                 feature_group_count=C)
    y = layer_norm(y.reshape(B, T, C) + dw_b, ln_g, ln_b)
    return jax.nn.silu(y) @ w_out

def sgu_branch(z, ln_g, ln_b, w_s, b_s, w_out):
    z = jax.nn.gelu(z)
    u, v = z[..., :SGU_DIM], z[..., SGU_DIM:]
    v = layer_norm(v, ln_g, ln_b)
    B, T, _ = v.shape
    v = v.reshape(B, T // CHUNK, CHUNK, SGU_GROUPS, SGU_DIM // SGU_GROUPS)
    v = jnp.einsum('gpq,bnqgd->bnpgd', w_s, v) + b_s.T[:, :, None]
    return (u * v.reshape(B, T, SGU_DIM)) @ w_out

def merge(z, branches, w_o):
    B, T, _ = z.shape
    g = jax.nn.sigmoid(z[..., OFF_GATE:].reshape(B, T, N_BRANCH, D_MODEL))
    m = branches[0] * g[:, :, 0] + branches[1] * g[:, :, 1] + branches[2] * g[:, :, 2]
    return m @ w_o

def swiglu(h, w_in, w_out):
    gu = h @ w_in
    return (jax.nn.silu(gu[..., :D_FF]) * gu[..., D_FF:]) @ w_out

def setup_inputs(seed: int = 0) -> dict:
    key = jax.random.key(seed)
    k = jax.random.split(key, 36)
    L, D, RD = DEPTH, D_MODEL, RWKV_DIM

    def nrm(i, shape, scale):
        return jax.random.normal(k[i], shape, jnp.float32) * scale

    shift_base = jnp.array([0.25, 1.0, 0.25], jnp.float32)[None, :, None]
    return {
        'x': nrm(0, (BATCH, SEQ, D), 1.0),
        'c': nrm(1, (BATCH, D), 1.0),
        'ctx': nrm(2, (BATCH, CTX_LEN, D), 1.0),
        'c_ctx': nrm(3, (D,), 1.0),
        'w_mod': nrm(4, (L, D, 6 * D), 0.5 * D ** -0.5),
        'b_mod': nrm(5, (L, 6 * D), 0.01),
        'norm1_g': 1.0 + nrm(6, (L, D), 0.05),
        'norm2_g': 1.0 + nrm(7, (L, D), 0.05),
        'w_in': nrm(8, (L, D, P_IN), D ** -0.5),
        'rwkv_shift': shift_base + nrm(9, (L, 3, RWKV_COLS), 0.1),
        'rwkv_w0': jax.random.uniform(k[10], (L, 2, RD), jnp.float32, -4.0, 1.0),
        'rwkv_w_up': nrm(11, (L, 2, DECAY_LORA, RD), 0.5 * DECAY_LORA ** -0.5),
        'rwkv_a0': nrm(12, (L, 2, RD), 0.5),
        'rwkv_a_up': nrm(13, (L, 2, ICLR_LORA, RD), 0.5 * ICLR_LORA ** -0.5),
        'rwkv_g_up': nrm(14, (L, GATE_LORA, RD), GATE_LORA ** -0.5),
        'rwkv_k_k': 0.85 + nrm(15, (L, RD), 0.05),
        'rwkv_k_a': 1.0 + nrm(16, (L, RD), 0.05),
        'rwkv_r_k': nrm(17, (L, RD), 0.1),
        'rwkv_gn_g': 1.0 + nrm(18, (L, RD), 0.05),
        'rwkv_gn_b': nrm(19, (L, RD), 0.01),
        'rwkv_out': nrm(20, (L, RD, D), RD ** -0.5),
        'conv_dw': nrm(21, (L, CONV_WIDTH, CONV_DIM), CONV_WIDTH ** -0.5),
        'conv_dw_b': nrm(22, (L, CONV_DIM), 0.01),
        'conv_ln_g': 1.0 + nrm(23, (L, CONV_DIM), 0.05),
        'conv_ln_b': nrm(24, (L, CONV_DIM), 0.01),
        'conv_out': nrm(25, (L, CONV_DIM, D), CONV_DIM ** -0.5),
        'sgu_ln_g': 1.0 + nrm(26, (L, SGU_DIM), 0.05),
        'sgu_ln_b': nrm(27, (L, SGU_DIM), 0.01),
        'sgu_w': nrm(28, (L, SGU_GROUPS, CHUNK, CHUNK), 0.5 * CHUNK ** -0.5),
        'sgu_b': 1.0 + nrm(29, (L, SGU_GROUPS, CHUNK), 0.1),
        'sgu_out': nrm(30, (L, SGU_DIM, D), SGU_DIM ** -0.5),
        'w_merge': nrm(31, (L, D, D), D ** -0.5),
        'ffn_w_in': nrm(32, (L, D, 2 * D_FF), D ** -0.5),
        'ffn_w_out': nrm(33, (L, D_FF, D), D_FF ** -0.5),
        'final_norm_g': 1.0 + nrm(34, (D,), 0.05),
    }

def reference(x, c, ctx, c_ctx, w_mod, b_mod, norm1_g, norm2_g, w_in, rwkv_shift,
              rwkv_w0, rwkv_w_up, rwkv_a0, rwkv_a_up, rwkv_g_up, rwkv_k_k, rwkv_k_a,
              rwkv_r_k, rwkv_gn_g, rwkv_gn_b, rwkv_out, conv_dw, conv_dw_b, conv_ln_g,
              conv_ln_b, conv_out, sgu_ln_g, sgu_ln_b, sgu_w, sgu_b, sgu_out, w_merge,
              ffn_w_in, ffn_w_out, final_norm_g):
    s0 = jnp.zeros((x.shape[0], RWKV_HEADS, RWKV_HEAD_DIM, RWKV_HEAD_DIM), jnp.float32)
    sc_lat = jax.nn.silu(c)
    sc_ctx = jax.nn.silu(c_ctx)
    h_ctx = ctx
    for l in range(DEPTH):
        need_ctx = l < DEPTH - 1
        sh1, sc1, g1, sh2, sc2, g2 = jnp.split((sc_lat @ w_mod[l] + b_mod[l])[:, None, :], 6, axis=-1)
        n_c = 6 if need_ctx else 2
        mc = jnp.split(sc_ctx @ w_mod[l][:, :n_c * D_MODEL] + b_mod[l][:n_c * D_MODEL], n_c)

        hx = modulate(rms_norm(x, norm1_g[l]), sh1, sc1)
        hc = modulate(rms_norm(h_ctx, norm1_g[l]), mc[0], mc[1])
        zx = hx @ w_in[l]
        zc = hc @ (w_in[l] if need_ctx else w_in[l][:, :RWKV_COLS])

        zr_x = short_conv(zx[..., :RWKV_COLS], rwkv_shift[l])
        zr_c = short_conv(zc[..., :RWKV_COLS], rwkv_shift[l])
        lora = (rwkv_w0[l], rwkv_w_up[l], rwkv_a0[l], rwkv_a_up[l], rwkv_k_k[l], rwkv_k_a[l])
        k_x, v_x, kk_x, dirs_x = rwkv_inputs(zr_x, *lora)
        k_c, v_c, kk_c, dirs_c = rwkv_inputs(zr_c, *lora)
        r_x = to_heads(zr_x[..., OFF_R:OFF_K])
        r_c = to_heads(zr_c[..., OFF_R:OFF_K]) if need_ctx else None
        y_lat, y_ctx = [], []
        for d, rev in enumerate((False, True)):
            dec_c, kd_c, kka_c = dirs_c[d]
            s_ctx, yc = wkv_scan(s0, dec_c, kd_c, v_c, kk_c, kka_c, r_c, rev)
            dec_x, kd_x, kka_x = dirs_x[d]
            _, yx = wkv_scan(s_ctx, dec_x, kd_x, v_x, kk_x, kka_x, r_x, rev)
            y_lat.append(yx)
            y_ctx.append(yc)
        out_par = (rwkv_gn_g[l], rwkv_gn_b[l], rwkv_r_k[l], rwkv_g_up[l], rwkv_out[l])
        a_x = rwkv_output(y_lat[0] + y_lat[1], r_x, k_x, v_x, zr_x[..., OFF_G:RWKV_COLS],
                          *out_par, x.dtype)
        conv_par = (conv_dw[l], conv_dw_b[l], conv_ln_g[l], conv_ln_b[l], conv_out[l])
        b_x = conformer_branch(zx[..., OFF_CONV:OFF_SGU], *conv_par, True, l % 2 == 0)
        sgu_par = (sgu_ln_g[l], sgu_ln_b[l], sgu_w[l], sgu_b[l], sgu_out[l])
        c_x = sgu_branch(zx[..., OFF_SGU:OFF_GATE], *sgu_par)
        x_new = x + g1 * merge(zx, (a_x, b_x, c_x), w_merge[l])
        if need_ctx:
            a_c = rwkv_output(y_ctx[0] + y_ctx[1], r_c, k_c, v_c, zr_c[..., OFF_G:RWKV_COLS],
                              *out_par, h_ctx.dtype)
            b_c = conformer_branch(zc[..., OFF_CONV:OFF_SGU], *conv_par, False, True)
            c_c = sgu_branch(zc[..., OFF_SGU:OFF_GATE], *sgu_par)
            h_ctx = h_ctx + mc[2] * merge(zc, (a_c, b_c, c_c), w_merge[l])
        x = x_new

        x = x + g2 * swiglu(modulate(rms_norm(x, norm2_g[l]), sh2, sc2), ffn_w_in[l], ffn_w_out[l])
        if need_ctx:
            h_ctx = h_ctx + mc[5] * swiglu(modulate(rms_norm(h_ctx, norm2_g[l]), mc[3], mc[4]),
                                           ffn_w_in[l], ffn_w_out[l])
    return rms_norm(x, final_norm_g)


_drawn_inputs = setup_inputs


def setup_inputs(seed=0):
    import zlib

    import numpy as np

    out = dict(_drawn_inputs(seed))
    spreads = {}
    factors = {'ctx': 3.03,
     'c_ctx': 3.975,
     'b_mod': 3.329,
     'rwkv_w_up': 5.279,
     'rwkv_k_k': 7.527,
     'rwkv_k_a': 5.205,
     'rwkv_gn_g': 8.0,
     'rwkv_gn_b': 58.724,
     'conv_dw_b': 8.0,
     'conv_ln_g': 6.763,
     'conv_ln_b': 46.998,
     'sgu_ln_g': 21.798,
     'sgu_ln_b': 64.0,
     'sgu_b': 3.417,
     'norm2_g': 3.936}
    for name, (base, spread) in spreads.items():
        noise = np.random.default_rng([zlib.crc32(name.encode()), seed]).standard_normal(out[name].shape)
        drawn = base * np.exp(spread * noise) if base else spread * noise
        out[name] = __import__('jax').numpy.asarray(drawn.astype(out[name].dtype))
    for name, factor in factors.items():
        out[name] = (out[name] * factor).astype(out[name].dtype)
    return out
```

```python
from contextlib import ExitStack

import numpy as np

import concourse.bass as bass
from concourse import mybir

ALU = mybir.AluOpType
ACT = mybir.ActivationFunctionType
F32 = mybir.dt.float32

P = 128
D = 1024
DEPTH = 2
CTX = 256
LAT = 512
T = CTX + LAT
GRID_W = 64
KT = D // P
HD = 64
C = 64
NCH = T // C
CTX_CH = CTX // C
RD = D
CONV = D // 2
SGU = D // 2
CT = CONV // P
TAPS = 31
DFF = ((8 * D // 3 + 255) // 256) * 256
FT = DFF // P
OFF_K, OFF_V, OFF_W = RD, 2 * RD, 3 * RD
OFF_A, OFF_G = OFF_W + 128, OFF_W + 256
OFF_CONV = OFF_G + 128
OFF_SGU = OFF_CONV + 2 * CONV
OFF_GATE = OFF_SGU + 2 * SGU
P_IN = OFF_GATE + 3 * D
GROUPS = 8
KAPPA = float(np.exp(-0.5))
BW = 8 * P

C_ID64, C_ID, C_ONES, C_HEADS, C_EPS, C_MASK = 0, 64, 192, 320, 448, 452
EPS = (1e-6, 1e-5, 64e-5)
MASKS = ["strict", "incl", "first"] + [f"lv{n}" for n in range(1, 6)]
NCONST = C_MASK + 2 * len(MASKS) * C

PAR = {}
_at = 0
for _name, _n in (("b_mod", 48), ("n1g", 8), ("n2g", 8), ("shift", 9), ("dw", CT * TAPS), ("dwb", CT),
                  ("clg", CT), ("clb", CT), ("slg", CT), ("slb", CT), ("fin", 8)):
    PAR[_name] = _at
    _at += _n
NPAR = _at

PP = {n: i for i, n in enumerate(
    ["r0", "r1", "r2", "k0", "k1", "k2", "v0", "v1", "v2", "w00", "w01", "a00", "a01",
     "kk", "ka", "rk", "gng", "gnb"])}
NPP = len(PP)

H0, YA0, LW, LA, LG = 0, 8, 16, 17, 18
DIR0 = 19
S_R, S_KK, S_B, S_K, S_BE, S_KE = range(6)
S_A, S_BT, S_RB, S_RK, S_BET, S_KET, S_KKT, S_S = range(6, 14)
R_, K_, V_, KK_, T0, T1, T2, VT, GZ = range(47, 56)
KD = 56
SCANMASK = 58
NSLOT = 59
M0, X0 = 19, 27
CU, CY, SU, SV, VTK = 35, 39, 43, 47, 51
G0 = 55
H1, SGW, SGB, MTMP = 19, 23, 25, 51
ACT0 = 35


class Steps:

    def __init__(self, sem, names, turns=1, lead=False):
        self.sem, self.names, self.turns, self.lead = sem, list(names), turns, lead
        self.index = {n: i for i, n in enumerate(self.names)}
        assert len(self.index) == len(self.names)
        self.k = 0

    def at(self, name, turn=0, back=0):
        return self.sem, turn * len(self.names) + (int(self.lead) - back) * len(self.names) + self.index[name] + 1

    def mark(self, name):
        assert self.names[self.k] == name, (self.names[self.k], name)
        self.k = (self.k + 1) % len(self.names)
        return self.sem, 1

    def end(self):
        return self.sem, (self.turns + int(self.lead)) * len(self.names)

    def credit(self, eng):
        if self.lead:
            eng.sem_inc(self.sem, len(self.names))


def names_norm():
    return dict(PE=["sum"], A=[f"sq{j}" for j in range(KT)] + ["rms"] + [f"h{j}" for j in range(KT)],
                V=["rstd"] + [f"xn{j}" for j in range(KT)], G=[])


def names_lora():
    return dict(PE=["w", "a", "g", "pad"],
                A=["raw0", "raw1", "raw2", "act0", "act2"],
                V=[f"s{n}{x}" for n in range(3) for x in "abc"], G=[])


LEVELS = range(1, 6)
DIRS = (0, 1)
CHAIN = range(1, NCH - 1)


def names_pair():
    pe = ["zr", "zk", "zv", "lw0", "la0", "lw1", "la1", "gu", "kkn", "vT"]
    for d in DIRS:
        pe += [f"kkT{d}", f"bT{d}", f"kT{d}"]
    for d in DIRS:
        pe += [f"A{d}", f"B{d}", f"RB{d}", f"RK{d}"]
    pe += ["BV0", "BV1"]
    for n in LEVELS:
        pe += [f"T{n}{d}" for d in DIRS] + [f"U{n}{d}" for d in DIRS]
    for d in DIRS:
        pe += [f"U0{d}", f"G{d}"]
    for d in DIRS:
        pe += [f"MT{d}", f"N{d}", f"Q{d}"]
    wide = list(pe)
    pe += [f"c{n}{d}" for n in CHAIN for d in DIRS]
    wide += ["chain0", "chain1", "Y", "mean", "var", "bonus"]
    pe += ["Y", "mean", "var", "bonus"]
    a = ["raw_r", "raw_k", "raw_v", "sw0", "sa0", "sw1", "sa1", "gz", "kksq", "kks"]
    for d in DIRS:
        a += [f"Ei{d}", f"En{d}", f"Ee{d}"]
    a += ["vT"]
    for d in DIRS:
        a += [f"kkT{d}", f"bT{d}", f"kT{d}"]
    a += ["A0", "A1", "BV0", "BV1"]
    for d in DIRS:
        a += [f"U0{d}", f"G{d}"]
    a += ["N0", "N1", "yc", "ysq", "ysd", "yn"]
    v = ["ra", "rb", "rc", "ka", "kb", "kc", "kk0", "va", "vb", "vc", "L0", "kkm", "kkr", "kk", "L1"]
    for d in DIRS:
        v += [f"rP{d}", f"kkP{d}", f"b{d}", f"bQ{d}"]
    for d in DIRS:
        v += [f"X1a{d}", f"X1b{d}", f"X{d}", f"B{d}", f"RB{d}", f"RK{d}"]
    for n in LEVELS:
        v += [f"T{n}{d}" for d in DIRS]
        for d in DIRS:
            v += [f"XT{n}{d}"] + ([f"Xt{n}{d}"] if n < 5 else [])
    v += ["MT0", "Q0", "MT1", "Q1"]
    v += [f"c{n}{d}" for n in CHAIN for d in DIRS]
    v += ["yc", "rs", "ynr", "bon", "bv", "yb", "ya"]
    g = ["pp", "omk", "Le0", "Le1", "Li1"]
    for d in DIRS:
        g += [f"kt{d}", f"kd{d}", f"kQ{d}", f"bE{d}", f"kE{d}"]
    g += ["D0", "D1"]
    return dict(PE=pe, A=a, V=v, G=g), wide


def names_branch(l):
    taps = conv_taps(l)
    pe = []
    for j in range(CT):
        pe += [f"cb{j}", f"ca{j}"]
    pe += [f"su{j}" for j in range(CT)] + [f"sv{j}" for j in range(CT)]
    pe += ["cmean", "cvar", "smean", "svar"] + [f"tr{j}" for j in range(CT)] + [f"sp{j}" for j in range(CT)]
    a = [f"cb{j}" for j in range(CT)] + [f"su{j}" for j in range(CT)] + [f"sv{j}" for j in range(CT)]
    a += [f"csq{j}" for j in range(CT)] + [f"ssq{j}" for j in range(CT)]
    a += ["csd", "ssd"] + [f"cs{j}" for j in range(CT)]
    a += [f"sn{j}" for j in range(CT)] + [f"tr{j}" for j in range(CT)]
    v = []
    for j in range(CT):
        v += [f"u{j}"] + [f"y{j}_{n}" for n in range(len(taps))]
    v += [f"cc{j}" for j in range(CT)] + [f"sc{j}" for j in range(CT)] + ["cr"]
    v += [f"cn{j}" for j in range(CT)] + ["sr"] + [f"sm{j}" for j in range(CT)]
    for j in range(CT):
        v += [f"sp{j}", f"uv{j}"]
    return dict(PE=pe, A=a, V=v, G=[])


MERGE_TILES = 4


def names_merge():
    pe, a, v, g = [], [], [], []
    for q in range(MERGE_TILES):
        for b in range(3):
            pe += [f"g{b}{q}", f"p{b}{q}"]
            a += [f"g{b}{q}"]
            v += [f"p{b}{q}"]
            if b:
                g += [f"m{b}{q}"]
    return dict(PE=pe, A=a, V=v, G=g)


def names_outproj():
    return dict(PE=[f"o{q}" for q in range(4)], A=[], V=[f"x{q}" for q in range(4)], G=[])


def names_ffn():
    return dict(PE=["g0", "u0", "g1", "u1"], A=["s0", "s1"], V=["a0", "a1"], G=[])


def conv_taps(l):
    reach = 15 if l % 2 == 0 else (LAT // GRID_W) - 1
    return [0] + [o for n in range(1, reach + 1) for o in (-n, n)]


def build(nc, x_in, c_in, w_stream, par_in, const_in, scanmask_in, sgu_w_in, sgu_b_in, out):
    spill = nc.dram_tensor("x_spill", (P, KT * T), F32, kind="Internal").ap()
    with ExitStack() as st:
        def sem(name):
            return st.enter_context(nc.semaphore(name))

        arena = st.enter_context(nc.sbuf_tensor("arena", [P, NSLOT * T], F32))
        ring = st.enter_context(nc.sbuf_tensor("ring", [P, 4 * BW], F32))
        const = st.enter_context(nc.sbuf_tensor("const", [P, NCONST], F32))
        par = st.enter_context(nc.sbuf_tensor("par", [P, NPAR], F32))
        cvec = st.enter_context(nc.sbuf_tensor("cvec", [P, 2 * KT], F32))
        sc = st.enter_context(nc.sbuf_tensor("sc", [P, 2 * KT], F32))
        mod = st.enter_context(nc.sbuf_tensor("mod", [P, 48 * 2], F32))
        a_mod = st.enter_context(nc.sbuf_tensor("a_mod", [P, 2 * 2 * KT], F32))
        pp = st.enter_context(nc.sbuf_tensor("pp", [P, NPP + 1], F32))
        psum = st.enter_context(nc.psum_tensor("psum", [P, 4, 1024], F32))

        w_in = [sem(f"weights_in_{i}") for i in range(4)]
        s_load = sem("inputs_loaded")
        s_settled = sem("settled")
        s_par = sem("params_loaded")
        s_spill = sem("x_spilled")
        s_back = sem("x_reloaded")
        s_sgu = sem("sgu_params_loaded")
        s_out = sem("output_stored")

        phases, at_end = {}, []

        def phase(key, names, turns=1, lead=False, chunks=()):
            ph = {e: Steps(sem(f"{key}_{e}"), ns, turns, lead) for e, ns in names.items() if ns}
            ph["chunks"], ph["turns"] = list(chunks), turns
            phases[key] = ph
            at_end.append((key, ph))
            return ph

        phase("cond", dict(PE=[], A=["silu"], V=[], G=[]))
        for l in range(DEPTH):
            phase(f"mod{l}", dict(PE=["m0", "m1", "m2", "m3"], A=[], V=[], G=[]), 12, chunks=["m0", "m1", "m2", "m3"])
            phase(f"modv{l}", dict(PE=[], A=[], V=["mod", "a1", "a2"], G=[]))
            phase(f"norm1_{l}", names_norm())
            phase(f"lora{l}", names_lora(), chunks=["w", "a", "g", "pad"])
            phase(f"pair{l}", names_pair()[0], KT, lead=True, chunks=["zr", "zk", "zv", "gu"])
            ch = []
            for j in range(CT):
                ch += [f"cb{j}", f"ca{j}"]
            phase(f"branch{l}", names_branch(l), chunks=ch + [f"su{j}" for j in range(CT)] + [f"sv{j}" for j in range(CT)])
            ch = []
            for q in range(MERGE_TILES):
                ch += [f"g0{q}", f"p0{q}", f"g1{q}", f"g2{q}", f"p2{q}"]
            phase(f"merge{l}", names_merge(), KT // MERGE_TILES, lead=True, chunks=ch)
            phase(f"res1_{l}", names_outproj(), 2, lead=True, chunks=["o0", "o1", "o2", "o3"])
            phase(f"norm2_{l}", names_norm())
            phase(f"ffn{l}", names_ffn(), FT // 2, lead=True, chunks=["g0", "u0", "g1", "u1"])
            phase(f"res2_{l}", names_outproj(), 2, lead=True,
                  chunks=[f"o{q}" for q in range(4) for _ in range(3)])
        phase("final", dict(PE=["sum"], A=[f"sq{j}" for j in range(KT)] + ["rms"], V=["rstd"] + [f"xn{j}" for j in range(KT)] + [f"y{j}" for j in range(KT)], G=[]))

        order = [k for k, _ in at_end]
        for key, ph in phases.items():
            assert len(ph["chunks"]) % 4 == 0
        chunk_base, n = {}, 0
        for key in order:
            chunk_base[key] = n
            n += len(phases[key]["chunks"]) * phases[key]["turns"]
        assert n * P == w_stream.shape[0]
        w_v = w_stream.rearrange("(n p) c -> p n c", p=P)

        def enter(eng, key, own):
            k = order.index(key)
            if k:
                prev = phases[order[k - 1]]
                for e in ("PE", "A", "V", "G"):
                    if e in prev:
                        eng.wait_ge(*prev[e].end())
            if own in phases[key]:
                phases[key][own].credit(eng)
            return phases[key]

        def settle(eng):
            eng.sem_inc(s_settled, 1)

        def wait_steps(eng, turn, *steps):
            latest = {}
            for E, name in steps:
                if E not in latest or E.index[name] > E.index[latest[E]]:
                    latest[E] = name
            for E, name in latest.items():
                eng.wait_ge(*E.at(name, turn))

        def each(eng, ph, body):
            if ph["turns"] == 1:
                body(0)
            else:
                with eng.Fori(0, ph["turns"]) as i:
                    body(i)

        def slot(n, a=0, b=T):
            return arena[:, n * T + a:n * T + b]

        def slot_at(n0, turn, per, q, a=0, b=T):
            return arena[:, bass.ds((turn * per + (n0 + q)) * T + a, b - a)]

        def by_chunk(ap, c0=0):
            return ap.rearrange("p (c t) -> p c t", t=C)

        def const_b(col, n, nch=NCH):
            return const[:, None, col:col + n].to_broadcast([P, nch, n])

        def mask(name, d, nch=NCH):
            return const_b(C_MASK + (d * len(MASKS) + MASKS.index(name)) * C, C, nch)

        def par_c(name, k=0, n=1):
            return par[:, PAR[name] + k:PAR[name] + k + n]

        def ppc(name):
            return pp[:, PP[name]:PP[name] + 1]

        def eps_c(n):
            return const[:, C_EPS + n:C_EPS + n + 1]

        ident = const[:, C_ID:C_ID + P]
        ones = const[:, C_ONES:C_ONES + P]
        heads = const[:, C_HEADS:C_HEADS + P]

        def cols(l):
            return 0 if l < DEPTH - 1 else CTX

        def segs(c0):
            return ([(0, 0, CTX)] if c0 == 0 else []) + [(1, CTX, T)]

        def halves(c0, off):
            cut = 512 + off
            return [(a, b) for a, b in ((c0, min(cut, T)), (max(cut, c0), T)) if a < b]

        def project(eng, tile, lhs, rhs, c0, off):
            mm = None
            for a, b in halves(c0, off):
                for k in range(len(lhs)):
                    mm = eng.matmul(psum[0:lhs[k].shape[-1], tile, a - off:b - off], lhsT=lhs[k], rhs=rhs[k][:, a:b],
                                    start=(k == 0), stop=(k == len(lhs) - 1))
            return mm

        def chunk_blocks(n, k0=0, nk=8):
            s = n % 4
            return [ring[:, s * BW + k * P:s * BW + (k + 1) * P] for k in range(k0, k0 + nk)]

        def arrived(eng, key, turn, q):
            base = chunk_base[key] // 4
            per = len(phases[key]["chunks"]) // 4
            eng.wait_ge(w_in[q % 4], 16 * (turn * per + (base + q // 4 + 1)))

        hs = [slot(H0 + j) for j in range(KT)]
        sgu_w = arena[:, SGW * T:SGW * T + GROUPS * P]
        sgu_b = arena[:, SGB * T:SGB * T + CT * P]
        block = st.enter_context(nc.Block())

        @block.sync
        def _(sp):
            last = {}

            def load(key, turn, q, n):
                sp.dma_start(ring[:, (q % 4) * BW:(q % 4 + 1) * BW], w_v[:, n, :]).then_inc(w_in[q % 4], 16)

            for key in order:
                ph = phases[key]
                names, turns = ph["chunks"], ph["turns"]
                if not names:
                    continue
                nq = len(names)
                for q in range(nq):
                    if q % 4 in last:
                        sp.wait_ge(*last[q % 4])
                    load(key, 0, q, chunk_base[key] + q)
                    last[q % 4] = ph["PE"].at(names[q], 0)
                if turns > 1:
                    with sp.Fori(1, turns) as i:
                        for q in range(nq):
                            if q < 4:
                                sp.wait_ge(*ph["PE"].at(names[nq - 4 + q], i, back=1))
                            else:
                                sp.wait_ge(*ph["PE"].at(names[q - 4], i))
                            sp.dma_start(ring[:, None, (q % 4) * BW:(q % 4 + 1) * BW],
                                         w_v[:, bass.ds(i * nq + (chunk_base[key] + q), 1), :]
                                         ).then_inc(w_in[q % 4], 16)
                    for q in range(nq):
                        last[q % 4] = ph["PE"].at(names[q], turns - 1)

        @block.tensor
        def _(pe):
            def mod_phase(l):
                key = f"mod{l}"
                ph = enter(pe, key, "PE")
                S = ph["PE"]

                def turn(i):
                    for q in range(4):
                        arrived(pe, key, i, q)
                        blocks = chunk_blocks(q)
                        for k in range(KT):
                            mm = pe.matmul(psum[:, 0, bass.ds((i * 4 + q) * 2, 2)], lhsT=blocks[k],
                                           rhs=sc[:, 2 * k:2 * k + 2], start=(k == 0), stop=(k == KT - 1))
                        mm.then_inc(*S.mark(f"m{q}"))
                each(pe, ph, turn)

            def norm_phase(key, c0):
                ph = enter(pe, key, "PE")
                for j in range(KT):
                    pe.wait_ge(*ph["A"].at(f"sq{j}"))
                    for a, b in halves(c0, 0):
                        mm = pe.matmul(psum[:, 0, a:b], lhsT=ones, rhs=slot(H0 + j, a, b),
                                       start=(j == 0), stop=(j == KT - 1), skip_group_check=True)
                mm.then_inc(*ph["PE"].mark("sum"))

            def lora_phase(l):
                key = f"lora{l}"
                ph = enter(pe, key, "PE")
                for q, name in enumerate(["w", "a", "g"]):
                    arrived(pe, key, 0, q)
                    project(pe, q, chunk_blocks(q), hs, 0, 0).then_inc(*ph["PE"].mark(name))
                arrived(pe, key, 0, 3)
                pe.matmul(psum[:, 3, 0:2], lhsT=chunk_blocks(3)[0], rhs=hs[0][:, 0:2], start=True,
                          stop=True).then_inc(*ph["PE"].mark("pad"))

            def pair_phase(l):
                key = f"pair{l}"
                ph = enter(pe, key, "PE")
                S, A, V, G = ph["PE"], ph["A"], ph["V"], ph["G"]
                _, wide = names_pair()
                y0 = cols(l)
                freed = {"zr": (A, "raw_r"), "zk": (A, "raw_k"), "zv": (A, "raw_v"), "gu": (A, "gz"),
                         "kkn": (V, "kkm"), "vT": (A, "vT"), "Y": (A, "yc"), "mean": (V, "yc"),
                         "var": (A, "ysd"), "bonus": (V, "bv")}
                for d in DIRS:
                    freed.update({f"lw{d}": (A, f"sw{d}"), f"la{d}": (A, f"sa{d}"), f"kkT{d}": (A, f"kkT{d}"),
                                  f"bT{d}": (A, f"bT{d}"), f"kT{d}": (A, f"kT{d}"), f"A{d}": (V, f"X1a{d}"),
                                  f"B{d}": (V, f"B{d}"), f"RB{d}": (V, f"RB{d}"), f"RK{d}": (V, f"RK{d}"),
                                  f"BV{d}": (A, f"BV{d}"), f"U0{d}": (A, f"U0{d}"), f"G{d}": (A, f"G{d}"),
                                  f"MT{d}": (V, f"MT{d}"), f"N{d}": (A, f"N{d}"), f"Q{d}": (V, f"Q{d}"),
                                  f"chain{d}": (V, f"c{NCH - 2}{d}")})
                    for n in LEVELS:
                        freed.update({f"T{n}{d}": (V, f"T{n}{d}"), f"U{n}{d}": (V, f"XT{n}{d}")})

                def turn(i):
                    def take(name, *also):
                        k = wide.index(name)
                        steps = list(also)
                        if k >= 4:
                            steps.append(freed[wide[k - 4]])
                            if wide[k - 4] in ("A0", "A1"):
                                steps.append((A, wide[k - 4]))
                        else:
                            pe.wait_ge(*V.at("ya", i, back=1))
                        wait_steps(pe, i, *steps)
                        return k % 4

                    def units(tile, terms, c0=0):
                        mm = None
                        settle(pe)
                        for c in range(c0 // C, NCH):
                            for h in range(2):
                                p0, a = h * HD, c * C
                                for k, (lo, ro) in enumerate(terms):
                                    rhs = (const[p0:p0 + HD, C_ID64:C_ID64 + C] if ro is None else
                                           arena[p0:p0 + HD, ro * T + a:ro * T + a + C])
                                    mm = pe.matmul(psum[p0:p0 + HD, tile, a:a + C],
                                                   lhsT=arena[p0:p0 + HD, lo * T + a:lo * T + a + C], rhs=rhs,
                                                   start=(k == 0), stop=(k == len(terms) - 1), skip_group_check=True)
                        return mm

                    for q, name in enumerate(["zr", "zk", "zv"]):
                        tile = take(name)
                        arrived(pe, key, i, q)
                        project(pe, tile, chunk_blocks(q), hs, 0, 0).then_inc(*S.mark(name))
                    arrived(pe, key, i, 3)
                    up = 3 * BW
                    for d in DIRS:
                        for n, (name, src) in enumerate((("lw", LW), ("la", LA))):
                            tile = take(f"{name}{d}")
                            rows = slice(d * HD, d * HD + HD)
                            for a, b in halves(0, 0):
                                mm = pe.matmul(psum[:, tile, a:b], lhsT=ring[rows, up + n * P:up + n * P + P],
                                               rhs=arena[rows, src * T + a:src * T + b], start=True, stop=True)
                            mm.then_inc(*S.mark(f"{name}{d}"))
                    tile = take("gu")
                    pe.wait_ge(*G.at("pp", i))
                    project(pe, tile, [ring[:, up + 2 * P:up + 3 * P]], [slot(LG)], y0, 0).then_inc(*S.mark("gu"))

                    tile = take("kkn", (A, "kksq"))
                    project(pe, tile, [heads], [slot(T0)], 0, 0).then_inc(*S.mark("kkn"))
                    tile = take("vT", (V, "vc"))
                    units(tile, [(V_, None)]).then_inc(*S.mark("vT"))
                    for d in DIRS:
                        s = DIR0 + 14 * d
                        ready = [(V, f"bQ{d}"), (G, f"kE{d}")]
                        for name, src in (("kkT", S_KK), ("bT", S_BE), ("kT", S_KE)):
                            units(take(f"{name}{d}", *ready), [(s + src, None)]).then_inc(*S.mark(f"{name}{d}"))
                    for d in DIRS:
                        s = DIR0 + 14 * d
                        units(take(f"A{d}"), [(s + S_B, s + S_KK)]).then_inc(*S.mark(f"A{d}"))
                        units(take(f"B{d}"), [(s + S_K, s + S_KK)]).then_inc(*S.mark(f"B{d}"))
                        units(take(f"RB{d}"), [(s + S_B, s + S_R)], y0).then_inc(*S.mark(f"RB{d}"))
                        units(take(f"RK{d}"), [(s + S_K, s + S_R)], y0).then_inc(*S.mark(f"RK{d}"))
                    for d in DIRS:
                        s = DIR0 + 14 * d
                        tile = take(f"BV{d}", (V, f"B{d}"), (A, "vT"))
                        units(tile, [(s + S_BT, VT)]).then_inc(*S.mark(f"BV{d}"))
                    for n in LEVELS:
                        for d in DIRS:
                            s = DIR0 + 14 * d
                            tile = take(f"T{n}{d}", (V, f"X{d}" if n == 1 else f"Xt{n - 1}{d}"), (A, f"A{d}"))
                            units(tile, [(s + S_A, s + S_KE)]).then_inc(*S.mark(f"T{n}{d}"))
                        for d in DIRS:
                            s = DIR0 + 14 * d
                            tile = take(f"U{n}{d}", (V, f"T{n}{d}"))
                            units(tile, [(s + S_B, s + S_BE)]).then_inc(*S.mark(f"U{n}{d}"))
                    for d in DIRS:
                        s = DIR0 + 14 * d
                        tile = take(f"U0{d}", (V, f"XT5{d}"), (A, f"BV{d}"))
                        units(tile, [(s + S_BE, s + S_KK)]).then_inc(*S.mark(f"U0{d}"))
                        units(take(f"G{d}"), [(s + S_BE, s + S_KKT)]).then_inc(*S.mark(f"G{d}"))
                    for d in DIRS:
                        s = DIR0 + 14 * d
                        tile = take(f"MT{d}", (A, f"G{d}"))
                        units(tile, [(s + S_BT, s + S_BET)]).then_inc(*S.mark(f"MT{d}"))
                        units(take(f"N{d}"), [(s + S_BET, s + S_A), (s + S_KET, VT)]).then_inc(*S.mark(f"N{d}"))
                        tile = take(f"Q{d}", (V, f"RB{d}"))
                        units(tile, [(s + S_BT, s + S_RB)], y0).then_inc(*S.mark(f"Q{d}"))
                    tiles = [take("chain0", (V, "MT0"), (A, "N0")), take("chain1", (V, "MT1"), (A, "N1"))]
                    for n in CHAIN:
                        for d in DIRS:
                            s, c = DIR0 + 14 * d, seq(d)[n]
                            if n == 1:
                                src = (s + S_KKT) * T + seq(d)[0] * C
                            else:
                                pe.wait_ge(*V.at(f"c{n - 1}{d}", i))
                                src = (s + S_S) * T + c * C
                            settle(pe)
                            for h in range(2):
                                p0 = h * HD
                                mm = pe.matmul(psum[p0:p0 + HD, tiles[d], c * C:c * C + C],
                                               lhsT=arena[p0:p0 + HD, (s + S_K) * T + c * C:(s + S_K) * T + c * C + C],
                                               rhs=arena[p0:p0 + HD, src:src + C],
                                               start=True, stop=True, skip_group_check=True)
                            mm.then_inc(*S.mark(f"c{n}{d}"))
                    tile = take("Y", (V, f"c{NCH - 2}1"))
                    settle(pe)
                    for c in range(y0 // C, NCH):
                        for h in range(2):
                            terms = []
                            for d in DIRS:
                                s, n = DIR0 + 14 * d, seq(d).index(c)
                                col = c * C
                                terms += [((s + S_A) * T + col, (s + S_RB) * T + col), (VT * T + col, (s + S_RK) * T + col)]
                                if n == 1:
                                    terms.append(((s + S_KKT) * T + seq(d)[0] * C, (s + S_R) * T + col))
                                elif n > 1:
                                    terms.append(((s + S_S) * T + col, (s + S_R) * T + col))
                            p0 = h * HD
                            for k, (lo, ro) in enumerate(terms):
                                mm = pe.matmul(psum[p0:p0 + HD, tile, c * C:c * C + C], lhsT=arena[p0:p0 + HD, lo:lo + C],
                                               rhs=arena[p0:p0 + HD, ro:ro + C], start=(k == 0),
                                               stop=(k == len(terms) - 1), skip_group_check=True)
                    mm.then_inc(*S.mark("Y"))
                    tile = take("mean", (A, "yc"))
                    project(pe, tile, [heads], [slot(T0)], y0, 0).then_inc(*S.mark("mean"))
                    tile = take("var", (A, "ysq"))
                    project(pe, tile, [heads], [slot(T1)], y0, 0).then_inc(*S.mark("var"))
                    tile = take("bonus", (V, "bon"))
                    project(pe, tile, [heads], [slot(T2)], y0, 0).then_inc(*S.mark("bonus"))
                each(pe, ph, turn)

            def branch_phase(l):
                key = f"branch{l}"
                ph = enter(pe, key, "PE")
                S, A, V = ph["PE"], ph["A"], ph["V"]
                c0 = cols(l)
                seq_ = []
                for j in range(CT):
                    seq_ += [(f"cb{j}", A, f"cb{j}"), (f"ca{j}", V, f"u{j}")]
                seq_ += [(f"su{j}", A, f"su{j}") for j in range(CT)] + [(f"sv{j}", A, f"sv{j}") for j in range(CT)]
                for n, (name, _, _) in enumerate(seq_):
                    if n >= 4:
                        _, E, step = seq_[n - 4]
                        pe.wait_ge(*E.at(step))
                    arrived(pe, key, 0, n)
                    project(pe, n % 4, chunk_blocks(n), hs, c0, c0).then_inc(*S.mark(name))
                pe.wait_ge(*A.at(f"sv{CT - 1}"))
                for name, tile, src, E, step in (("cmean", 0, CY, V, None), ("cvar", 1, CU, A, "csq"),
                                                 ("smean", 2, SV, A, None), ("svar", 3, H1, A, "ssq")):
                    if name == "cmean":
                        pe.wait_ge(*V.at(f"y{CT - 1}_{len(conv_taps(l)) - 1}"))
                    if step:
                        pe.wait_ge(*A.at(f"{step}{CT - 1}"))
                    project(pe, tile, [ones] * CT, [slot(src + j) for j in range(CT)], c0, c0).then_inc(*S.mark(name))
                for j in range(CT):
                    pe.wait_ge(*A.at(f"sn{j}"))
                    if j == 0:
                        pe.wait_ge(*V.at("cr"))
                        pe.wait_ge(*V.at("sr"))
                    for n in range((T - c0) // P):
                        a = c0 + n * P
                        mm = pe.matmul(psum[:, j, n * P:n * P + P], lhsT=slot(SV + j, a, a + P), rhs=ident,
                                       start=True, stop=True, skip_group_check=True)
                    mm.then_inc(*S.mark(f"tr{j}"))
                for j in range(CT):
                    pe.wait_ge(*A.at(f"tr{j}"))
                    if j == 0:
                        pe.wait_ge(s_sgu, 32 * (l + 1))
                    for n in range((T - c0) // P):
                        for g in range(2):
                            mm = pe.matmul(psum[g * HD:g * HD + HD, j, n * P:n * P + P],
                                           lhsT=arena[:, (VTK + j) * T + n * P + g * HD:(VTK + j) * T + n * P + g * HD + HD],
                                           rhs=sgu_w[:, (2 * j + g) * P:(2 * j + g + 1) * P],
                                           start=True, stop=True, skip_group_check=True)
                    mm.then_inc(*S.mark(f"sp{j}"))

            def merge_phase(l):
                key = f"merge{l}"
                ph = enter(pe, key, "PE")
                S, A, V = ph["PE"], ph["A"], ph["V"]
                c0 = cols(l)
                ya = [slot(YA0 + j) for j in range(KT)]
                cv = [slot(CY + j) for j in range(CT)]
                sg = [slot(SU + j) for j in range(CT)]

                def turn(i):
                    flow = []
                    for q in range(MERGE_TILES):
                        flow += [(f"g0{q}", 5 * q, 0, 8, hs, A), (f"p0{q}", 5 * q + 1, 0, 8, ya, V),
                                 (f"g1{q}", 5 * q + 2, 0, 8, hs, A), (f"p1{q}", 5 * q + 4, 0, 4, cv, V),
                                 (f"g2{q}", 5 * q + 3, 0, 8, hs, A), (f"p2{q}", 5 * q + 4, 4, 4, sg, V)]
                    for n, (name, chunk, k0, nk, mov, _) in enumerate(flow):
                        if n >= 4:
                            pe.wait_ge(*flow[n - 4][5].at(flow[n - 4][0], i))
                        else:
                            pe.wait_ge(*flow[n - 4][5].at(flow[n - 4][0], i, back=1))
                        arrived(pe, key, i, chunk)
                        project(pe, n % 4, chunk_blocks(chunk, k0, nk), mov, c0, c0).then_inc(*S.mark(name))
                each(pe, ph, turn)

            def outproj_phase(key, c0, mov, per):
                ph = enter(pe, key, "PE")
                S, V = ph["PE"], ph["V"]

                def turn(i):
                    for q in range(4):
                        pe.wait_ge(*V.at(f"x{q}", i, back=1))
                        lhs = []
                        for n in range(per):
                            arrived(pe, key, i, per * q + n)
                            lhs += chunk_blocks(per * q + n)
                        project(pe, q, lhs[:len(mov)], mov, c0, c0).then_inc(*S.mark(f"o{q}"))
                each(pe, ph, turn)

            def ffn_phase(l):
                key = f"ffn{l}"
                ph = enter(pe, key, "PE")
                S, A, V = ph["PE"], ph["A"], ph["V"]
                c0 = cols(l)

                def turn(i):
                    for q, (name, E, step) in enumerate((("g0", A, "s0"), ("u0", V, "a0"), ("g1", A, "s1"), ("u1", V, "a1"))):
                        pe.wait_ge(*E.at(step, i, back=1))
                        arrived(pe, key, i, q)
                        project(pe, q, chunk_blocks(q), hs, c0, c0).then_inc(*S.mark(name))
                each(pe, ph, turn)

            pe.wait_ge(*phases["cond"]["A"].at("silu"))
            for l in range(DEPTH):
                mod_phase(l)
                norm_phase(f"norm1_{l}", 0)
                lora_phase(l)
                pair_phase(l)
                branch_phase(l)
                merge_phase(l)
                outproj_phase(f"res1_{l}", cols(l), [slot(M0 + j) for j in range(KT)], 1)
                norm_phase(f"norm2_{l}", cols(l))
                ffn_phase(l)
                outproj_phase(f"res2_{l}", cols(l), [slot(ACT0 + j) for j in range(FT)], 3)
            norm_phase("final", CTX)

        @block.scalar
        def _(act):
            act.dma_start(const[:, :], const_in).then_inc(s_load, 16)
            act.dma_start(cvec[:, :], c_in).then_inc(s_load, 16)
            act.dma_start(slot(SCANMASK), scanmask_in).then_inc(s_load, 16)
            act.dma_start(arena[:, X0 * T:(X0 + KT) * T], x_in).then_inc(s_load, 16)
            act.dma_start(par[:, :], par_in[0, :, :]).then_inc(s_par, 16)
            act.wait_ge(s_load, 64)
            act.activation(sc[:, :], cvec[:, :], ACT.Silu).then_inc(*phases["cond"]["A"].mark("silu"))

            def norm_phase(key, c0, which, affine=True):
                ph = enter(act, key, "A")
                A, V = ph["A"], ph["V"]
                for j in range(KT):
                    act.activation(slot(H0 + j, c0), slot(X0 + j, c0), ACT.Square).then_inc(*A.mark(f"sq{j}"))
                act.wait_ge(*ph["PE"].at("sum"))
                act.activation(slot(T0, c0), psum[:, 0, c0:T], ACT.Sqrt, bias=eps_c(0), scale=1.0 / D).then_inc(*A.mark("rms"))
                if not affine:
                    return
                for j in range(KT):
                    act.wait_ge(*V.at(f"xn{j}"))
                    for s, a, b in segs(c0):
                        shift = mod[:, 2 * (24 * which + j) + s:2 * (24 * which + j) + s + 1]
                        gain = a_mod[:, 2 * (KT * which + j) + s:2 * (KT * which + j) + s + 1]
                        ins = act.activation(slot(H0 + j, a, b), slot(H0 + j, a, b), ACT.Identity, bias=shift, scale=gain)
                    ins.then_inc(*A.mark(f"h{j}"))

            def lora_phase(l):
                ph = enter(act, f"lora{l}", "A")
                A, V, PE = ph["A"], ph["V"], ph["PE"]
                act.dma_start(spill, arena[:, X0 * T:(X0 + KT) * T]).then_inc(s_spill, 16)
                for n, name in enumerate(["w", "a", "g"]):
                    act.wait_ge(*PE.at(name))
                    act.activation(slot(T0 + n), psum[:, n, 0:T], ACT.Copy).then_inc(*A.mark(f"raw{n}"))
                act.wait_ge(*V.at("s0c"))
                act.activation(slot(LW), slot(LW), ACT.Tanh).then_inc(*A.mark("act0"))
                act.wait_ge(*V.at("s2c"))
                act.wait_ge(s_spill, 16 * (l + 1))
                act.activation(slot(LG), slot(LG), ACT.Sigmoid).then_inc(*A.mark("act2"))

            def pair_phase(l):
                ph = enter(act, f"pair{l}", "A")
                A, V, PE, G = ph["A"], ph["V"], ph["PE"], ph["G"]
                _, wide = names_pair()
                y0 = cols(l)

                def turn(i):
                    def ps(name, a=0, b=T):
                        return psum[:, wide.index(name) % 4, a:b]

                    def evac(name, dst, a=0, scale=1.0):
                        act.wait_ge(*PE.at(name, i))
                        act.activation(slot(dst, a), ps(name, a), ACT.Copy, scale=scale).then_inc(*A.mark(name))

                    for n, x in enumerate("rkv"):
                        act.wait_ge(*PE.at(f"z{x}", i))
                        if n == 0:
                            act.wait_ge(*V.at("ya", i, back=1))
                        act.activation(slot(T0 + n), ps(f"z{x}"), ACT.Copy).then_inc(*A.mark(f"raw_{x}"))
                    act.wait_ge(*G.at("pp", i))
                    for d in DIRS:
                        s = DIR0 + 14 * d
                        act.wait_ge(*PE.at(f"lw{d}", i))
                        act.activation(slot(s + 8), ps(f"lw{d}"), ACT.Sigmoid, bias=ppc(f"w0{d}")).then_inc(*A.mark(f"sw{d}"))
                        act.wait_ge(*PE.at(f"la{d}", i))
                        act.activation(slot(s + 9), ps(f"la{d}"), ACT.Sigmoid, bias=ppc(f"a0{d}")).then_inc(*A.mark(f"sa{d}"))
                    act.wait_ge(*PE.at("gu", i))
                    act.activation(slot(GZ, y0), ps("gu", y0), ACT.Copy).then_inc(*A.mark("gz"))
                    act.wait_ge(*V.at("kk0", i))
                    act.activation(slot(T0), slot(KK_), ACT.Square).then_inc(*A.mark("kksq"))
                    act.wait_ge(*V.at("kkm", i))
                    act.activation(slot(T1), slot(T1), ACT.Sqrt).then_inc(*A.mark("kks"))
                    for d in DIRS:
                        s = DIR0 + 14 * d
                        act.wait_ge(*V.at(f"L{d}", i))
                        act.wait_ge(*G.at("Le0" if d == 0 else "Li1", i))
                        act.activation(slot(s + 13), slot(s + 10), ACT.Exp, scale=-KAPPA).then_inc(*A.mark(f"Ei{d}"))
                        act.activation(slot(s + 12), slot(s + 10), ACT.Exp, scale=KAPPA).then_inc(*A.mark(f"En{d}"))
                        act.activation(slot(s + 11), slot(s + 11), ACT.Exp, scale=-KAPPA).then_inc(*A.mark(f"Ee{d}"))
                    evac("vT", VT)
                    for d in DIRS:
                        s = DIR0 + 14 * d
                        evac(f"kkT{d}", s + S_KKT)
                        evac(f"bT{d}", s + S_BET)
                        evac(f"kT{d}", s + S_KET)
                    for d in DIRS:
                        act.wait_ge(*V.at(f"X1a{d}", i))
                        evac(f"A{d}", DIR0 + 14 * d + S_A)
                    for d in DIRS:
                        evac(f"BV{d}", DIR0 + 14 * d + S_KK)
                    for d in DIRS:
                        evac(f"U0{d}", DIR0 + 14 * d + S_A, scale=-1.0)
                        evac(f"G{d}", DIR0 + 14 * d + S_BT, scale=-1.0)
                    for d in DIRS:
                        evac(f"N{d}", DIR0 + 14 * d + S_KKT)
                    act.wait_ge(*PE.at("Y", i))
                    act.activation(slot(T0, y0), ps("Y", y0), ACT.Copy).then_inc(*A.mark("yc"))
                    act.wait_ge(*V.at("yc", i))
                    act.activation(slot(T1, y0), slot(T0, y0), ACT.Square).then_inc(*A.mark("ysq"))
                    act.wait_ge(*PE.at("var", i))
                    act.activation(slot(T1, y0), ps("var", y0), ACT.Sqrt, bias=eps_c(2), scale=1.0 / HD).then_inc(*A.mark("ysd"))
                    act.wait_ge(*V.at("ynr", i))
                    act.activation(slot(T0, y0), slot(T0, y0), ACT.Identity, bias=ppc("gnb"), scale=ppc("gng")).then_inc(*A.mark("yn"))
                each(act, ph, turn)

            def branch_phase(l):
                ph = enter(act, f"branch{l}", "A")
                A, V, PE = ph["A"], ph["V"], ph["PE"]
                c0 = cols(l)
                n = T - c0
                act.dma_start(arena[:, X0 * T:(X0 + KT) * T], spill).then_inc(s_back, 16)
                act.dma_start(sgu_w, sgu_w_in[l, :, :]).then_inc(s_sgu, 16)
                act.dma_start(sgu_b, sgu_b_in[l, :, :]).then_inc(s_sgu, 16)
                for j in range(CT):
                    act.wait_ge(*PE.at(f"cb{j}"))
                    if j >= 2:
                        act.wait_ge(*V.at(f"u{j - 2}"))
                    act.activation(slot(G0 + j % 2, c0), psum[:, (2 * j) % 4, 0:n], ACT.Sigmoid).then_inc(*A.mark(f"cb{j}"))
                for name, dst in (("su", SU), ("sv", SV)):
                    for j in range(CT):
                        act.wait_ge(*PE.at(f"{name}{j}"))
                        act.activation(slot(dst + j, c0), psum[:, j, 0:n], ACT.Gelu_apprx_tanh).then_inc(*A.mark(f"{name}{j}"))
                for j in range(CT):
                    act.wait_ge(*V.at(f"cc{j}"))
                    act.activation(slot(CU + j, c0), slot(CY + j, c0), ACT.Square).then_inc(*A.mark(f"csq{j}"))
                for j in range(CT):
                    act.wait_ge(*V.at(f"sc{j}"))
                    act.activation(slot(H1 + j, c0), slot(SV + j, c0), ACT.Square).then_inc(*A.mark(f"ssq{j}"))
                for name, var, tile, dst in (("csd", "cvar", 1, G0), ("ssd", "svar", 3, G0 + 1)):
                    act.wait_ge(*PE.at(var))
                    act.activation(slot(dst, c0), psum[:, tile, 0:n], ACT.Sqrt, bias=eps_c(1), scale=1.0 / CONV).then_inc(*A.mark(name))
                for j in range(CT):
                    act.wait_ge(*V.at(f"cn{j}"))
                    act.activation(slot(CY + j, c0), slot(CY + j, c0), ACT.Silu, bias=par_c("clb", j), scale=par_c("clg", j)).then_inc(*A.mark(f"cs{j}"))
                for j in range(CT):
                    act.wait_ge(*V.at(f"sm{j}"))
                    act.activation(slot(SV + j, c0), slot(SV + j, c0), ACT.Identity, bias=par_c("slb", j), scale=par_c("slg", j)).then_inc(*A.mark(f"sn{j}"))
                for j in range(CT):
                    act.wait_ge(*PE.at(f"tr{j}"))
                    act.activation(slot(VTK + j, 0, n), psum[:, j, 0:n], ACT.Copy).then_inc(*A.mark(f"tr{j}"))

            def merge_phase(l):
                ph = enter(act, f"merge{l}", "A")
                A, V, PE = ph["A"], ph["V"], ph["PE"]
                c0 = cols(l)
                n = T - c0
                order_g = [(b, q) for q in range(MERGE_TILES) for b in range(3)]

                def turn(i):
                    for k, (b, q) in enumerate(order_g):
                        act.wait_ge(*PE.at(f"g{b}{q}", i))
                        if k >= 3:
                            act.wait_ge(*V.at("p%d%d" % order_g[k - 3], i))
                        else:
                            act.wait_ge(*V.at("p%d%d" % order_g[k - 3], i, back=1))
                        act.activation(slot(G0 + k % 3, c0), psum[:, (2 * k) % 4, 0:n], ACT.Sigmoid).then_inc(*A.mark(f"g{b}{q}"))
                each(act, ph, turn)

            def ffn_phase(l):
                ph = enter(act, f"ffn{l}", "A")
                A, V, PE = ph["A"], ph["V"], ph["PE"]
                c0 = cols(l)
                n = T - c0

                def turn(i):
                    for q in range(2):
                        act.wait_ge(*PE.at(f"g{q}", i))
                        act.wait_ge(*V.at(f"a{q}", i, back=1))
                        act.activation(slot(YA0 + q, c0), psum[:, 2 * q, 0:n], ACT.Silu).then_inc(*A.mark(f"s{q}"))
                each(act, ph, turn)

            for l in range(DEPTH):
                if l:
                    act.wait_ge(*phases[f"res2_{l - 1}"]["V"].end())
                    act.wait_ge(*phases[f"res2_{l - 1}"]["PE"].end())
                    act.dma_start(par[:, :], par_in[l, :, :]).then_inc(s_par, 16)
                norm_phase(f"norm1_{l}", 0, 0)
                lora_phase(l)
                pair_phase(l)
                branch_phase(l)
                merge_phase(l)
                norm_phase(f"norm2_{l}", cols(l), 1)
                ffn_phase(l)
            norm_phase("final", CTX, 0, affine=False)
            act.wait_ge(*phases["final"]["V"].end())
            act.dma_start(out, arena[:, H0 * T:(H0 + KT) * T].rearrange("p (j t) -> p j t", t=T)[:, :, CTX:T]).then_inc(s_out, 16)
            act.wait_ge(s_out, 16)

        @block.vector
        def _(dve):
            def modv_phase(l):
                ph = enter(dve, f"modv{l}", "V")
                V = ph["V"]
                dve.wait_ge(s_par, 16 * (l + 1))
                dve.tensor_tensor(mod[:, :].rearrange("p (j s) -> p j s", s=2),
                                  psum[:, 0, 0:96].rearrange("p (j s) -> p j s", s=2),
                                  par[:, PAR["b_mod"]:PAR["b_mod"] + 48, None].to_broadcast([P, 48, 2]),
                                  ALU.add).then_inc(*V.mark("mod"))
                dve.wait_ge(*V.at("mod"))
                for which, g, name in ((0, "n1g", "a1"), (1, "n2g", "a2")):
                    o = 2 * (24 * which + KT)
                    dve.scalar_tensor_tensor(
                        out=a_mod[:, 2 * KT * which:2 * KT * (which + 1)].rearrange("p (j s) -> p j s", s=2),
                        in0=mod[:, o:o + 2 * KT].rearrange("p (j s) -> p j s", s=2), scalar=1.0,
                        in1=par[:, PAR[g]:PAR[g] + KT, None].to_broadcast([P, KT, 2]),
                        op0=ALU.add, op1=ALU.mult).then_inc(*V.mark(name))

            def norm_phase(key, c0, final=False):
                ph = enter(dve, key, "V")
                V, A = ph["V"], ph["A"]
                dve.wait_ge(*A.at("rms"))
                dve.reciprocal(slot(T0, c0), slot(T0, c0)).then_inc(*V.mark("rstd"))
                dve.wait_ge(*V.at("rstd"))
                for j in range(KT):
                    dve.tensor_tensor(slot(H0 + j, c0), slot(X0 + j, c0), slot(T0, c0), ALU.mult).then_inc(*V.mark(f"xn{j}"))
                if final:
                    for j in range(KT):
                        dve.wait_ge(*V.at(f"xn{j}"))
                        dve.tensor_scalar(slot(H0 + j, c0), slot(H0 + j, c0), par_c("fin", j), None, ALU.mult).then_inc(*V.mark(f"y{j}"))

            def shift(V, i, raw, dst, w0, w1, w2, n0, n1, n2):
                dve.tensor_scalar(slot(dst), slot(raw), w1, None, ALU.mult).then_inc(*V.mark(n0))
                dve.wait_ge(*V.at(n0, i))
                for a, b in ((0, CTX), (CTX, T)):
                    ins = dve.scalar_tensor_tensor(out=slot(dst, a + 1, b), in0=slot(raw, a, b - 1), scalar=w0,
                                                   in1=slot(dst, a + 1, b), op0=ALU.mult, op1=ALU.add)
                ins.then_inc(*V.mark(n1))
                dve.wait_ge(*V.at(n1, i))
                for a, b in ((0, CTX), (CTX, T)):
                    ins = dve.scalar_tensor_tensor(out=slot(dst, a, b - 1), in0=slot(raw, a + 1, b), scalar=w2,
                                                   in1=slot(dst, a, b - 1), op0=ALU.mult, op1=ALU.add)
                ins.then_inc(*V.mark(n2))

            def lora_phase(l):
                ph = enter(dve, f"lora{l}", "V")
                A, V = ph["A"], ph["V"]
                for n in range(3):
                    dve.wait_ge(*A.at(f"raw{n}"))
                    shift(V, 0, T0 + n, LW + n, *[par_c("shift", 3 * n + t) for t in range(3)],
                          *[f"s{n}{x}" for x in "abc"])

            def pair_phase(l):
                ph = enter(dve, f"pair{l}", "V")
                A, V, PE, G = ph["A"], ph["V"], ph["PE"], ph["G"]
                _, wide = names_pair()
                y0 = cols(l)
                ny = (T - y0) // C

                def turn(i):
                    def ps(name, a=0, b=T):
                        return psum[:, wide.index(name) % 4, a:b]

                    def mul(name, out_, a, b):
                        dve.tensor_tensor(slot(out_), slot(a), slot(b), ALU.mult).then_inc(*V.mark(name))

                    for n, x in enumerate("rkv"):
                        dve.wait_ge(*A.at(f"raw_{x}", i))
                        if n == 0:
                            dve.wait_ge(*G.at("pp", i))
                        shift(V, i, T0 + n, R_ + n, ppc(f"{x}0"), ppc(f"{x}1"), ppc(f"{x}2"), f"{x}a", f"{x}b", f"{x}c")
                        if x == "k":
                            dve.wait_ge(*V.at("kc", i))
                            dve.tensor_scalar(slot(KK_), slot(K_), ppc("kk"), None, ALU.mult).then_inc(*V.mark("kk0"))

                    def scan(d):
                        s = DIR0 + 14 * d
                        dve.wait_ge(*A.at(f"sw{d}", i))
                        dve.tensor_tensor_scan(slot(s + 10), slot(SCANMASK), slot(s + 8), 0.0, ALU.mult, ALU.add).then_inc(*V.mark(f"L{d}"))

                    scan(0)
                    dve.wait_ge(*PE.at("kkn", i))
                    dve.tensor_scalar(slot(T1), ps("kkn"), 1e-24, None, ALU.max).then_inc(*V.mark("kkm"))
                    dve.wait_ge(*A.at("kks", i))
                    dve.reciprocal(slot(T1), slot(T1)).then_inc(*V.mark("kkr"))
                    dve.wait_ge(*V.at("kkr", i))
                    mul("kk", KK_, KK_, T1)
                    scan(1)
                    dve.wait_ge(*V.at("kk", i))
                    for d in DIRS:
                        s = DIR0 + 14 * d
                        dve.wait_ge(*A.at(f"Ei{d}", i))
                        mul(f"rP{d}", s + S_R, R_, s + 13)
                        dve.wait_ge(*A.at(f"Ee{d}", i))
                        mul(f"kkP{d}", s + S_KK, KK_, s + 11)
                        dve.wait_ge(*A.at(f"sa{d}", i))
                        mul(f"b{d}", s + S_B, KK_, s + 9)
                        dve.wait_ge(*V.at(f"b{d}", i))
                        mul(f"bQ{d}", s + S_B, s + S_B, s + 12)

                    def masked(name, dst, m, d, a=0):
                        dve.wait_ge(*PE.at(name, i))
                        dve.tensor_tensor(by_chunk(slot(dst, a)), by_chunk(ps(name, a)), mask(m, d, (T - a) // C), ALU.mult)

                    for d in DIRS:
                        s = DIR0 + 14 * d
                        dve.wait_ge(*PE.at(f"A{d}", i))
                        dve.tensor_tensor(by_chunk(slot(s + S_BE)), by_chunk(ps(f"A{d}")), mask("first", d), ALU.mult).then_inc(*V.mark(f"X1a{d}"))
                        dve.wait_ge(*V.at(f"X1a{d}", i))
                        dve.tensor_tensor(by_chunk(slot(s + S_BE)), by_chunk(slot(s + S_BE)), const_b(C_ID64, C), ALU.add).then_inc(*V.mark(f"X1b{d}"))
                        dve.wait_ge(*V.at(f"X1b{d}", i))
                        dve.transpose(slot(s + S_KE), slot(s + S_BE)).then_inc(*V.mark(f"X{d}"))
                        dve.wait_ge(*PE.at(f"B{d}", i))
                        dve.tensor_tensor(by_chunk(slot(s + S_BT)), by_chunk(ps(f"B{d}")), mask("strict", d), ALU.mult).then_inc(*V.mark(f"B{d}"))
                        dve.wait_ge(*PE.at(f"RB{d}", i))
                        dve.tensor_tensor(by_chunk(slot(s + S_RB, y0)), by_chunk(ps(f"RB{d}", y0)), mask("incl", d, ny), ALU.mult).then_inc(*V.mark(f"RB{d}"))
                        dve.wait_ge(*PE.at(f"RK{d}", i))
                        dve.tensor_tensor(by_chunk(slot(s + S_RK, y0)), by_chunk(ps(f"RK{d}", y0)), mask("incl", d, ny), ALU.mult).then_inc(*V.mark(f"RK{d}"))
                    for n in LEVELS:
                        for d in DIRS:
                            s = DIR0 + 14 * d
                            dve.wait_ge(*PE.at(f"T{n}{d}", i))
                            dve.tensor_tensor(by_chunk(slot(s + S_B)), by_chunk(ps(f"T{n}{d}")), mask(f"lv{n}", d), ALU.mult).then_inc(*V.mark(f"T{n}{d}"))
                        for d in DIRS:
                            s = DIR0 + 14 * d
                            dve.wait_ge(*PE.at(f"U{n}{d}", i))
                            dve.tensor_tensor(slot(s + S_BE), slot(s + S_BE), ps(f"U{n}{d}"), ALU.subtract).then_inc(*V.mark(f"XT{n}{d}"))
                            if n < 5:
                                dve.wait_ge(*V.at(f"XT{n}{d}", i))
                                dve.transpose(slot(s + S_KE), slot(s + S_BE)).then_inc(*V.mark(f"Xt{n}{d}"))
                    for d in DIRS:
                        s = DIR0 + 14 * d
                        dve.wait_ge(*PE.at(f"MT{d}", i))
                        dve.wait_ge(*G.at(f"D{d}", i))
                        dve.tensor_tensor(slot(s + S_K), slot(s + S_K), ps(f"MT{d}"), ALU.add).then_inc(*V.mark(f"MT{d}"))
                        dve.wait_ge(*PE.at(f"Q{d}", i))
                        dve.tensor_tensor(slot(s + S_R, y0), slot(s + S_R, y0), ps(f"Q{d}", y0), ALU.add).then_inc(*V.mark(f"Q{d}"))
                    for n in CHAIN:
                        for d in DIRS:
                            s, c, nxt = DIR0 + 14 * d, seq(d)[n], seq(d)[n + 1]
                            dve.wait_ge(*PE.at(f"c{n}{d}", i))
                            if n == 1:
                                dve.wait_ge(*A.at(f"N{d}", i))
                            dve.tensor_tensor(slot(s + S_S, nxt * C, nxt * C + C), slot(s + S_KKT, c * C, c * C + C),
                                              psum[:, wide.index(f"chain{d}") % 4, c * C:c * C + C], ALU.add).then_inc(*V.mark(f"c{n}{d}"))
                    dve.wait_ge(*PE.at("mean", i))
                    dve.scalar_tensor_tensor(out=slot(T0, y0), in0=ps("mean", y0), scalar=-1.0 / HD, in1=slot(T0, y0),
                                             op0=ALU.mult, op1=ALU.add).then_inc(*V.mark("yc"))
                    dve.wait_ge(*A.at("ysd", i))
                    dve.reciprocal(slot(T1, y0), slot(T1, y0)).then_inc(*V.mark("rs"))
                    dve.wait_ge(*V.at("rs", i))
                    dve.tensor_tensor(slot(T0, y0), slot(T0, y0), slot(T1, y0), ALU.mult).then_inc(*V.mark("ynr"))
                    dve.scalar_tensor_tensor(out=slot(T2, y0), in0=slot(R_, y0), scalar=ppc("rk"), in1=slot(K_, y0),
                                             op0=ALU.mult, op1=ALU.mult).then_inc(*V.mark("bon"))
                    dve.wait_ge(*PE.at("bonus", i))
                    dve.tensor_tensor(slot(T2, y0), slot(V_, y0), ps("bonus", y0), ALU.mult).then_inc(*V.mark("bv"))
                    dve.wait_ge(*V.at("bv", i))
                    dve.wait_ge(*A.at("yn", i))
                    dve.tensor_tensor(slot(T0, y0), slot(T0, y0), slot(T2, y0), ALU.add).then_inc(*V.mark("yb"))
                    dve.wait_ge(*V.at("yb", i))
                    dve.wait_ge(*A.at("gz", i))
                    dve.tensor_tensor(slot_at(YA0, i, 1, 0, y0), slot(T0, y0), slot(GZ, y0), ALU.mult).then_inc(*V.mark("ya"))
                each(dve, ph, turn)

            def branch_phase(l):
                ph = enter(dve, f"branch{l}", "V")
                A, V, PE = ph["A"], ph["V"], ph["PE"]
                c0 = cols(l)
                n = T - c0
                taps = conv_taps(l)

                def grid(k, t, horizontal=True):
                    return slot(k, CTX).rearrange("p (r w) -> p r w", w=GRID_W)

                def tap(j, o, m):
                    w = par_c("dw", j * TAPS + 15 + o)
                    lo, hi = max(0, -o), max(0, o)
                    ins = None
                    if c0 == 0:
                        ins = dve.scalar_tensor_tensor(out=slot(CY + j, lo, CTX - hi), in0=slot(CU + j, lo + o, CTX - hi + o),
                                                       scalar=w, in1=slot(CY + j, lo, CTX - hi), op0=ALU.mult, op1=ALU.add)
                    if l % 2 == 0:
                        y, u = grid(CY + j, 0), grid(CU + j, 0)
                        ins = dve.scalar_tensor_tensor(out=y[:, :, lo:GRID_W - hi], in0=u[:, :, lo + o:GRID_W - hi + o],
                                                       scalar=w, in1=y[:, :, lo:GRID_W - hi], op0=ALU.mult, op1=ALU.add)
                    else:
                        a, b, s = CTX + lo * GRID_W, T - hi * GRID_W, o * GRID_W
                        ins = dve.scalar_tensor_tensor(out=slot(CY + j, a, b), in0=slot(CU + j, a + s, b + s),
                                                       scalar=w, in1=slot(CY + j, a, b), op0=ALU.mult, op1=ALU.add)
                    return ins

                for j in range(CT):
                    dve.wait_ge(*A.at(f"cb{j}"))
                    dve.wait_ge(*PE.at(f"ca{j}"))
                    dve.tensor_tensor(slot(CU + j, c0), psum[:, (2 * j + 1) % 4, 0:n], slot(G0 + j % 2, c0), ALU.mult).then_inc(*V.mark(f"u{j}"))
                    dve.wait_ge(*V.at(f"u{j}"))
                    for m, o in enumerate(taps):
                        if m == 0:
                            dve.tensor_scalar(slot(CY + j, c0), slot(CU + j, c0), par_c("dw", j * TAPS + 15), par_c("dwb", j),
                                              ALU.mult, ALU.add).then_inc(*V.mark(f"y{j}_0"))
                        else:
                            dve.wait_ge(*V.at(f"y{j}_{m - 1}"))
                            tap(j, o, m).then_inc(*V.mark(f"y{j}_{m}"))
                for pre, mean, dst, tile in (("cc", "cmean", CY, 0), ("sc", "smean", SV, 2)):
                    dve.wait_ge(*PE.at(mean))
                    for j in range(CT):
                        dve.scalar_tensor_tensor(out=slot(dst + j, c0), in0=psum[:, tile, 0:n], scalar=-1.0 / CONV,
                                                 in1=slot(dst + j, c0), op0=ALU.mult, op1=ALU.add).then_inc(*V.mark(f"{pre}{j}"))
                for pre, r, dst, tmp in (("c", "cn", CY, G0), ("s", "sm", SV, G0 + 1)):
                    dve.wait_ge(*A.at(f"{pre}sd"))
                    dve.reciprocal(slot(tmp, c0), slot(tmp, c0)).then_inc(*V.mark(f"{pre}r"))
                    dve.wait_ge(*V.at(f"{pre}r"))
                    for j in range(CT):
                        dve.tensor_tensor(slot(dst + j, c0), slot(dst + j, c0), slot(tmp, c0), ALU.mult).then_inc(*V.mark(f"{r}{j}"))
                for j in range(CT):
                    dve.wait_ge(*PE.at(f"sp{j}"))
                    if j == 0:
                        dve.wait_ge(s_sgu, 32 * (l + 1))
                    dve.tensor_tensor(slot(H1 + j, 0, n).rearrange("p (c t) -> p c t", t=P),
                                      psum[:, j, 0:n].rearrange("p (c t) -> p c t", t=P),
                                      sgu_b[:, None, j * P:(j + 1) * P].to_broadcast([P, n // P, P]), ALU.add).then_inc(*V.mark(f"sp{j}"))
                    dve.wait_ge(*V.at(f"sp{j}"))
                    dve.tensor_tensor(slot(SU + j, c0), slot(SU + j, c0), slot(H1 + j, 0, n), ALU.mult).then_inc(*V.mark(f"uv{j}"))

            def merge_phase(l):
                ph = enter(dve, f"merge{l}", "V")
                A, V, PE, G = ph["A"], ph["V"], ph["PE"], ph["G"]
                c0 = cols(l)
                n = T - c0

                def turn(i):
                    k = 0
                    for q in range(MERGE_TILES):
                        for b in range(3):
                            dve.wait_ge(*PE.at(f"p{b}{q}", i))
                            dve.wait_ge(*A.at(f"g{b}{q}", i))
                            if b == 0:
                                dst = slot_at(M0, i, MERGE_TILES, q, c0)
                            else:
                                dst = slot(MTMP + b - 1, c0)
                                if q:
                                    dve.wait_ge(*G.at(f"m{b}{q - 1}", i))
                                else:
                                    dve.wait_ge(*G.at(f"m{b}{MERGE_TILES - 1}", i, back=1))
                            dve.tensor_tensor(dst, psum[:, (2 * k + 1) % 4, 0:n], slot(G0 + k % 3, c0), ALU.mult).then_inc(*V.mark(f"p{b}{q}"))
                            k += 1
                each(dve, ph, turn)

            def outproj_phase(key, c0, gate):
                ph = enter(dve, key, "V")
                V, PE = ph["V"], ph["PE"]

                def turn(i):
                    for q in range(4):
                        dve.wait_ge(*PE.at(f"o{q}", i))
                        for s, a, b in segs(c0):
                            x = slot_at(X0, i, 4, q, a, b)
                            ins = dve.scalar_tensor_tensor(out=x, in0=psum[:, q, a - c0:b - c0],
                                                           scalar=mod[:, bass.ds(i * 8 + (2 * (gate * KT + q) + s), 1)],
                                                           in1=x, op0=ALU.mult, op1=ALU.add)
                        ins.then_inc(*V.mark(f"x{q}"))
                each(dve, ph, turn)

            def ffn_phase(l):
                ph = enter(dve, f"ffn{l}", "V")
                A, V, PE = ph["A"], ph["V"], ph["PE"]
                c0 = cols(l)
                n = T - c0

                def turn(i):
                    for q in range(2):
                        dve.wait_ge(*PE.at(f"u{q}", i))
                        dve.wait_ge(*A.at(f"s{q}", i))
                        dve.tensor_tensor(slot_at(ACT0, i, 2, q, c0), psum[:, 2 * q + 1, 0:n], slot(YA0 + q, c0), ALU.mult).then_inc(*V.mark(f"a{q}"))
                each(dve, ph, turn)

            dve.wait_ge(s_load, 64)
            for l in range(DEPTH):
                modv_phase(l)
                norm_phase(f"norm1_{l}", 0)
                lora_phase(l)
                pair_phase(l)
                branch_phase(l)
                merge_phase(l)
                dve.wait_ge(s_back, 16 * (l + 1))
                outproj_phase(f"res1_{l}", cols(l), 2)
                norm_phase(f"norm2_{l}", cols(l))
                ffn_phase(l)
                outproj_phase(f"res2_{l}", cols(l), 5)
            norm_phase("final", CTX, final=True)

        @block.gpsimd
        def _(pool):
            def pair_phase(l):
                key = f"pair{l}"
                ph = enter(pool, key, "G")
                A, V, PE, G = ph["A"], ph["V"], ph["PE"], ph["G"]

                def turn(i):
                    def tt(name, out_, a, b, op):
                        settle(pool)
                        pool.tensor_tensor(out_, a, b, op).then_inc(*G.mark(name))

                    arrived(pool, key, i, 3)
                    pool.wait_ge(*V.at("ya", i, back=1))
                    settle(pool)
                    pool.tensor_copy(pp[:, 0:NPP], ring[:, 3 * BW + 3 * P:3 * BW + 3 * P + NPP]).then_inc(*G.mark("pp"))
                    pool.wait_ge(*G.at("pp", i))
                    settle(pool)
                    pool.tensor_scalar(pp[:, NPP:NPP + 1], ppc("ka"), -1.0, 1.0, ALU.mult, ALU.add).then_inc(*G.mark("omk"))
                    pool.wait_ge(*V.at("L0", i))
                    s = DIR0
                    tt("Le0", slot(s + 11), slot(s + 10), slot(s + 8), ALU.subtract)
                    s = DIR0 + 14
                    pool.wait_ge(*V.at("L1", i))
                    total = by_chunk(slot(s + 10))[:, :, C - 1:C].to_broadcast([P, NCH, C])
                    tt("Le1", by_chunk(slot(s + 11)), total, by_chunk(slot(s + 10)), ALU.subtract)
                    pool.wait_ge(*G.at("Le1", i))
                    tt("Li1", slot(s + 10), slot(s + 11), slot(s + 8), ALU.add)
                    for d in DIRS:
                        s = DIR0 + 14 * d
                        pool.wait_ge(*A.at(f"sa{d}", i))
                        settle(pool)
                        pool.tensor_scalar(slot(KD + d), slot(s + 9), ppc("ka"), pp[:, NPP:NPP + 1], ALU.mult, ALU.add).then_inc(*G.mark(f"kt{d}"))
                        pool.wait_ge(*G.at(f"kt{d}", i))
                        pool.wait_ge(*V.at("kc", i))
                        tt(f"kd{d}", slot(KD + d), slot(KD + d), slot(K_), ALU.mult)
                        pool.wait_ge(*G.at(f"kd{d}", i))
                        pool.wait_ge(*A.at(f"Ee{d}", i))
                        tt(f"kQ{d}", slot(s + S_K), slot(KD + d), slot(s + 12), ALU.mult)
                        end = by_chunk(slot(s + 13))[:, :, C - 1:C] if d == 0 else by_chunk(slot(s + 13))[:, :, 0:1]
                        decay = end.to_broadcast([P, NCH, C])
                        pool.wait_ge(*V.at(f"bQ{d}", i))
                        tt(f"bE{d}", by_chunk(slot(s + S_BE)), by_chunk(slot(s + S_B)), decay, ALU.mult)
                        pool.wait_ge(*G.at(f"kQ{d}", i))
                        tt(f"kE{d}", by_chunk(slot(s + S_KE)), by_chunk(slot(s + S_K)), decay, ALU.mult)
                    for d in DIRS:
                        s = DIR0 + 14 * d
                        end = by_chunk(slot(s + 13))[:, :, C - 1:C] if d == 0 else by_chunk(slot(s + 13))[:, :, 0:1]
                        pool.wait_ge(*PE.at(f"RK{d}", i))
                        tt(f"D{d}", by_chunk(slot(s + S_K)), const_b(C_ID64, C), end.to_broadcast([P, NCH, C]), ALU.mult)
                each(pool, ph, turn)

            def merge_phase(l):
                ph = enter(pool, f"merge{l}", "G")
                V, G = ph["V"], ph["G"]
                c0 = cols(l)

                def turn(i):
                    for q in range(MERGE_TILES):
                        m = slot_at(M0, i, MERGE_TILES, q, c0)
                        for b in (1, 2):
                            pool.wait_ge(*V.at(f"p{b}{q}", i))
                            if b == 2:
                                pool.wait_ge(*G.at(f"m1{q}", i))
                            settle(pool)
                            pool.tensor_tensor(m, m, slot(MTMP + b - 1, c0), ALU.add).then_inc(*G.mark(f"m{b}{q}"))
                each(pool, ph, turn)

            for l in range(DEPTH):
                pair_phase(l)
                merge_phase(l)


def seq(d):
    ctx, lat = list(range(CTX_CH)), list(range(CTX_CH, NCH))
    return ctx + lat if d == 0 else ctx[::-1] + lat[::-1]


def blocks(w):
    return w.reshape(-1, P, P).transpose(1, 0, 2).reshape(P, -1)


def tiled(v):
    return v.reshape(-1, P).T


def weight_stream(x):
    out = []

    def put(w):
        if w.shape[1] < BW:
            w = np.concatenate([w, np.zeros((P, BW - w.shape[1]), np.float32)], 1)
        out.append(w)

    def tile(w, col):
        return blocks(w[:, col:col + P])

    for l in range(DEPTH):
        w_in, up = x["w_in"][l], x["ffn_w_in"][l]
        for j in range(48):
            put(tile(x["w_mod"][l], j * P))
        for off in (OFF_W, OFF_A, OFF_G):
            put(tile(w_in, off))
        put(np.zeros((P, BW), np.float32))
        for p in range(KT):
            s = slice(p * P, p * P + P)
            for off in (0, OFF_K, OFF_V):
                put(tile(w_in, off + p * P))
            taps = [x["rwkv_shift"][l][t, off + p * P:off + p * P + P] for off in (0, OFF_K, OFF_V) for t in range(3)]
            vec = taps + [x["rwkv_w0"][l][0, s], x["rwkv_w0"][l][1, s], x["rwkv_a0"][l][0, s], x["rwkv_a0"][l][1, s],
                          x["rwkv_k_k"][l][s], x["rwkv_k_a"][l][s], x["rwkv_r_k"][l][s], x["rwkv_gn_g"][l][s],
                          x["rwkv_gn_b"][l][s]]
            put(np.concatenate([x["rwkv_w_up"][l].reshape(P, RD)[:, s], x["rwkv_a_up"][l].reshape(P, RD)[:, s],
                                x["rwkv_g_up"][l][:, s], np.stack(vec, 1)], 1))
        for j in range(CT):
            put(tile(w_in, OFF_CONV + CONV + j * P))
            put(tile(w_in, OFF_CONV + j * P))
        for j in range(2 * CT):
            put(tile(w_in, OFF_SGU + j * P))
        for j in range(KT):
            put(tile(w_in, OFF_GATE + j * P))
            put(tile(x["rwkv_out"][l], j * P))
            put(tile(w_in, OFF_GATE + D + j * P))
            put(tile(w_in, OFF_GATE + 2 * D + j * P))
            put(np.concatenate([tile(x["conv_out"][l], j * P), tile(x["sgu_out"][l], j * P)], 1))
        for j in range(KT):
            put(tile(x["w_merge"][l], j * P))
        for j in range(FT):
            put(tile(up, j * P))
            put(tile(up, DFF + j * P))
        for j in range(KT):
            w = np.concatenate([tile(x["ffn_w_out"][l], j * P), np.zeros((P, 3 * BW - FT * P), np.float32)], 1)
            for n in range(3):
                put(w[:, n * BW:(n + 1) * BW])
    return np.concatenate(out, 0)


def parameters(x, l):
    cols = [tiled(x["b_mod"][l]), tiled(x["norm1_g"][l]), tiled(x["norm2_g"][l])]
    cols.append(np.stack([x["rwkv_shift"][l][t, off:off + P] for off in (OFF_W, OFF_A, OFF_G) for t in range(3)], 1))
    cols.append(x["conv_dw"][l].reshape(TAPS, CT, P).transpose(2, 1, 0).reshape(P, CT * TAPS))
    cols += [tiled(x[n][l]) for n in ("conv_dw_b", "conv_ln_g", "conv_ln_b", "sgu_ln_g", "sgu_ln_b")]
    cols.append(tiled(x["final_norm_g"]))
    return np.concatenate(cols, 1)


def constants():
    out = np.zeros((P, NCONST), np.float32)
    r = np.arange(P)
    out[r, C_ID64 + r % C] = 1
    out[r, C_ID + r] = 1
    out[:, C_ONES:C_ONES + P] = 1
    out[:, C_EPS:C_EPS + len(EPS)] = EPS
    out[:, C_HEADS:C_HEADS + P] = (r[:, None] // HD == r[None, :] // HD)
    a, b = r[:, None] % C, np.arange(C)[None, :]
    for d in DIRS:
        after = (b > a) if d == 0 else (b < a)
        for n, name in enumerate(MASKS):
            if name == "strict":
                m = 1.0 * after
            elif name == "incl":
                m = 1.0 * (after | (a == b))
            elif name == "first":
                m = -1.0 * (after & (a // 2 == b // 2))
            else:
                w = 2 ** int(name[2:])
                same = a // (2 * w) == b // (2 * w)
                up, lo = a % (2 * w) >= w, b % (2 * w) < w
                m = 1.0 * (same & ((up & lo) if d == 0 else (~up & ~lo)))
            out[:, C_MASK + (d * len(MASKS) + n) * C:C_MASK + (d * len(MASKS) + n + 1) * C] = m
    mask = np.ones((P, T), np.float32)
    mask[:, ::C] = 0
    return out, mask


def kernel(**inputs):
    import concourse.bacc as _bacc
    from concourse.bass_utils import run_bass_kernel_spmd as _run

    x = {k: np.asarray(v) for k, v in inputs.items()}
    const, scanmask = constants()
    tokens = np.concatenate([x["ctx"][0], x["x"][0]], 0)
    arrays = {
        "x": tokens.reshape(T, KT, P).transpose(2, 1, 0).reshape(P, KT * T),
        "c": np.stack([x["c_ctx"], x["c"][0]], 1).reshape(KT, P, 2).transpose(1, 0, 2).reshape(P, 2 * KT),
        "w_stream": weight_stream(x),
        "par": np.stack([parameters(x, l) for l in range(DEPTH)]),
        "const": const,
        "scanmask": scanmask,
        "sgu_w": x["sgu_w"].transpose(0, 3, 1, 2).reshape(DEPTH, P, GROUPS * P),
        "sgu_b": np.repeat(x["sgu_b"].reshape(DEPTH, CT, 2, P), HD, axis=2).transpose(0, 2, 1, 3).reshape(DEPTH, P, CT * P),
    }
    arrays = {f"{k}_in": np.ascontiguousarray(v) for k, v in arrays.items()}
    nc = _bacc.Bacc("TRN2", target_bir_lowering=False, num_devices=1)
    args = [nc.dram_tensor(k, v.shape, F32, kind="ExternalInput").ap() for k, v in arrays.items()]
    out = nc.dram_tensor("out", (P, KT, LAT), F32, kind="ExternalOutput").ap()
    build(nc, *args, out)
    r = _run(nc, [arrays], core_ids=[0])
    y = r.results[0]["out"]
    return y.transpose(2, 1, 0).reshape(1, LAT, D)
```

```python
from contextlib import ExitStack

import numpy as np

import concourse.bass as bass
from concourse import mybir

ALU = mybir.AluOpType
ACT = mybir.ActivationFunctionType
F32 = mybir.dt.float32

P = 128
D = 1024
DEPTH = 2
CTX = 256
LAT = 512
T = CTX + LAT
GRID_W = 64
KT = D // P
HD = 64
C = 64
NCH = T // C
CTX_CH = CTX // C
RD = D
CONV = D // 2
SGU = D // 2
CT = CONV // P
TAPS = 31
DFF = ((8 * D // 3 + 255) // 256) * 256
FT = DFF // P
OFF_K, OFF_V, OFF_W = RD, 2 * RD, 3 * RD
OFF_A, OFF_G = OFF_W + 128, OFF_W + 256
OFF_CONV = OFF_G + 128
OFF_SGU = OFF_CONV + 2 * CONV
OFF_GATE = OFF_SGU + 2 * SGU
P_IN = OFF_GATE + 3 * D
GROUPS = 8
KAPPA = float(np.exp(-0.5))
BW = 8 * P

C_ID64, C_ID, C_ONES, C_HEADS, C_EPS, C_MASK = 0, 64, 192, 320, 448, 452
LN_SHIFT = 24
EPS = (1e-6, 1e-5, 64e-5, 0.5 * LN_SHIFT * float(np.log(2.0)))
MASKS = ["strict", "incl", "first"] + [f"lv{n}" for n in range(1, 6)]
NCONST = C_MASK + 2 * len(MASKS) * C

PAR = {}
_at = 0
for _name, _n in (("b_mod", 48), ("n1g", 8), ("n2g", 8), ("shift", 9), ("dw", CT * TAPS), ("dwb", CT),
                  ("clg", CT), ("clb", CT), ("slg", CT), ("slb", CT), ("fin", 8)):
    PAR[_name] = _at
    _at += _n
NPAR = _at

PP = {n: i for i, n in enumerate(
    ["r0", "r1", "r2", "k0", "k1", "k2", "v0", "v1", "v2", "w00", "w01", "a00", "a01",
     "kk", "ka", "rk", "gng", "gnb"])}
NPP = len(PP)

H0, LW, LA, LG = 0, 8, 9, 10
SCANMASK = 11
F0 = 12
F_R, F_KK, F_B, F_K, F_BE, F_KE = range(6)
M0_ = 24
M_A, M_BT, M_RB, M_RK, M_BET, M_KET, M_KKT, M_XT, M_X, M_T, M_BV = range(11)
M_U0, M_G, M_N, M_Q, M_MT, M_S = M_A, M_BT, M_KKT, M_X, M_T, M_BV
VT, R_, K_, V_, BN, GZ, T0, T1, T2, KK_ = range(46, 56)
LE0, EI0, LE1, EI1 = range(56, 60)
NSLOT = 61
PT0, PT1 = M0_ + M_XT, M0_ + 11 + M_XT
YA0 = 12
M0, X0 = 21, 29
CU, CY, SU, SV, VTK = 37, 41, 45, 49, 53
G0 = 57
NT = 60
H1, SGW, SGB, MTMP = 21, 25, 27, 53
ACT0 = 37


class Steps:

    def __init__(self, sem, names, turns=1, lead=False):
        self.sem, self.names, self.turns, self.lead = sem, list(names), turns, lead
        self.index = {n: i for i, n in enumerate(self.names)}
        assert len(self.index) == len(self.names)
        self.k = 0

    def at(self, name, turn=0, back=0):
        return self.sem, turn * len(self.names) + (int(self.lead) - back) * len(self.names) + self.index[name] + 1

    def mark(self, name):
        assert self.names[self.k] == name, (self.names[self.k], name)
        self.k = (self.k + 1) % len(self.names)
        return self.sem, 1

    def end(self):
        return self.sem, (self.turns + int(self.lead)) * len(self.names)

    def credit(self, eng):
        if self.lead:
            eng.sem_inc(self.sem, len(self.names))


def names_norm():
    return dict(PE=["sum"], A=[f"sq{j}" for j in range(KT)] + ["ln", "rstd"] + [f"h{j}" for j in range(KT)],
                V=[f"xn{j}" for j in range(KT)], G=[])


def names_lora():
    return dict(PE=["w", "a", "g", "pad"],
                A=["raw0", "raw1", "raw2", "act0", "act2"],
                V=[f"s{n}{x}" for n in range(3) for x in "abc"], G=[])


LEVELS = range(1, 6)
DIRS = (0, 1)
CHAIN = range(1, NCH - 1)
BOTH = {"prep", "scan"}
PAIR_PHASES = (("first", {"prep"}, 1), ("pairs", BOTH, KT - 1), ("last", {"scan"}, 1))


def names_pair(parts):
    def pick(*groups):
        return [n for part, names in groups if part in parts for n in names]

    def both(*names):
        return [f"{n}{d}" for d in DIRS for n in names]

    def level(n, *names):
        return [f"{x}{n}{d}" for x in names for d in DIRS]

    pe = pick(
        ("scan", both("kkT", "bT", "kT") + ["vT", "bonus", "gu"] + both("A", "B", "RB", "RK") + ["BV0", "BV1"]),
        ("prep", ["zr"]), ("scan", level(1, "T", "U")),
        ("prep", ["zk"]), ("scan", level(2, "T", "U")),
        ("prep", both("lw", "la")), ("scan", level(3, "T", "U")),
        ("prep", ["kkn"]), ("scan", level(4, "T", "U") + level(5, "T", "U")),
        ("scan", both("U0", "G") + both("MT", "N", "Q") + [f"c{n}{d}" for n in CHAIN for d in DIRS] + ["Y"]),
        ("prep", ["zv"]), ("scan", ["mean", "var"]))
    wide = [n for n in pe if not (n[0] == "c")]
    if "scan" in parts:
        k = wide.index("Y")
        wide[k:k] = ["chain0", "chain1"]
    a = pick(
        ("scan", both("kkT", "bT", "kT") + ["vT", "gz", "A0", "A1", "BV0", "BV1"]),
        ("prep", ["raw_r", "raw_k"] + both("sw", "sa") + ["kksq", "kkl", "kke"] + both("Ei", "En", "Ee")),
        ("scan", both("U0", "G") + ["N0", "N1", "y"]),
        ("prep", ["raw_v"]), ("scan", ["ysq", "yln", "yrs", "yn"]))
    v = pick(
        ("scan", ["bon", "bv"] + both("X1a", "X1b", "X", "B", "RB", "RK")
         + level(1, "T") + both("XT1", "Xt1")),
        ("prep", ["ra", "rb", "rc"]), ("scan", level(2, "T") + both("XT2", "Xt2")),
        ("prep", ["ka", "kb", "kc", "kk0"]), ("scan", level(3, "T") + both("XT3", "Xt3")),
        ("prep", ["L0", "L1", "kkm"]), ("scan", level(4, "T") + both("XT4", "Xt4")),
        ("prep", ["kk"]), ("scan", level(5, "T") + both("XT5")),
        ("prep", both("b", "kkP", "bQ")), ("scan", both("MT", "Q")),
        ("prep", ["rP0", "rP1"]), ("scan", [f"c{n}{d}" for n in CHAIN for d in DIRS] + ["yc"]),
        ("prep", ["va", "vb", "vc"]), ("scan", ["ynr", "yb", "ya"]))
    g = pick(
        ("scan", ["ppc"]), ("prep", ["pp", "omk", "Le0", "Le1", "Li1"] + both("kt", "kd")),
        ("scan", ["D0", "D1"]), ("prep", both("kQ", "bE", "kE") + ["pc0", "pc1"]), ("scan", ["yst"]))
    return dict(PE=pe, A=a, V=v, G=g), wide


def names_branch(l):
    taps = conv_taps(l)
    pe = []
    for j in range(CT):
        pe += [f"cb{j}", f"ca{j}"]
    pe += [f"su{j}" for j in range(CT)] + [f"sv{j}" for j in range(CT)]
    pe += ["cmean", "cvar", "smean", "svar"] + [f"tr{j}" for j in range(CT)] + [f"sp{j}" for j in range(CT)]
    a = [f"cb{j}" for j in range(CT)] + [f"su{j}" for j in range(CT)] + [f"sv{j}" for j in range(CT)]
    a += [f"csq{j}" for j in range(CT)] + [f"ssq{j}" for j in range(CT)]
    a += ["cln", "cr", "sln", "sr"] + [f"cs{j}" for j in range(CT)]
    a += [f"sn{j}" for j in range(CT)] + [f"tr{j}" for j in range(CT)]
    v = []
    for j in range(CT):
        v += [f"u{j}"] + [f"y{j}_{n}" for n in range(len(taps))]
    v += [f"cc{j}" for j in range(CT)] + [f"sc{j}" for j in range(CT)]
    v += [f"cn{j}" for j in range(CT)] + [f"sm{j}" for j in range(CT)]
    for j in range(CT):
        v += [f"sp{j}", f"uv{j}"]
    return dict(PE=pe, A=a, V=v, G=[])


MERGE_TILES = 4


def names_merge():
    pe, a, v, g = [], [], [], []
    for q in range(MERGE_TILES):
        for b in range(3):
            pe += [f"g{b}{q}", f"p{b}{q}"]
            a += [f"g{b}{q}"]
            v += [f"p{b}{q}"]
            if b:
                g += [f"m{b}{q}"]
    return dict(PE=pe, A=a, V=v, G=g)


def names_outproj():
    return dict(PE=[f"o{q}" for q in range(4)], A=[], V=[f"x{q}" for q in range(4)], G=[])


def names_ffn():
    return dict(PE=["g0", "u0", "g1", "u1"], A=["s0", "s1"], V=["a0", "a1"], G=[])


def conv_taps(l):
    reach = 15 if l % 2 == 0 else (LAT // GRID_W) - 1
    return [0] + [o for n in range(1, reach + 1) for o in (-n, n)]


def build(nc, x_in, c_in, w_stream, par_in, const_in, scanmask_in, sgu_w_in, sgu_b_in, out):
    spill = nc.dram_tensor("x_spill", (P, KT * T), F32, kind="Internal").ap()
    ya_spill = nc.dram_tensor("ya_spill", (P, KT * T), F32, kind="Internal").ap()
    ya_v = ya_spill.rearrange("p (j t) -> p j t", t=T)
    with ExitStack() as st:
        def sem(name):
            return st.enter_context(nc.semaphore(name))

        arena = st.enter_context(nc.sbuf_tensor("arena", [P, NSLOT * T], F32))
        ring = st.enter_context(nc.sbuf_tensor("ring", [P, 4 * BW], F32))
        const = st.enter_context(nc.sbuf_tensor("const", [P, NCONST], F32))
        par = st.enter_context(nc.sbuf_tensor("par", [P, NPAR], F32))
        cvec = st.enter_context(nc.sbuf_tensor("cvec", [P, 2 * KT], F32))
        sc = st.enter_context(nc.sbuf_tensor("sc", [P, 2 * KT], F32))
        mod = st.enter_context(nc.sbuf_tensor("mod", [P, 48 * 2], F32))
        a_mod = st.enter_context(nc.sbuf_tensor("a_mod", [P, 2 * 2 * KT], F32))
        pp = st.enter_context(nc.sbuf_tensor("pp", [P, 2 * NPP + 1], F32))
        decays = st.enter_context(nc.sbuf_tensor("decays", [P, 2 * NCH], F32))
        psum = st.enter_context(nc.psum_tensor("psum", [P, 4, 1024], F32))

        w_in = [sem(f"weights_in_{i}") for i in range(4)]
        s_load = sem("inputs_loaded")
        s_settled = sem("settled")
        s_par = sem("params_loaded")
        s_spill = sem("x_spilled")
        s_back = sem("x_reloaded")
        s_ya = sem("scan_output_stored")
        s_sgu = sem("sgu_params_loaded")
        s_out = sem("output_stored")

        phases, at_end = {}, []

        def phase(key, names, turns=1, lead=False, chunks=()):
            ph = {e: Steps(sem(f"{key}_{e}"), ns, turns, lead) for e, ns in names.items() if ns}
            ph["chunks"], ph["turns"] = list(chunks), turns
            phases[key] = ph
            at_end.append((key, ph))
            return ph

        phase("cond", dict(PE=[], A=["silu"], V=[], G=[]))
        for l in range(DEPTH):
            phase(f"mod{l}", dict(PE=["m0", "m1", "m2", "m3"], A=[], V=[], G=[]), 12, chunks=["m0", "m1", "m2", "m3"])
            phase(f"modv{l}", dict(PE=[], A=[], V=["mod", "a1", "a2"], G=[]))
            phase(f"norm1_{l}", names_norm())
            phase(f"lora{l}", names_lora(), chunks=["w", "a", "g", "pad"])
            for name, parts, turns in PAIR_PHASES:
                phase(f"{name}{l}", names_pair(parts)[0], turns, lead=turns > 1,
                      chunks=["zr", "zk", None, "zv"] if "prep" in parts else [])
                phases[f"{name}{l}"]["parts"] = parts
            ch = []
            for j in range(CT):
                ch += [f"cb{j}", f"ca{j}"]
            phase(f"branch{l}", names_branch(l), chunks=ch + [f"su{j}" for j in range(CT)] + [f"sv{j}" for j in range(CT)])
            ch = []
            for q in range(MERGE_TILES):
                ch += [f"g0{q}", f"p0{q}", f"g1{q}", f"g2{q}", f"p2{q}"]
            phase(f"merge{l}", names_merge(), KT // MERGE_TILES, lead=True, chunks=ch)
            phase(f"res1_{l}", names_outproj(), 2, lead=True, chunks=["o0", "o1", "o2", "o3"])
            phase(f"norm2_{l}", names_norm())
            phase(f"ffn{l}", names_ffn(), FT // 2, lead=True, chunks=["g0", "u0", "g1", "u1"])
            phase(f"res2_{l}", names_outproj(), 2, lead=True,
                  chunks=[f"o{q}" for q in range(4) for _ in range(3)])
        phase("final", dict(PE=["sum"], A=[f"sq{j}" for j in range(KT)] + ["ln", "rstd"], V= [f"xn{j}" for j in range(KT)] + [f"y{j}" for j in range(KT)], G=[]))

        order = [k for k, _ in at_end]
        for key, ph in phases.items():
            assert len(ph["chunks"]) % 4 == 0
        chunk_base, n = {}, 0
        for key in order:
            chunk_base[key] = n
            n += len(phases[key]["chunks"]) * phases[key]["turns"]
        assert n * P == w_stream.shape[0]
        w_v = w_stream.rearrange("(n p) c -> p n c", p=P)

        def enter(eng, key, own):
            k = order.index(key)
            if k:
                prev = phases[order[k - 1]]
                for e in ("PE", "A", "V", "G"):
                    if e in prev:
                        eng.wait_ge(*prev[e].end())
            if own in phases[key]:
                phases[key][own].credit(eng)
            return phases[key]

        def settle(eng):
            eng.sem_inc(s_settled, 1)

        def wait_steps(eng, turn, *steps):
            latest = {}
            for E, name, back in steps:
                if back and not E.lead:
                    continue
                if E not in latest or (-back, E.index[name]) > latest[E]:
                    latest[E] = (-back, E.index[name])
            for E, (back, k) in latest.items():
                eng.wait_ge(*E.at(E.names[k], turn, back=-back))

        def each(eng, ph, body):
            if ph["turns"] == 1:
                body(0)
            else:
                with eng.Fori(0, ph["turns"]) as i:
                    body(i)

        def slot(n, a=0, b=T):
            return arena[:, n * T + a:n * T + b]

        def slot_at(n0, turn, per, q, a=0, b=T):
            return arena[:, bass.ds((turn * per + (n0 + q)) * T + a, b - a)]

        def by_chunk(ap, c0=0):
            return ap.rearrange("p (c t) -> p c t", t=C)

        def const_b(col, n, nch=NCH):
            return const[:, None, col:col + n].to_broadcast([P, nch, n])

        def mask(name, d, nch=NCH):
            return const_b(C_MASK + (d * len(MASKS) + MASKS.index(name)) * C, C, nch)

        def par_c(name, k=0, n=1):
            return par[:, PAR[name] + k:PAR[name] + k + n]

        def ppc(name):
            return pp[:, PP[name]:PP[name] + 1]

        def ppn(name):
            return pp[:, NPP + 1 + PP[name]:NPP + 2 + PP[name]]

        def eps_c(n):
            return const[:, C_EPS + n:C_EPS + n + 1]

        ident = const[:, C_ID:C_ID + P]
        ones = const[:, C_ONES:C_ONES + P]
        heads = const[:, C_HEADS:C_HEADS + P]

        def cols(l):
            return 0 if l < DEPTH - 1 else CTX

        def segs(c0):
            return ([(0, 0, CTX)] if c0 == 0 else []) + [(1, CTX, T)]

        def halves(c0, off):
            cut = 512 + off
            return [(a, b) for a, b in ((c0, min(cut, T)), (max(cut, c0), T)) if a < b]

        def project(eng, tile, lhs, rhs, c0, off):
            mm = None
            for a, b in halves(c0, off):
                for k in range(len(lhs)):
                    mm = eng.matmul(psum[0:lhs[k].shape[-1], tile, a - off:b - off], lhsT=lhs[k], rhs=rhs[k][:, a:b],
                                    start=(k == 0), stop=(k == len(lhs) - 1))
            return mm

        def chunk_blocks(n, k0=0, nk=8):
            s = n % 4
            return [ring[:, s * BW + k * P:s * BW + (k + 1) * P] for k in range(k0, k0 + nk)]

        def arrived(eng, key, turn, q):
            base = chunk_base[key] // 4
            per = len(phases[key]["chunks"]) // 4
            eng.wait_ge(w_in[q % 4], 16 * (turn * per + (base + q // 4 + 1)))

        hs = [slot(H0 + j) for j in range(KT)]
        sgu_w = arena[:, SGW * T:SGW * T + GROUPS * P]
        sgu_b = arena[:, SGB * T:SGB * T + CT * P]
        block = st.enter_context(nc.Block())

        @block.sync
        def _(sp):
            last = {}

            def load(q, n):
                sp.dma_start(ring[:, None, (q % 4) * BW:(q % 4 + 1) * BW], w_v[:, n, :]).then_inc(w_in[q % 4], 16)

            for key in order:
                ph = phases[key]
                names, turns = ph["chunks"], ph["turns"]
                if not names:
                    continue
                nq, S = len(names), ph["PE"]
                for q in range(nq):
                    if names[q] is None and key.startswith("pairs"):
                        sp.wait_ge(*S.at("gu", 0))
                    elif q % 4 in last:
                        sp.wait_ge(*last[q % 4])
                    load(q, slice(chunk_base[key] + q, chunk_base[key] + q + 1))
                    if names[q]:
                        last[q % 4] = S.at(names[q], 0)
                if turns > 1:
                    with sp.Fori(1, turns) as i:
                        for q in range(nq):
                            if names[q] is None:
                                sp.wait_ge(*S.at("gu", i))
                            elif q < 4:
                                sp.wait_ge(*S.at(names[nq - 4 + q], i, back=1))
                            else:
                                sp.wait_ge(*S.at(names[q - 4], i))
                            load(q, bass.ds(i * nq + (chunk_base[key] + q), 1))
                    for q in range(nq):
                        if names[q]:
                            last[q % 4] = S.at(names[q], turns - 1)
                        else:
                            last[q % 4] = phases["last" + key[-1]]["PE"].at("gu")

        @block.tensor
        def _(pe):
            def mod_phase(l):
                key = f"mod{l}"
                ph = enter(pe, key, "PE")
                S = ph["PE"]

                def turn(i):
                    for q in range(4):
                        arrived(pe, key, i, q)
                        blocks = chunk_blocks(q)
                        for k in range(KT):
                            mm = pe.matmul(psum[:, 0, bass.ds((i * 4 + q) * 2, 2)], lhsT=blocks[k],
                                           rhs=sc[:, 2 * k:2 * k + 2], start=(k == 0), stop=(k == KT - 1))
                        mm.then_inc(*S.mark(f"m{q}"))
                each(pe, ph, turn)

            def norm_phase(key, c0):
                ph = enter(pe, key, "PE")
                for j in range(KT):
                    pe.wait_ge(*ph["A"].at(f"sq{j}"))
                    for a, b in halves(c0, 0):
                        mm = pe.matmul(psum[:, 0, a:b], lhsT=ones, rhs=slot(H0 + j, a, b),
                                       start=(j == 0), stop=(j == KT - 1), skip_group_check=True)
                mm.then_inc(*ph["PE"].mark("sum"))

            def lora_phase(l):
                key = f"lora{l}"
                ph = enter(pe, key, "PE")
                for q, name in enumerate(["w", "a", "g"]):
                    arrived(pe, key, 0, q)
                    project(pe, q, chunk_blocks(q), hs, 0, 0).then_inc(*ph["PE"].mark(name))
                arrived(pe, key, 0, 3)
                pe.matmul(psum[:, 3, 0:2], lhsT=chunk_blocks(3)[0], rhs=hs[0][:, 0:2], start=True,
                          stop=True).then_inc(*ph["PE"].mark("pad"))

            def pair_phase(key, l):
                ph = enter(pe, key, "PE")
                S, A, V, G = (ph.get(e) for e in ("PE", "A", "V", "G"))
                parts = ph["parts"]
                prep, scan = "prep" in parts, "scan" in parts
                _, wide = names_pair(parts)
                y0 = cols(l)
                freed = {"zr": (A, "raw_r"), "zk": (A, "raw_k"), "zv": (A, "raw_v"), "gu": (A, "gz"),
                         "kkn": (V, "kkm"), "vT": (A, "vT"), "Y": (A, "y"), "mean": (V, "yc"),
                         "var": (A, "yln"), "bonus": (V, "bv")}
                for d in DIRS:
                    freed.update({f"lw{d}": (A, f"sw{d}"), f"la{d}": (A, f"sa{d}"), f"kkT{d}": (A, f"kkT{d}"),
                                  f"bT{d}": (A, f"bT{d}"), f"kT{d}": (A, f"kT{d}"), f"A{d}": (A, f"A{d}"),
                                  f"B{d}": (V, f"B{d}"), f"RB{d}": (V, f"RB{d}"), f"RK{d}": (V, f"RK{d}"),
                                  f"BV{d}": (A, f"BV{d}"), f"U0{d}": (A, f"U0{d}"), f"G{d}": (A, f"G{d}"),
                                  f"MT{d}": (V, f"MT{d}"), f"N{d}": (A, f"N{d}"), f"Q{d}": (V, f"Q{d}"),
                                  f"chain{d}": (V, f"c{NCH - 2}{d}")})
                    for n in LEVELS:
                        freed.update({f"T{n}{d}": (V, f"T{n}{d}"), f"U{n}{d}": (V, f"XT{n}{d}")})

                def turn(i):
                    def take(name, *also):
                        k = wide.index(name)
                        steps = [(*x, 0)[:3] for x in also]
                        if k >= 4:
                            steps.append((*freed[wide[k - 4]], 0))
                        else:
                            before = [n for m, n in enumerate(wide) if m % 4 == k]
                            steps.append((*freed[before[-1]], 1))
                        wait_steps(pe, i, *steps)
                        return k % 4

                    def mm64(tile, c, h, lhs, rhs, start, stop):
                        rows = slice(h * HD, h * HD + HD)
                        right = const[rows, C_ID64:C_ID64 + C] if rhs is None else arena[rows, rhs:rhs + C]
                        return pe.matmul(psum[rows, tile, c * C:c * C + C], lhsT=arena[rows, lhs:lhs + C], rhs=right,
                                         start=start, stop=stop, skip_group_check=True)

                    def units(tile, terms, c0=0):
                        mm = None
                        settle(pe)
                        for c in range(c0 // C, NCH):
                            for h in range(2):
                                for k, (lo, ro) in enumerate(terms):
                                    mm = mm64(tile, c, h, lo * T + c * C, None if ro is None else ro * T + c * C,
                                              k == 0, k == len(terms) - 1)
                        return mm

                    def inputs(name, q):
                        tile = take(name)
                        arrived(pe, key, i, q)
                        project(pe, tile, chunk_blocks(q), hs, 0, 0).then_inc(*S.mark(name))

                    def level(n):
                        for d in DIRS:
                            m = M0_ + 11 * d
                            tile = take(f"T{n}{d}", (V, f"X{d}" if n == 1 else f"Xt{n - 1}{d}"), (A, f"A{d}"))
                            units(tile, [(m + M_A, m + M_X)]).then_inc(*S.mark(f"T{n}{d}"))
                        for d in DIRS:
                            m = M0_ + 11 * d
                            tile = take(f"U{n}{d}", (V, f"T{n}{d}"))
                            units(tile, [(m + M_T, m + M_XT)]).then_inc(*S.mark(f"U{n}{d}"))

                    if scan:
                        for d in DIRS:
                            f = F0 + 6 * d
                            ready = [(V, f"bQ{d}", 1), (G, f"kE{d}", 1)] if prep else []
                            for name, src in (("kkT", F_KK), ("bT", F_BE), ("kT", F_KE)):
                                units(take(f"{name}{d}", *ready), [(f + src, None)]).then_inc(*S.mark(f"{name}{d}"))
                        tile = take("vT", *([(V, "vc", 1)] if prep else []))
                        units(tile, [(V_, None)]).then_inc(*S.mark("vT"))
                        tile = take("bonus", (V, "bon"))
                        project(pe, tile, [heads], [slot(BN)], y0, 0).then_inc(*S.mark("bonus"))
                        tile = take("gu")
                        project(pe, tile, [ring[:, 2 * BW + 2 * P:2 * BW + 3 * P]], [slot(LG)], y0, 0).then_inc(*S.mark("gu"))
                        for d in DIRS:
                            f = F0 + 6 * d
                            ready = [(V, f"rP{d}", 1)] if prep else []
                            units(take(f"A{d}"), [(f + F_B, f + F_KK)]).then_inc(*S.mark(f"A{d}"))
                            units(take(f"B{d}"), [(f + F_K, f + F_KK)]).then_inc(*S.mark(f"B{d}"))
                            units(take(f"RB{d}", *ready), [(f + F_B, f + F_R)], y0).then_inc(*S.mark(f"RB{d}"))
                            units(take(f"RK{d}"), [(f + F_K, f + F_R)], y0).then_inc(*S.mark(f"RK{d}"))
                        for d in DIRS:
                            m = M0_ + 11 * d
                            tile = take(f"BV{d}", (V, f"B{d}"), (A, "vT"))
                            units(tile, [(m + M_BT, VT)]).then_inc(*S.mark(f"BV{d}"))
                    if prep:
                        inputs("zr", 0)
                    if scan:
                        level(1)
                    if prep:
                        inputs("zk", 1)
                    if scan:
                        level(2)
                    if prep:
                        arrived(pe, key, i, 2)
                        for d in DIRS:
                            for n, (name, src) in enumerate((("lw", LW), ("la", LA))):
                                tile = take(f"{name}{d}")
                                rows = slice(d * HD, d * HD + HD)
                                for a, b in halves(0, 0):
                                    mm = pe.matmul(psum[:, tile, a:b], lhsT=ring[rows, 2 * BW + n * P:2 * BW + n * P + P],
                                                   rhs=arena[rows, src * T + a:src * T + b], start=True, stop=True)
                                mm.then_inc(*S.mark(f"{name}{d}"))
                    if scan:
                        level(3)
                    if prep:
                        tile = take("kkn", (A, "kksq"))
                        project(pe, tile, [heads], [slot(T0)], 0, 0).then_inc(*S.mark("kkn"))
                    if scan:
                        level(4)
                        level(5)
                        for d in DIRS:
                            m = M0_ + 11 * d
                            tile = take(f"U0{d}", (V, f"XT5{d}"), (A, f"BV{d}"))
                            units(tile, [(m + M_XT, m + M_BV)]).then_inc(*S.mark(f"U0{d}"))
                            units(take(f"G{d}"), [(m + M_XT, m + M_KKT)]).then_inc(*S.mark(f"G{d}"))
                        for d in DIRS:
                            m = M0_ + 11 * d
                            tile = take(f"MT{d}", (A, f"G{d}"))
                            units(tile, [(m + M_G, m + M_BET)]).then_inc(*S.mark(f"MT{d}"))
                            units(take(f"N{d}"), [(m + M_BET, m + M_U0), (m + M_KET, VT)]).then_inc(*S.mark(f"N{d}"))
                            units(take(f"Q{d}"), [(m + M_G, m + M_RB)], y0).then_inc(*S.mark(f"Q{d}"))
                        tiles = [take(f"chain{d}", (V, f"MT{d}"), (A, f"N{d}")) for d in DIRS]
                        ytile = take("Y")
                        free = []
                        for d in DIRS:
                            m = M0_ + 11 * d
                            free += [(c, h, lo * T + c * C, ro * T + c * C) for c in range(y0 // C, NCH) for h in range(2)
                                     for lo, ro in ((m + M_U0, m + M_RB), (VT, m + M_RK))]
                        per = -(-len(free) // (len(CHAIN) * 2))
                        opened = set()
                        for n in CHAIN:
                            for d in DIRS:
                                m, c = M0_ + 11 * d, seq(d)[n]
                                if n == 1:
                                    state = (m + M_N) * T + seq(d)[0] * C
                                else:
                                    pe.wait_ge(*V.at(f"c{n - 1}{d}", i))
                                    state = (m + M_S) * T + c * C
                                settle(pe)
                                for h in range(2):
                                    mm = mm64(tiles[d], c, h, (m + M_MT) * T + c * C, state, True, True)
                                mm.then_inc(*S.mark(f"c{n}{d}"))
                                for cc, h, lo, ro in free[:per]:
                                    bank = (cc * C // 512, h)
                                    mm64(ytile, cc, h, lo, ro, bank not in opened, False)
                                    opened.add(bank)
                                free = free[per:]
                        assert not free
                        wait_steps(pe, i, (V, f"c{NCH - 2}1", 0))
                        settle(pe)
                        for c in range(y0 // C, NCH):
                            for d in DIRS:
                                m, n = M0_ + 11 * d, seq(d).index(c)
                                if n == 0:
                                    continue
                                state = (m + M_N) * T + seq(d)[0] * C if n == 1 else (m + M_S) * T + c * C
                                for h in range(2):
                                    mm = mm64(ytile, c, h, state, (m + M_Q) * T + c * C, False, True)
                        mm.then_inc(*S.mark("Y"))
                    if prep:
                        inputs("zv", 3)
                    if scan:
                        tile = take("mean", (A, "y"))
                        project(pe, tile, [heads], [slot(PT0)], y0, 0).then_inc(*S.mark("mean"))
                        tile = take("var", (A, "ysq"))
                        project(pe, tile, [heads], [slot(PT1)], y0, 0).then_inc(*S.mark("var"))
                each(pe, ph, turn)

            def branch_phase(l):
                key = f"branch{l}"
                ph = enter(pe, key, "PE")
                S, A, V = ph["PE"], ph["A"], ph["V"]
                c0 = cols(l)
                seq_ = []
                for j in range(CT):
                    seq_ += [(f"cb{j}", A, f"cb{j}"), (f"ca{j}", V, f"u{j}")]
                seq_ += [(f"su{j}", A, f"su{j}") for j in range(CT)] + [(f"sv{j}", A, f"sv{j}") for j in range(CT)]
                for n, (name, _, _) in enumerate(seq_):
                    if n >= 4:
                        _, E, step = seq_[n - 4]
                        pe.wait_ge(*E.at(step))
                    arrived(pe, key, 0, n)
                    project(pe, n % 4, chunk_blocks(n), hs, c0, c0).then_inc(*S.mark(name))
                pe.wait_ge(*A.at(f"sv{CT - 1}"))
                for name, tile, src, E, step in (("cmean", 0, CY, V, None), ("cvar", 1, CU, A, "csq"),
                                                 ("smean", 2, SV, A, None), ("svar", 3, H1, A, "ssq")):
                    if name == "cmean":
                        pe.wait_ge(*V.at(f"y{CT - 1}_{len(conv_taps(l)) - 1}"))
                    if step:
                        pe.wait_ge(*A.at(f"{step}{CT - 1}"))
                    project(pe, tile, [ones] * CT, [slot(src + j) for j in range(CT)], c0, c0).then_inc(*S.mark(name))
                for j in range(CT):
                    pe.wait_ge(*A.at(f"sn{j}"))
                    if j == 0:
                        pe.wait_ge(*A.at("sr"))
                        pe.wait_ge(*V.at(f"sc{CT - 1}"))
                    for n in range((T - c0) // P):
                        a = c0 + n * P
                        mm = pe.matmul(psum[:, j, n * P:n * P + P], lhsT=slot(SV + j, a, a + P), rhs=ident,
                                       start=True, stop=True, skip_group_check=True)
                    mm.then_inc(*S.mark(f"tr{j}"))
                for j in range(CT):
                    pe.wait_ge(*A.at(f"tr{j}"))
                    if j == 0:
                        pe.wait_ge(s_sgu, 32 * (l + 1))
                    for n in range((T - c0) // P):
                        for g in range(2):
                            mm = pe.matmul(psum[g * HD:g * HD + HD, j, n * P:n * P + P],
                                           lhsT=arena[:, (VTK + j) * T + n * P + g * HD:(VTK + j) * T + n * P + g * HD + HD],
                                           rhs=sgu_w[:, (2 * j + g) * P:(2 * j + g + 1) * P],
                                           start=True, stop=True, skip_group_check=True)
                    mm.then_inc(*S.mark(f"sp{j}"))

            def merge_phase(l):
                key = f"merge{l}"
                ph = enter(pe, key, "PE")
                S, A, V = ph["PE"], ph["A"], ph["V"]
                c0 = cols(l)
                ya = [slot(YA0 + j) for j in range(KT)]
                cv = [slot(CY + j) for j in range(CT)]
                sg = [slot(SU + j) for j in range(CT)]

                pe.wait_ge(s_back, 32 * (l + 1))

                def turn(i):
                    flow = []
                    for q in range(MERGE_TILES):
                        flow += [(f"g0{q}", 5 * q, 0, 8, hs, A), (f"p0{q}", 5 * q + 1, 0, 8, ya, V),
                                 (f"g1{q}", 5 * q + 2, 0, 8, hs, A), (f"p1{q}", 5 * q + 4, 0, 4, cv, V),
                                 (f"g2{q}", 5 * q + 3, 0, 8, hs, A), (f"p2{q}", 5 * q + 4, 4, 4, sg, V)]
                    for n, (name, chunk, k0, nk, mov, _) in enumerate(flow):
                        if n >= 4:
                            pe.wait_ge(*flow[n - 4][5].at(flow[n - 4][0], i))
                        else:
                            pe.wait_ge(*flow[n - 4][5].at(flow[n - 4][0], i, back=1))
                        arrived(pe, key, i, chunk)
                        project(pe, n % 4, chunk_blocks(chunk, k0, nk), mov, c0, c0).then_inc(*S.mark(name))
                each(pe, ph, turn)

            def outproj_phase(key, c0, mov, per):
                ph = enter(pe, key, "PE")
                S, V = ph["PE"], ph["V"]

                def turn(i):
                    for q in range(4):
                        pe.wait_ge(*V.at(f"x{q}", i, back=1))
                        lhs = []
                        for n in range(per):
                            arrived(pe, key, i, per * q + n)
                            lhs += chunk_blocks(per * q + n)
                        project(pe, q, lhs[:len(mov)], mov, c0, c0).then_inc(*S.mark(f"o{q}"))
                each(pe, ph, turn)

            def ffn_phase(l):
                key = f"ffn{l}"
                ph = enter(pe, key, "PE")
                S, A, V = ph["PE"], ph["A"], ph["V"]
                c0 = cols(l)

                def turn(i):
                    for q, (name, E, step) in enumerate((("g0", A, "s0"), ("u0", V, "a0"), ("g1", A, "s1"), ("u1", V, "a1"))):
                        pe.wait_ge(*E.at(step, i, back=1))
                        arrived(pe, key, i, q)
                        project(pe, q, chunk_blocks(q), hs, c0, c0).then_inc(*S.mark(name))
                each(pe, ph, turn)

            pe.wait_ge(*phases["cond"]["A"].at("silu"))
            for l in range(DEPTH):
                mod_phase(l)
                norm_phase(f"norm1_{l}", 0)
                lora_phase(l)
                for name, _, _ in PAIR_PHASES:
                    pair_phase(f"{name}{l}", l)
                branch_phase(l)
                merge_phase(l)
                outproj_phase(f"res1_{l}", cols(l), [slot(M0 + j) for j in range(KT)], 1)
                norm_phase(f"norm2_{l}", cols(l))
                ffn_phase(l)
                outproj_phase(f"res2_{l}", cols(l), [slot(ACT0 + j) for j in range(FT)], 3)
            norm_phase("final", CTX)

        @block.scalar
        def _(act):
            act.dma_start(const[:, :], const_in).then_inc(s_load, 16)
            act.dma_start(cvec[:, :], c_in).then_inc(s_load, 16)
            act.dma_start(slot(SCANMASK), scanmask_in).then_inc(s_load, 16)
            act.dma_start(arena[:, X0 * T:(X0 + KT) * T], x_in).then_inc(s_load, 16)
            act.dma_start(par[:, :], par_in[0, :, :]).then_inc(s_par, 16)
            act.wait_ge(s_load, 64)
            act.activation(sc[:, :], cvec[:, :], ACT.Silu).then_inc(*phases["cond"]["A"].mark("silu"))

            def rsqrt(A, turn, out_, in_, scale, bias, name_ln, name_exp):
                act.activation(out_, in_, ACT.Ln, bias=bias, scale=scale).then_inc(*A.mark(name_ln))
                act.wait_ge(*A.at(name_ln, turn))
                act.activation(out_, out_, ACT.Exp, scale=-0.5).then_inc(*A.mark(name_exp))

            def norm_phase(key, c0, which, affine=True):
                ph = enter(act, key, "A")
                A, V = ph["A"], ph["V"]
                for j in range(KT):
                    act.activation(slot(H0 + j, c0), slot(X0 + j, c0), ACT.Square).then_inc(*A.mark(f"sq{j}"))
                act.wait_ge(*ph["PE"].at("sum"))
                rsqrt(A, 0, slot(NT, c0), psum[:, 0, c0:T], 1.0 / D, eps_c(0), "ln", "rstd")
                if not affine:
                    return
                for j in range(KT):
                    act.wait_ge(*V.at(f"xn{j}"))
                    for s, a, b in segs(c0):
                        shift = mod[:, 2 * (24 * which + j) + s:2 * (24 * which + j) + s + 1]
                        gain = a_mod[:, 2 * (KT * which + j) + s:2 * (KT * which + j) + s + 1]
                        ins = act.activation(slot(H0 + j, a, b), slot(H0 + j, a, b), ACT.Identity, bias=shift, scale=gain)
                    ins.then_inc(*A.mark(f"h{j}"))

            def lora_phase(l):
                ph = enter(act, f"lora{l}", "A")
                A, V, PE = ph["A"], ph["V"], ph["PE"]
                act.dma_start(spill, arena[:, X0 * T:(X0 + KT) * T]).then_inc(s_spill, 16)
                for n, name in enumerate(["w", "a", "g"]):
                    act.wait_ge(*PE.at(name))
                    act.activation(slot(T0 + n), psum[:, n, 0:T], ACT.Copy).then_inc(*A.mark(f"raw{n}"))
                act.wait_ge(*V.at("s0c"))
                act.activation(slot(LW), slot(LW), ACT.Tanh).then_inc(*A.mark("act0"))
                act.wait_ge(*V.at("s2c"))
                act.wait_ge(s_spill, 16 * (l + 1))
                act.activation(slot(LG), slot(LG), ACT.Sigmoid).then_inc(*A.mark("act2"))

            def pair_phase(key, l):
                ph = enter(act, key, "A")
                A, V, PE, G = (ph.get(e) for e in ("A", "V", "PE", "G"))
                parts = ph["parts"]
                prep, scan = "prep" in parts, "scan" in parts
                _, wide = names_pair(parts)
                y0 = cols(l)

                def turn(i):
                    def ps(name, a=0, b=T):
                        return psum[:, wide.index(name) % 4, a:b]

                    def evac(name, dst, a=0, scale=1.0):
                        act.wait_ge(*PE.at(name, i))
                        act.activation(slot(dst, a), ps(name, a), ACT.Copy, scale=scale).then_inc(*A.mark(name))

                    def raw(x, dst):
                        act.wait_ge(*PE.at(f"z{x}", i))
                        act.activation(slot(dst), ps(f"z{x}"), ACT.Copy).then_inc(*A.mark(f"raw_{x}"))

                    if scan:
                        for d in DIRS:
                            m = M0_ + 11 * d
                            evac(f"kkT{d}", m + M_KKT)
                            evac(f"bT{d}", m + M_BET)
                            evac(f"kT{d}", m + M_KET)
                        evac("vT", VT)
                        act.wait_ge(*PE.at("gu", i))
                        wait_steps(act, i, (G, "yst", 1))
                        act.activation(slot(GZ, y0), ps("gu", y0), ACT.Copy).then_inc(*A.mark("gz"))
                        for d in DIRS:
                            act.wait_ge(*V.at(f"X1a{d}", i))
                            evac(f"A{d}", M0_ + 11 * d + M_A)
                        for d in DIRS:
                            evac(f"BV{d}", M0_ + 11 * d + M_BV)
                    if prep:
                        raw("r", T0)
                        raw("k", T1)
                        act.wait_ge(*G.at("pp", i))
                        for d in DIRS:
                            f = F0 + 6 * d
                            act.wait_ge(*PE.at(f"lw{d}", i))
                            act.activation(slot(f + F_BE), ps(f"lw{d}"), ACT.Sigmoid, bias=ppn(f"w0{d}")).then_inc(*A.mark(f"sw{d}"))
                            act.wait_ge(*PE.at(f"la{d}", i))
                            act.activation(slot(f + F_KE), ps(f"la{d}"), ACT.Sigmoid, bias=ppn(f"a0{d}")).then_inc(*A.mark(f"sa{d}"))
                        act.wait_ge(*V.at("kk0", i))
                        act.activation(slot(T0), slot(KK_), ACT.Square).then_inc(*A.mark("kksq"))
                        act.wait_ge(*V.at("kkm", i))
                        act.activation(slot(T1), slot(T1), ACT.Ln, scale=float(2 ** LN_SHIFT)).then_inc(*A.mark("kkl"))
                        act.wait_ge(*A.at("kkl", i))
                        act.activation(slot(T1), slot(T1), ACT.Exp, scale=-0.5, bias=eps_c(3)).then_inc(*A.mark("kke"))
                        for d in DIRS:
                            f, le, ei = F0 + 6 * d, (LE0, LE1)[d], (EI0, EI1)[d]
                            act.wait_ge(*V.at(f"L{d}", i))
                            act.wait_ge(*G.at("Le0" if d == 0 else "Li1", i))
                            act.activation(slot(ei), slot(le), ACT.Exp, scale=-KAPPA).then_inc(*A.mark(f"Ei{d}"))
                            act.activation(slot(le), slot(le), ACT.Exp, scale=KAPPA).then_inc(*A.mark(f"En{d}"))
                            act.activation(slot(f + F_KK), slot(f + F_KK), ACT.Exp, scale=-KAPPA).then_inc(*A.mark(f"Ee{d}"))
                    if scan:
                        for d in DIRS:
                            evac(f"U0{d}", M0_ + 11 * d + M_U0, scale=-1.0)
                            evac(f"G{d}", M0_ + 11 * d + M_G, scale=-1.0)
                        for d in DIRS:
                            evac(f"N{d}", M0_ + 11 * d + M_N)
                        act.wait_ge(*PE.at("Y", i))
                        act.activation(slot(PT0, y0), ps("Y", y0), ACT.Copy).then_inc(*A.mark("y"))
                    if prep:
                        raw("v", T2)
                    if scan:
                        act.wait_ge(*V.at("yc", i))
                        act.activation(slot(PT1, y0), slot(PT0, y0), ACT.Square).then_inc(*A.mark("ysq"))
                        act.wait_ge(*PE.at("var", i))
                        rsqrt(A, i, slot(PT1, y0), ps("var", y0), 1.0 / HD, eps_c(2), "yln", "yrs")
                        act.wait_ge(*V.at("ynr", i))
                        act.wait_ge(*G.at("ppc", i))
                        act.activation(slot(PT0, y0), slot(PT0, y0), ACT.Identity, bias=ppc("gnb"), scale=ppc("gng")).then_inc(*A.mark("yn"))
                each(act, ph, turn)

            def branch_phase(l):
                ph = enter(act, f"branch{l}", "A")
                A, V, PE = ph["A"], ph["V"], ph["PE"]
                c0 = cols(l)
                n = T - c0
                act.dma_start(arena[:, YA0 * T:(YA0 + KT) * T], ya_spill).then_inc(s_back, 16)
                act.dma_start(arena[:, X0 * T:(X0 + KT) * T], spill).then_inc(s_back, 16)
                act.dma_start(sgu_w, sgu_w_in[l, :, :]).then_inc(s_sgu, 16)
                act.dma_start(sgu_b, sgu_b_in[l, :, :]).then_inc(s_sgu, 16)
                for j in range(CT):
                    act.wait_ge(*PE.at(f"cb{j}"))
                    if j >= 2:
                        act.wait_ge(*V.at(f"u{j - 2}"))
                    act.activation(slot(G0 + j % 2, c0), psum[:, (2 * j) % 4, 0:n], ACT.Sigmoid).then_inc(*A.mark(f"cb{j}"))
                for name, dst in (("su", SU), ("sv", SV)):
                    for j in range(CT):
                        act.wait_ge(*PE.at(f"{name}{j}"))
                        act.activation(slot(dst + j, c0), psum[:, j, 0:n], ACT.Gelu_apprx_tanh).then_inc(*A.mark(f"{name}{j}"))
                for j in range(CT):
                    act.wait_ge(*V.at(f"cc{j}"))
                    act.activation(slot(CU + j, c0), slot(CY + j, c0), ACT.Square).then_inc(*A.mark(f"csq{j}"))
                for j in range(CT):
                    act.wait_ge(*V.at(f"sc{j}"))
                    act.activation(slot(H1 + j, c0), slot(SV + j, c0), ACT.Square).then_inc(*A.mark(f"ssq{j}"))
                for x, tile, dst in (("c", 1, G0), ("s", 3, G0 + 1)):
                    act.wait_ge(*PE.at(f"{x}var"))
                    rsqrt(A, 0, slot(dst, c0), psum[:, tile, 0:n], 1.0 / CONV, eps_c(1), f"{x}ln", f"{x}r")
                for j in range(CT):
                    act.wait_ge(*V.at(f"cn{j}"))
                    act.activation(slot(CY + j, c0), slot(CY + j, c0), ACT.Silu, bias=par_c("clb", j), scale=par_c("clg", j)).then_inc(*A.mark(f"cs{j}"))
                for j in range(CT):
                    act.wait_ge(*V.at(f"sm{j}"))
                    act.activation(slot(SV + j, c0), slot(SV + j, c0), ACT.Identity, bias=par_c("slb", j), scale=par_c("slg", j)).then_inc(*A.mark(f"sn{j}"))
                for j in range(CT):
                    act.wait_ge(*PE.at(f"tr{j}"))
                    act.activation(slot(VTK + j, 0, n), psum[:, j, 0:n], ACT.Copy).then_inc(*A.mark(f"tr{j}"))

            def merge_phase(l):
                ph = enter(act, f"merge{l}", "A")
                A, V, PE = ph["A"], ph["V"], ph["PE"]
                c0 = cols(l)
                n = T - c0
                order_g = [(b, q) for q in range(MERGE_TILES) for b in range(3)]

                def turn(i):
                    for k, (b, q) in enumerate(order_g):
                        act.wait_ge(*PE.at(f"g{b}{q}", i))
                        if k >= 3:
                            act.wait_ge(*V.at("p%d%d" % order_g[k - 3], i))
                        else:
                            act.wait_ge(*V.at("p%d%d" % order_g[k - 3], i, back=1))
                        act.activation(slot(G0 + k % 3, c0), psum[:, (2 * k) % 4, 0:n], ACT.Sigmoid).then_inc(*A.mark(f"g{b}{q}"))
                each(act, ph, turn)

            def ffn_phase(l):
                ph = enter(act, f"ffn{l}", "A")
                A, V, PE = ph["A"], ph["V"], ph["PE"]
                c0 = cols(l)
                n = T - c0

                def turn(i):
                    for q in range(2):
                        act.wait_ge(*PE.at(f"g{q}", i))
                        act.wait_ge(*V.at(f"a{q}", i, back=1))
                        act.activation(slot(YA0 + q, c0), psum[:, 2 * q, 0:n], ACT.Silu).then_inc(*A.mark(f"s{q}"))
                each(act, ph, turn)

            for l in range(DEPTH):
                if l:
                    act.wait_ge(*phases[f"res2_{l - 1}"]["V"].end())
                    act.wait_ge(*phases[f"res2_{l - 1}"]["PE"].end())
                    act.dma_start(par[:, :], par_in[l, :, :]).then_inc(s_par, 16)
                norm_phase(f"norm1_{l}", 0, 0)
                lora_phase(l)
                for name, _, _ in PAIR_PHASES:
                    pair_phase(f"{name}{l}", l)
                branch_phase(l)
                merge_phase(l)
                norm_phase(f"norm2_{l}", cols(l), 1)
                ffn_phase(l)
            norm_phase("final", CTX, 0, affine=False)
            act.wait_ge(*phases["final"]["V"].end())
            act.dma_start(out, arena[:, H0 * T:(H0 + KT) * T].rearrange("p (j t) -> p j t", t=T)[:, :, CTX:T]).then_inc(s_out, 16)
            act.wait_ge(s_out, 16)

        @block.vector
        def _(dve):
            def modv_phase(l):
                ph = enter(dve, f"modv{l}", "V")
                V = ph["V"]
                dve.wait_ge(s_par, 16 * (l + 1))
                dve.tensor_tensor(mod[:, :].rearrange("p (j s) -> p j s", s=2),
                                  psum[:, 0, 0:96].rearrange("p (j s) -> p j s", s=2),
                                  par[:, PAR["b_mod"]:PAR["b_mod"] + 48, None].to_broadcast([P, 48, 2]),
                                  ALU.add).then_inc(*V.mark("mod"))
                dve.wait_ge(*V.at("mod"))
                for which, g, name in ((0, "n1g", "a1"), (1, "n2g", "a2")):
                    o = 2 * (24 * which + KT)
                    dve.scalar_tensor_tensor(
                        out=a_mod[:, 2 * KT * which:2 * KT * (which + 1)].rearrange("p (j s) -> p j s", s=2),
                        in0=mod[:, o:o + 2 * KT].rearrange("p (j s) -> p j s", s=2), scalar=1.0,
                        in1=par[:, PAR[g]:PAR[g] + KT, None].to_broadcast([P, KT, 2]),
                        op0=ALU.add, op1=ALU.mult).then_inc(*V.mark(name))

            def norm_phase(key, c0, final=False):
                ph = enter(dve, key, "V")
                V, A = ph["V"], ph["A"]
                dve.wait_ge(*A.at("rstd"))
                for j in range(KT):
                    dve.tensor_tensor(slot(H0 + j, c0), slot(X0 + j, c0), slot(NT, c0), ALU.mult).then_inc(*V.mark(f"xn{j}"))
                if final:
                    for j in range(KT):
                        dve.wait_ge(*V.at(f"xn{j}"))
                        dve.tensor_scalar(slot(H0 + j, c0), slot(H0 + j, c0), par_c("fin", j), None, ALU.mult).then_inc(*V.mark(f"y{j}"))

            def shift(V, i, raw, dst, w0, w1, w2, n0, n1, n2):
                dve.tensor_scalar(slot(dst), slot(raw), w1, None, ALU.mult).then_inc(*V.mark(n0))
                dve.wait_ge(*V.at(n0, i))
                for a, b in ((0, CTX), (CTX, T)):
                    ins = dve.scalar_tensor_tensor(out=slot(dst, a + 1, b), in0=slot(raw, a, b - 1), scalar=w0,
                                                   in1=slot(dst, a + 1, b), op0=ALU.mult, op1=ALU.add)
                ins.then_inc(*V.mark(n1))
                dve.wait_ge(*V.at(n1, i))
                for a, b in ((0, CTX), (CTX, T)):
                    ins = dve.scalar_tensor_tensor(out=slot(dst, a, b - 1), in0=slot(raw, a + 1, b), scalar=w2,
                                                   in1=slot(dst, a, b - 1), op0=ALU.mult, op1=ALU.add)
                ins.then_inc(*V.mark(n2))

            def lora_phase(l):
                ph = enter(dve, f"lora{l}", "V")
                A, V = ph["A"], ph["V"]
                for n in range(3):
                    dve.wait_ge(*A.at(f"raw{n}"))
                    shift(V, 0, T0 + n, LW + n, *[par_c("shift", 3 * n + t) for t in range(3)],
                          *[f"s{n}{x}" for x in "abc"])

            def pair_phase(key, l):
                ph = enter(dve, key, "V")
                A, V, PE, G = (ph.get(e) for e in ("A", "V", "PE", "G"))
                parts = ph["parts"]
                prep, scan = "prep" in parts, "scan" in parts
                _, wide = names_pair(parts)
                y0 = cols(l)
                ny = (T - y0) // C

                def turn(i):
                    def ps(name, a=0, b=T):
                        return psum[:, wide.index(name) % 4, a:b]

                    def mul(name, out_, a, b):
                        dve.tensor_tensor(slot(out_), slot(a), slot(b), ALU.mult).then_inc(*V.mark(name))

                    def shifted(x, raw, dst):
                        dve.wait_ge(*A.at(f"raw_{x}", i))
                        shift(V, i, raw, dst, ppn(f"{x}0"), ppn(f"{x}1"), ppn(f"{x}2"), f"{x}a", f"{x}b", f"{x}c")

                    def masked(name, dst, m, d, a=0):
                        dve.wait_ge(*PE.at(name[:-1].replace("X1a", "A") + name[-1], i))
                        dve.tensor_tensor(by_chunk(slot(dst, a)), by_chunk(ps(name.replace("X1a", "A"), a)),
                                          mask(m, d, (T - a) // C), ALU.mult).then_inc(*V.mark(name))

                    def level(n):
                        for d in DIRS:
                            masked(f"T{n}{d}", M0_ + 11 * d + M_T, f"lv{n}", d)
                        for d in DIRS:
                            m = M0_ + 11 * d
                            dve.wait_ge(*PE.at(f"U{n}{d}", i))
                            dve.tensor_tensor(slot(m + M_XT), slot(m + M_XT), ps(f"U{n}{d}"), ALU.subtract).then_inc(*V.mark(f"XT{n}{d}"))
                            if n < 5:
                                dve.wait_ge(*V.at(f"XT{n}{d}", i))
                                dve.transpose(slot(m + M_X), slot(m + M_XT)).then_inc(*V.mark(f"Xt{n}{d}"))

                    if scan:
                        dve.scalar_tensor_tensor(out=slot(BN, y0), in0=slot(R_, y0), scalar=ppn("rk"), in1=slot(K_, y0),
                                                 op0=ALU.mult, op1=ALU.mult).then_inc(*V.mark("bon"))
                        dve.wait_ge(*PE.at("bonus", i))
                        dve.tensor_tensor(slot(BN, y0), slot(V_, y0), ps("bonus", y0), ALU.mult).then_inc(*V.mark("bv"))
                        for d in DIRS:
                            m = M0_ + 11 * d
                            masked(f"X1a{d}", m + M_XT, "first", d)
                            dve.wait_ge(*V.at(f"X1a{d}", i))
                            dve.tensor_tensor(by_chunk(slot(m + M_XT)), by_chunk(slot(m + M_XT)), const_b(C_ID64, C), ALU.add).then_inc(*V.mark(f"X1b{d}"))
                            dve.wait_ge(*V.at(f"X1b{d}", i))
                            dve.transpose(slot(m + M_X), slot(m + M_XT)).then_inc(*V.mark(f"X{d}"))
                            masked(f"B{d}", m + M_BT, "strict", d)
                            masked(f"RB{d}", m + M_RB, "incl", d, y0)
                            masked(f"RK{d}", m + M_RK, "incl", d, y0)
                        level(1)
                    if prep:
                        dve.wait_ge(*G.at("pp", i))
                        shifted("r", T0, R_)
                    if scan:
                        level(2)
                    if prep:
                        shifted("k", T1, K_)
                        dve.wait_ge(*V.at("kc", i))
                        dve.tensor_scalar(slot(KK_), slot(K_), ppn("kk"), None, ALU.mult).then_inc(*V.mark("kk0"))
                    if scan:
                        level(3)
                    if prep:
                        for d in DIRS:
                            dve.wait_ge(*A.at(f"sw{d}", i))
                            dve.tensor_tensor_scan(slot((LE0, LE1)[d]), slot(SCANMASK), slot(F0 + 6 * d + F_BE), 0.0,
                                                   ALU.mult, ALU.add).then_inc(*V.mark(f"L{d}"))
                        dve.wait_ge(*PE.at("kkn", i))
                        dve.tensor_scalar(slot(T1), ps("kkn"), 1e-24, None, ALU.max).then_inc(*V.mark("kkm"))
                    if scan:
                        level(4)
                    if prep:
                        dve.wait_ge(*A.at("kke", i))
                        mul("kk", KK_, KK_, T1)
                    if scan:
                        level(5)
                    if prep:
                        dve.wait_ge(*V.at("kk", i))
                        for d in DIRS:
                            f, le = F0 + 6 * d, (LE0, LE1)[d]
                            mul(f"b{d}", f + F_B, KK_, f + F_KE)
                            dve.wait_ge(*A.at(f"Ee{d}", i))
                            mul(f"kkP{d}", f + F_KK, KK_, f + F_KK)
                            dve.wait_ge(*V.at(f"b{d}", i))
                            mul(f"bQ{d}", f + F_B, f + F_B, le)
                    if scan:
                        for d in DIRS:
                            m, f = M0_ + 11 * d, F0 + 6 * d
                            dve.wait_ge(*PE.at(f"MT{d}", i))
                            dve.wait_ge(*G.at(f"D{d}", i))
                            dve.tensor_tensor(slot(m + M_MT), slot(m + M_MT), ps(f"MT{d}"), ALU.add).then_inc(*V.mark(f"MT{d}"))
                            dve.wait_ge(*PE.at(f"Q{d}", i))
                            dve.tensor_tensor(slot(m + M_Q, y0), slot(f + F_R, y0), ps(f"Q{d}", y0), ALU.add).then_inc(*V.mark(f"Q{d}"))
                    if prep:
                        if scan:
                            dve.wait_ge(*V.at("Q1", i))
                        for d in DIRS:
                            mul(f"rP{d}", F0 + 6 * d + F_R, R_, (EI0, EI1)[d])
                    if scan:
                        for n in CHAIN:
                            for d in DIRS:
                                m, c, nxt = M0_ + 11 * d, seq(d)[n], seq(d)[n + 1]
                                dve.wait_ge(*PE.at(f"c{n}{d}", i))
                                if n == 1:
                                    dve.wait_ge(*A.at(f"N{d}", i))
                                dve.tensor_tensor(slot(m + M_S, nxt * C, nxt * C + C), slot(m + M_N, c * C, c * C + C),
                                                  psum[:, wide.index(f"chain{d}") % 4, c * C:c * C + C], ALU.add).then_inc(*V.mark(f"c{n}{d}"))
                        dve.wait_ge(*PE.at("mean", i))
                        dve.scalar_tensor_tensor(out=slot(PT0, y0), in0=ps("mean", y0), scalar=-1.0 / HD, in1=slot(PT0, y0),
                                                 op0=ALU.mult, op1=ALU.add).then_inc(*V.mark("yc"))
                    if prep:
                        shifted("v", T2, V_)
                    if scan:
                        dve.wait_ge(*A.at("yrs", i))
                        dve.tensor_tensor(slot(PT0, y0), slot(PT0, y0), slot(PT1, y0), ALU.mult).then_inc(*V.mark("ynr"))
                        dve.wait_ge(*A.at("yn", i))
                        dve.tensor_tensor(slot(PT0, y0), slot(PT0, y0), slot(BN, y0), ALU.add).then_inc(*V.mark("yb"))
                        dve.wait_ge(*V.at("yb", i))
                        dve.tensor_tensor(slot(GZ, y0), slot(PT0, y0), slot(GZ, y0), ALU.mult).then_inc(*V.mark("ya"))
                each(dve, ph, turn)

            def branch_phase(l):
                ph = enter(dve, f"branch{l}", "V")
                A, V, PE = ph["A"], ph["V"], ph["PE"]
                c0 = cols(l)
                n = T - c0
                taps = conv_taps(l)

                def grid(k, t, horizontal=True):
                    return slot(k, CTX).rearrange("p (r w) -> p r w", w=GRID_W)

                def tap(j, o, m):
                    w = par_c("dw", j * TAPS + 15 + o)
                    lo, hi = max(0, -o), max(0, o)
                    ins = None
                    if c0 == 0:
                        ins = dve.scalar_tensor_tensor(out=slot(CY + j, lo, CTX - hi), in0=slot(CU + j, lo + o, CTX - hi + o),
                                                       scalar=w, in1=slot(CY + j, lo, CTX - hi), op0=ALU.mult, op1=ALU.add)
                    if l % 2 == 0:
                        y, u = grid(CY + j, 0), grid(CU + j, 0)
                        ins = dve.scalar_tensor_tensor(out=y[:, :, lo:GRID_W - hi], in0=u[:, :, lo + o:GRID_W - hi + o],
                                                       scalar=w, in1=y[:, :, lo:GRID_W - hi], op0=ALU.mult, op1=ALU.add)
                    else:
                        a, b, s = CTX + lo * GRID_W, T - hi * GRID_W, o * GRID_W
                        ins = dve.scalar_tensor_tensor(out=slot(CY + j, a, b), in0=slot(CU + j, a + s, b + s),
                                                       scalar=w, in1=slot(CY + j, a, b), op0=ALU.mult, op1=ALU.add)
                    return ins

                for j in range(CT):
                    dve.wait_ge(*A.at(f"cb{j}"))
                    dve.wait_ge(*PE.at(f"ca{j}"))
                    dve.tensor_tensor(slot(CU + j, c0), psum[:, (2 * j + 1) % 4, 0:n], slot(G0 + j % 2, c0), ALU.mult).then_inc(*V.mark(f"u{j}"))
                    dve.wait_ge(*V.at(f"u{j}"))
                    for m, o in enumerate(taps):
                        if m == 0:
                            dve.tensor_scalar(slot(CY + j, c0), slot(CU + j, c0), par_c("dw", j * TAPS + 15), par_c("dwb", j),
                                              ALU.mult, ALU.add).then_inc(*V.mark(f"y{j}_0"))
                        else:
                            dve.wait_ge(*V.at(f"y{j}_{m - 1}"))
                            tap(j, o, m).then_inc(*V.mark(f"y{j}_{m}"))
                for pre, mean, dst, tile in (("cc", "cmean", CY, 0), ("sc", "smean", SV, 2)):
                    dve.wait_ge(*PE.at(mean))
                    for j in range(CT):
                        dve.scalar_tensor_tensor(out=slot(dst + j, c0), in0=psum[:, tile, 0:n], scalar=-1.0 / CONV,
                                                 in1=slot(dst + j, c0), op0=ALU.mult, op1=ALU.add).then_inc(*V.mark(f"{pre}{j}"))
                for pre, r, dst, tmp in (("c", "cn", CY, G0), ("s", "sm", SV, G0 + 1)):
                    dve.wait_ge(*A.at(f"{pre}r"))
                    for j in range(CT):
                        dve.tensor_tensor(slot(dst + j, c0), slot(dst + j, c0), slot(tmp, c0), ALU.mult).then_inc(*V.mark(f"{r}{j}"))
                for j in range(CT):
                    dve.wait_ge(*PE.at(f"sp{j}"))
                    if j == 0:
                        dve.wait_ge(s_sgu, 32 * (l + 1))
                    dve.tensor_tensor(slot(H1 + j, 0, n).rearrange("p (c t) -> p c t", t=P),
                                      psum[:, j, 0:n].rearrange("p (c t) -> p c t", t=P),
                                      sgu_b[:, None, j * P:(j + 1) * P].to_broadcast([P, n // P, P]), ALU.add).then_inc(*V.mark(f"sp{j}"))
                    dve.wait_ge(*V.at(f"sp{j}"))
                    dve.tensor_tensor(slot(SU + j, c0), slot(SU + j, c0), slot(H1 + j, 0, n), ALU.mult).then_inc(*V.mark(f"uv{j}"))

            def merge_phase(l):
                ph = enter(dve, f"merge{l}", "V")
                A, V, PE, G = ph["A"], ph["V"], ph["PE"], ph["G"]
                c0 = cols(l)
                n = T - c0

                def turn(i):
                    k = 0
                    for q in range(MERGE_TILES):
                        for b in range(3):
                            dve.wait_ge(*PE.at(f"p{b}{q}", i))
                            dve.wait_ge(*A.at(f"g{b}{q}", i))
                            if b == 0:
                                dst = slot_at(M0, i, MERGE_TILES, q, c0)
                            else:
                                dst = slot(MTMP + b - 1, c0)
                                if q:
                                    dve.wait_ge(*G.at(f"m{b}{q - 1}", i))
                                else:
                                    dve.wait_ge(*G.at(f"m{b}{MERGE_TILES - 1}", i, back=1))
                            dve.tensor_tensor(dst, psum[:, (2 * k + 1) % 4, 0:n], slot(G0 + k % 3, c0), ALU.mult).then_inc(*V.mark(f"p{b}{q}"))
                            k += 1
                each(dve, ph, turn)

            def outproj_phase(key, c0, gate):
                ph = enter(dve, key, "V")
                V, PE = ph["V"], ph["PE"]

                def turn(i):
                    for q in range(4):
                        dve.wait_ge(*PE.at(f"o{q}", i))
                        for s, a, b in segs(c0):
                            x = slot_at(X0, i, 4, q, a, b)
                            ins = dve.scalar_tensor_tensor(out=x, in0=psum[:, q, a - c0:b - c0],
                                                           scalar=mod[:, bass.ds(i * 8 + (2 * (gate * KT + q) + s), 1)],
                                                           in1=x, op0=ALU.mult, op1=ALU.add)
                        ins.then_inc(*V.mark(f"x{q}"))
                each(dve, ph, turn)

            def ffn_phase(l):
                ph = enter(dve, f"ffn{l}", "V")
                A, V, PE = ph["A"], ph["V"], ph["PE"]
                c0 = cols(l)
                n = T - c0

                def turn(i):
                    for q in range(2):
                        dve.wait_ge(*PE.at(f"u{q}", i))
                        dve.wait_ge(*A.at(f"s{q}", i))
                        dve.tensor_tensor(slot_at(ACT0, i, 2, q, c0), psum[:, 2 * q + 1, 0:n], slot(YA0 + q, c0), ALU.mult).then_inc(*V.mark(f"a{q}"))
                each(dve, ph, turn)

            dve.wait_ge(s_load, 64)
            for l in range(DEPTH):
                modv_phase(l)
                norm_phase(f"norm1_{l}", 0)
                lora_phase(l)
                for name, _, _ in PAIR_PHASES:
                    pair_phase(f"{name}{l}", l)
                branch_phase(l)
                merge_phase(l)
                dve.wait_ge(s_back, 32 * (l + 1))
                outproj_phase(f"res1_{l}", cols(l), 2)
                norm_phase(f"norm2_{l}", cols(l))
                ffn_phase(l)
                outproj_phase(f"res2_{l}", cols(l), 5)
            norm_phase("final", CTX, final=True)

        @block.gpsimd
        def _(pool):
            def pair_phase(key, l):
                ph = enter(pool, key, "G")
                A, V, PE, G = (ph.get(e) for e in ("A", "V", "PE", "G"))
                parts = ph["parts"]
                prep, scan = "prep" in parts, "scan" in parts
                y0 = cols(l)

                def turn(i):
                    def tt(name, out_, a, b, op):
                        settle(pool)
                        pool.tensor_tensor(out_, a, b, op).then_inc(*G.mark(name))

                    if scan:
                        wait_steps(pool, i, (A, "yn", 1))
                        settle(pool)
                        pool.tensor_copy(pp[:, 0:NPP], pp[:, NPP + 1:2 * NPP + 1]).then_inc(*G.mark("ppc"))
                    if prep:
                        if scan:
                            pool.wait_ge(*V.at("bon", i))
                            pool.wait_ge(*G.at("ppc", i))
                        arrived(pool, key, i, 2)
                        settle(pool)
                        pool.tensor_copy(pp[:, NPP + 1:2 * NPP + 1], ring[:, 2 * BW + 3 * P:2 * BW + 3 * P + NPP]).then_inc(*G.mark("pp"))
                        pool.wait_ge(*G.at("pp", i))
                        settle(pool)
                        pool.tensor_scalar(pp[:, NPP:NPP + 1], ppn("ka"), -1.0, 1.0, ALU.mult, ALU.add).then_inc(*G.mark("omk"))
                        pool.wait_ge(*V.at("L0", i))
                        tt("Le0", slot(F0 + F_KK), slot(LE0), slot(F0 + F_BE), ALU.subtract)
                        pool.wait_ge(*V.at("L1", i))
                        f = F0 + 6
                        total = by_chunk(slot(LE1))[:, :, C - 1:C].to_broadcast([P, NCH, C])
                        tt("Le1", by_chunk(slot(f + F_KK)), total, by_chunk(slot(LE1)), ALU.subtract)
                        pool.wait_ge(*G.at("Le1", i))
                        tt("Li1", slot(LE1), slot(f + F_KK), slot(f + F_BE), ALU.add)
                        for d in DIRS:
                            f = F0 + 6 * d
                            pool.wait_ge(*A.at(f"sa{d}", i))
                            settle(pool)
                            pool.tensor_scalar(slot(f + F_K), slot(f + F_KE), ppn("ka"), pp[:, NPP:NPP + 1], ALU.mult, ALU.add).then_inc(*G.mark(f"kt{d}"))
                            pool.wait_ge(*G.at(f"kt{d}", i))
                            pool.wait_ge(*V.at("kc", i))
                            tt(f"kd{d}", slot(f + F_K), slot(f + F_K), slot(K_), ALU.mult)
                    if scan:
                        for d in DIRS:
                            pool.wait_ge(*PE.at(f"U5{d}", i))
                            tt(f"D{d}", by_chunk(slot(M0_ + 11 * d + M_MT)), const_b(C_ID64, C),
                               decays[:, d * NCH:(d + 1) * NCH, None].to_broadcast([P, NCH, C]), ALU.mult)
                    if prep:
                        for d in DIRS:
                            f, le, ei = F0 + 6 * d, (LE0, LE1)[d], (EI0, EI1)[d]
                            pool.wait_ge(*G.at(f"kd{d}", i))
                            pool.wait_ge(*A.at(f"Ee{d}", i))
                            tt(f"kQ{d}", slot(f + F_K), slot(f + F_K), slot(le), ALU.mult)
                            end = C - 1 if d == 0 else 0
                            decay = by_chunk(slot(ei))[:, :, end:end + 1].to_broadcast([P, NCH, C])
                            pool.wait_ge(*V.at(f"bQ{d}", i))
                            tt(f"bE{d}", by_chunk(slot(f + F_BE)), by_chunk(slot(f + F_B)), decay, ALU.mult)
                            pool.wait_ge(*G.at(f"kQ{d}", i))
                            tt(f"kE{d}", by_chunk(slot(f + F_KE)), by_chunk(slot(f + F_K)), decay, ALU.mult)
                        for d in DIRS:
                            end = C - 1 if d == 0 else 0
                            if scan:
                                pool.wait_ge(*G.at(f"D{d}", i))
                            settle(pool)
                            pool.tensor_copy(decays[:, d * NCH:(d + 1) * NCH, None],
                                             by_chunk(slot((EI0, EI1)[d]))[:, :, end:end + 1]).then_inc(*G.mark(f"pc{d}"))
                    if scan:
                        pool.wait_ge(*V.at("ya", i))
                        settle(pool)
                        first = KT - 1 if key.startswith("last") else i
                        pool.dma_start(ya_v[:, bass.ds(first, 1), y0:T],
                                       arena[:, None, GZ * T + y0:GZ * T + T]).then_inc(s_ya, 16)
                        pool.wait_ge(s_ya, 16 * (first + (1 + KT * l)))
                        pool.wait_ge(*G.at("pc1" if prep else "D1", i))
                        pool.sem_inc(*G.mark("yst"))
                each(pool, ph, turn)

            def merge_phase(l):
                ph = enter(pool, f"merge{l}", "G")
                V, G = ph["V"], ph["G"]
                c0 = cols(l)

                def turn(i):
                    for q in range(MERGE_TILES):
                        m = slot_at(M0, i, MERGE_TILES, q, c0)
                        for b in (1, 2):
                            pool.wait_ge(*V.at(f"p{b}{q}", i))
                            if b == 2:
                                pool.wait_ge(*G.at(f"m1{q}", i))
                            settle(pool)
                            pool.tensor_tensor(m, m, slot(MTMP + b - 1, c0), ALU.add).then_inc(*G.mark(f"m{b}{q}"))
                each(pool, ph, turn)

            for l in range(DEPTH):
                for name, _, _ in PAIR_PHASES:
                    pair_phase(f"{name}{l}", l)
                merge_phase(l)


def seq(d):
    ctx, lat = list(range(CTX_CH)), list(range(CTX_CH, NCH))
    return ctx + lat if d == 0 else ctx[::-1] + lat[::-1]


def blocks(w):
    return w.reshape(-1, P, P).transpose(1, 0, 2).reshape(P, -1)


def tiled(v):
    return v.reshape(-1, P).T


def weight_stream(x):
    out = []

    def put(w):
        if w.shape[1] < BW:
            w = np.concatenate([w, np.zeros((P, BW - w.shape[1]), np.float32)], 1)
        out.append(w)

    def tile(w, col):
        return blocks(w[:, col:col + P])

    for l in range(DEPTH):
        w_in, up = x["w_in"][l], x["ffn_w_in"][l]
        for j in range(48):
            put(tile(x["w_mod"][l], j * P))
        for off in (OFF_W, OFF_A, OFF_G):
            put(tile(w_in, off))
        put(np.zeros((P, BW), np.float32))
        for p in range(KT):
            s = slice(p * P, p * P + P)
            put(tile(w_in, p * P))
            put(tile(w_in, OFF_K + p * P))
            taps = [x["rwkv_shift"][l][t, off + p * P:off + p * P + P] for off in (0, OFF_K, OFF_V) for t in range(3)]
            vec = taps + [x["rwkv_w0"][l][0, s], x["rwkv_w0"][l][1, s], x["rwkv_a0"][l][0, s], x["rwkv_a0"][l][1, s],
                          x["rwkv_k_k"][l][s], x["rwkv_k_a"][l][s], x["rwkv_r_k"][l][s], x["rwkv_gn_g"][l][s],
                          x["rwkv_gn_b"][l][s]]
            put(np.concatenate([x["rwkv_w_up"][l].reshape(P, RD)[:, s], x["rwkv_a_up"][l].reshape(P, RD)[:, s],
                                x["rwkv_g_up"][l][:, s], np.stack(vec, 1)], 1))
            put(tile(w_in, OFF_V + p * P))
        for j in range(CT):
            put(tile(w_in, OFF_CONV + CONV + j * P))
            put(tile(w_in, OFF_CONV + j * P))
        for j in range(2 * CT):
            put(tile(w_in, OFF_SGU + j * P))
        for j in range(KT):
            put(tile(w_in, OFF_GATE + j * P))
            put(tile(x["rwkv_out"][l], j * P))
            put(tile(w_in, OFF_GATE + D + j * P))
            put(tile(w_in, OFF_GATE + 2 * D + j * P))
            put(np.concatenate([tile(x["conv_out"][l], j * P), tile(x["sgu_out"][l], j * P)], 1))
        for j in range(KT):
            put(tile(x["w_merge"][l], j * P))
        for j in range(FT):
            put(tile(up, j * P))
            put(tile(up, DFF + j * P))
        for j in range(KT):
            w = np.concatenate([tile(x["ffn_w_out"][l], j * P), np.zeros((P, 3 * BW - FT * P), np.float32)], 1)
            for n in range(3):
                put(w[:, n * BW:(n + 1) * BW])
    return np.concatenate(out, 0)


def parameters(x, l):
    cols = [tiled(x["b_mod"][l]), tiled(x["norm1_g"][l]), tiled(x["norm2_g"][l])]
    cols.append(np.stack([x["rwkv_shift"][l][t, off:off + P] for off in (OFF_W, OFF_A, OFF_G) for t in range(3)], 1))
    cols.append(x["conv_dw"][l].reshape(TAPS, CT, P).transpose(2, 1, 0).reshape(P, CT * TAPS))
    cols += [tiled(x[n][l]) for n in ("conv_dw_b", "conv_ln_g", "conv_ln_b", "sgu_ln_g", "sgu_ln_b")]
    cols.append(tiled(x["final_norm_g"]))
    return np.concatenate(cols, 1)


def constants():
    out = np.zeros((P, NCONST), np.float32)
    r = np.arange(P)
    out[r, C_ID64 + r % C] = 1
    out[r, C_ID + r] = 1
    out[:, C_ONES:C_ONES + P] = 1
    out[:, C_EPS:C_EPS + len(EPS)] = EPS
    out[:, C_HEADS:C_HEADS + P] = (r[:, None] // HD == r[None, :] // HD)
    a, b = r[:, None] % C, np.arange(C)[None, :]
    for d in DIRS:
        after = (b > a) if d == 0 else (b < a)
        for n, name in enumerate(MASKS):
            if name == "strict":
                m = 1.0 * after
            elif name == "incl":
                m = 1.0 * (after | (a == b))
            elif name == "first":
                m = -1.0 * (after & (a // 2 == b // 2))
            else:
                w = 2 ** int(name[2:])
                same = a // (2 * w) == b // (2 * w)
                up, lo = a % (2 * w) >= w, b % (2 * w) < w
                m = 1.0 * (same & ((up & lo) if d == 0 else (~up & ~lo)))
            out[:, C_MASK + (d * len(MASKS) + n) * C:C_MASK + (d * len(MASKS) + n + 1) * C] = m
    mask = np.ones((P, T), np.float32)
    mask[:, ::C] = 0
    return out, mask


def kernel(**inputs):
    import concourse.bacc as _bacc
    from concourse.bass_utils import run_bass_kernel_spmd as _run

    x = {k: np.asarray(v) for k, v in inputs.items()}
    const, scanmask = constants()
    tokens = np.concatenate([x["ctx"][0], x["x"][0]], 0)
    arrays = {
        "x": tokens.reshape(T, KT, P).transpose(2, 1, 0).reshape(P, KT * T),
        "c": np.stack([x["c_ctx"], x["c"][0]], 1).reshape(KT, P, 2).transpose(1, 0, 2).reshape(P, 2 * KT),
        "w_stream": weight_stream(x),
        "par": np.stack([parameters(x, l) for l in range(DEPTH)]),
        "const": const,
        "scanmask": scanmask,
        "sgu_w": x["sgu_w"].transpose(0, 3, 1, 2).reshape(DEPTH, P, GROUPS * P),
        "sgu_b": np.repeat(x["sgu_b"].reshape(DEPTH, CT, 2, P), HD, axis=2).transpose(0, 2, 1, 3).reshape(DEPTH, P, CT * P),
    }
    arrays = {f"{k}_in": np.ascontiguousarray(v) for k, v in arrays.items()}
    nc = _bacc.Bacc("TRN2", target_bir_lowering=False, num_devices=1)
    args = [nc.dram_tensor(k, v.shape, F32, kind="ExternalInput").ap() for k, v in arrays.items()]
    out = nc.dram_tensor("out", (P, KT, LAT), F32, kind="ExternalOutput").ap()
    build(nc, *args, out)
    r = _run(nc, [arrays], core_ids=[0])
    y = r.results[0]["out"]
    return y.transpose(2, 1, 0).reshape(1, LAT, D)
```

```python
from contextlib import ExitStack

import numpy as np

import concourse.bass as bass
from concourse import mybir

ALU = mybir.AluOpType
ACT = mybir.ActivationFunctionType
F32 = mybir.dt.float32

P = 128
D = 1024
DEPTH = 2
CTX = 256
LAT = 512
T = CTX + LAT
GRID_W = 64
KT = D // P
HD = 64
C = 64
NCH = T // C
CTX_CH = CTX // C
RD = D
CONV = D // 2
SGU = D // 2
CT = CONV // P
TAPS = 31
DFF = ((8 * D // 3 + 255) // 256) * 256
FT = DFF // P
OFF_K, OFF_V, OFF_W = RD, 2 * RD, 3 * RD
OFF_A, OFF_G = OFF_W + 128, OFF_W + 256
OFF_CONV = OFF_G + 128
OFF_SGU = OFF_CONV + 2 * CONV
OFF_GATE = OFF_SGU + 2 * SGU
P_IN = OFF_GATE + 3 * D
GROUPS = 8
KAPPA = float(np.exp(-0.5))
BW = 8 * P

C_ID64, C_ID, C_ONES, C_HEADS, C_EPS, C_MASK = 0, 64, 192, 320, 448, 452
LN_SHIFT = 24
EPS = (1e-6, 1e-5, 64e-5, 0.5 * LN_SHIFT * float(np.log(2.0)))
MASKS = ["strict", "incl"]
H = C // 2
MASKS_H = ["first"] + [f"lv{n}" for n in range(1, 5)]
C_MASK_H = C_MASK + 2 * len(MASKS) * C
C_ID_H = C_MASK_H + 2 * len(MASKS_H) * H
NCONST = C_ID_H + H

PAR = {}
_at = 0
for _name, _n in (("b_mod", 48), ("n1g", 8), ("n2g", 8), ("shift", 9), ("dw", CT * TAPS), ("dwb", CT),
                  ("clg", CT), ("clb", CT), ("slg", CT), ("slb", CT), ("fin", 8)):
    PAR[_name] = _at
    _at += _n
NPAR = _at

PP = {n: i for i, n in enumerate(
    ["r0", "r1", "r2", "k0", "k1", "k2", "v0", "v1", "v2", "w00", "w01", "a00", "a01",
     "kk", "ka", "rk", "gng", "gnb"])}
NPP = len(PP)

MOD_TURNS = 6 * D // (4 * 512)
H0, LW, LA, LG = 0, 8, 9, 10
SCANMASK = 11
F0 = 12
F_R, F_KK, F_B, F_K, F_BE, F_KE = range(6)
M0_ = 24
M_A, M_BT, M_RB, M_RK, M_BET, M_KET, M_KKT, M_XT, M_X, M_T, M_BV = range(11)
M_U0, M_G, M_N, M_Q, M_MT, M_S = M_A, M_BT, M_KKT, M_X, M_T, M_BV
VT, R_, K_, V_, BN, GZ, T0, T1, T2, KK_ = range(46, 56)
LE0, EI0, LE1, EI1 = range(56, 60)
NSLOT = 61
PT0, PT1 = M0_ + M_XT, M0_ + 11 + M_XT
YA0 = 12
M0, X0 = 21, 29
CU, CY, SU, SV, VTK = 37, 41, 45, 49, 53
G0 = 57
NT = 60
COND, MODT = 0, 1
H1, SGW, SGB, MTMP = 21, 25, 27, 53
ACT0 = 37


class Steps:

    def __init__(self, sem, names, turns=1, lead=False):
        self.sem, self.names, self.turns, self.lead = sem, list(names), turns, lead
        self.index = {n: i for i, n in enumerate(self.names)}
        assert len(self.index) == len(self.names)
        self.k = 0

    def at(self, name, turn=0, back=0):
        return self.sem, turn * len(self.names) + (int(self.lead) - back) * len(self.names) + self.index[name] + 1

    def mark(self, name):
        assert self.names[self.k] == name, (self.names[self.k], name)
        self.k = (self.k + 1) % len(self.names)
        return self.sem, 1

    def end(self):
        return self.sem, (self.turns + int(self.lead)) * len(self.names)

    def credit(self, eng):
        if self.lead:
            eng.sem_inc(self.sem, len(self.names))


def names_norm():
    return dict(PE=["sum"], A=[f"sq{j}" for j in range(KT)] + ["ln", "rstd"] + [f"h{j}" for j in range(KT)],
                V=[f"xn{j}" for j in range(KT)], G=[])


def names_lora():
    return dict(PE=["w", "a", "g", "pad"],
                A=["raw0", "raw1", "raw2", "act0", "act2"],
                V=[f"s{n}{x}" for n in range(3) for x in "abc"], G=[])


DIRS = (0, 1)
CHAIN = range(1, NCH - 1)
BOTH = {"prep", "scan"}
PAIR_PHASES = (("first", {"prep"}, 1), ("pairs", BOTH, KT - 1), ("last", {"scan"}, 1))


def names_pair(parts):
    def pick(*groups):
        return [n for part, names in groups if part in parts for n in names]

    def both(*names):
        return [f"{n}{d}" for d in DIRS for n in names]

    def level(n, *names):
        return [f"{x}{n}{d}" for x in names for d in DIRS]

    pe = pick(
        ("scan", both("A", "B", "RB", "RK") + ["bonus", "gu", "BV0", "BV1"]),
        ("prep", ["zr"]), ("scan", level(1, "T", "U")),
        ("prep", ["zk"]), ("scan", level(2, "T", "U")),
        ("prep", both("lw", "la")), ("scan", level(3, "T", "U")),
        ("prep", ["kkn"]), ("scan", level(4, "T", "U") + level(5, "T", "U")),
        ("scan", both("U0", "G") + both("MT", "N", "Q") + [f"c{n}{d}" for n in CHAIN for d in DIRS] + ["Y"]),
        ("prep", ["zv"]), ("scan", ["mean", "var"]))
    wide = [n for n in pe if not (n[0] == "c")]
    if "scan" in parts:
        k = wide.index("Y")
        wide[k:k] = ["chain0", "chain1"]
    a = pick(
        ("scan", ["A0", "A1", "gz", "BV0", "BV1"]),
        ("prep", ["raw_r", "raw_k"] + both("sw", "sa") + ["kksq", "kkl", "kke"] + both("Ei", "En", "Ee")),
        ("scan", ["xd0", "xd1", "T50", "T51", "XT50", "XT51"] + both("U0", "G") + ["N0", "N1", "y"]),
        ("prep", ["raw_v"]), ("scan", ["ysq", "yln", "yrs", "yn"]))
    v = pick(
        ("scan", ["bon", "vT"] + both("X1a", "X1b", "X", "B", "RB", "RK", "zero") + ["bv", "bT0", "bT1"]
         + level(1, "T") + ["kT0"] + both("XT1", "Xt1") + ["kkT0"]),
        ("prep", ["ra", "rb", "rc"]), ("scan", level(2, "T") + ["kT1"] + both("XT2", "Xt2")),
        ("prep", ["ka", "kb", "kc", "kk0"]), ("scan", level(3, "T") + ["kkT1"] + both("XT3", "Xt3")),
        ("prep", ["L0", "L1", "kkm"]), ("scan", level(4, "T") + both("XT4", "Xt4")),
        ("prep", ["kk"] + both("b", "kkP", "bQ")), ("scan", both("MT", "Q")),
        ("prep", ["rP0", "rP1"]), ("scan", [f"c{n}{d}" for n in CHAIN for d in DIRS] + ["yc"]),
        ("prep", ["va", "vb", "vc"]), ("scan", ["ynr", "yb", "ya"]))
    g = pick(
        ("scan", ["ppc"]), ("prep", ["pp", "omk", "Le0", "Le1", "Li1"] + both("kt", "kd")),
        ("scan", ["D0", "D1"]), ("prep", both("kQ", "bE", "kE") + ["pc0", "pc1"]), ("scan", ["yst"]))
    return dict(PE=pe, A=a, V=v, G=g), wide


def names_branch(l):
    taps = conv_taps(l)
    pe = []
    for j in range(CT):
        pe += [f"cb{j}", f"ca{j}"]
    pe += [f"su{j}" for j in range(CT)] + [f"sv{j}" for j in range(CT)]
    pe += ["cmean", "cvar", "smean", "svar"] + [f"tr{j}" for j in range(CT)] + [f"sp{j}" for j in range(CT)]
    a = [f"cb{j}" for j in range(CT)] + [f"su{j}" for j in range(CT)] + [f"sv{j}" for j in range(CT)]
    a += [f"csq{j}" for j in range(CT)] + [f"ssq{j}" for j in range(CT)]
    a += ["cln", "cr", "sln", "sr"] + [f"cs{j}" for j in range(CT)]
    a += [f"sn{j}" for j in range(CT)] + [f"tr{j}" for j in range(CT)]
    v = []
    for j in range(CT):
        v += [f"u{j}"] + [f"y{j}_{n}" for n in range(len(taps))]
    v += [f"cc{j}" for j in range(CT)] + [f"sc{j}" for j in range(CT)]
    v += [f"cn{j}" for j in range(CT)] + [f"sm{j}" for j in range(CT)]
    for j in range(CT):
        v += [f"sp{j}", f"uv{j}"]
    return dict(PE=pe, A=a, V=v, G=[])


MERGE_TILES = 4


def names_merge():
    pe, a, v, g = [], [], [], []
    for q in range(MERGE_TILES):
        for b in range(3):
            pe += [f"g{b}{q}", f"p{b}{q}"]
            a += [f"g{b}{q}"]
            v += [f"p{b}{q}"]
            if b:
                g += [f"m{b}{q}"]
    return dict(PE=pe, A=a, V=v, G=g)


def names_outproj(per):
    return dict(PE=[f"o{q}{n}" for q in range(4) for n in range(per)], A=[], V=[f"x{q}" for q in range(4)], G=[])


def names_ffn():
    return dict(PE=["g0", "u0", "g1", "u1"], A=["s0", "s1"], V=["a0", "a1"], G=[])


def conv_taps(l):
    reach = 15 if l % 2 == 0 else (LAT // GRID_W) - 1
    return [0] + [o for n in range(1, reach + 1) for o in (-n, n)]


def build(nc, x_in, c_in, w_stream, par_in, const_in, scanmask_in, sgu_w_in, sgu_b_in, out):
    spill = nc.dram_tensor("x_spill", (P, KT * T), F32, kind="Internal").ap()
    ya_spill = nc.dram_tensor("ya_spill", (P, KT * T), F32, kind="Internal").ap()
    ya_v = ya_spill.rearrange("p (j t) -> p j t", t=T)
    with ExitStack() as st:
        def sem(name):
            return st.enter_context(nc.semaphore(name))

        arena = st.enter_context(nc.sbuf_tensor("arena", [P, NSLOT * T], F32))
        ring = st.enter_context(nc.sbuf_tensor("ring", [P, 4 * BW], F32))
        const = st.enter_context(nc.sbuf_tensor("const", [P, NCONST], F32))
        par = st.enter_context(nc.sbuf_tensor("par", [P, NPAR], F32))
        cvec = st.enter_context(nc.sbuf_tensor("cvec", [P, 2 * KT], F32))
        mod = st.enter_context(nc.sbuf_tensor("mod", [P, 48 * 2], F32))
        a_mod = st.enter_context(nc.sbuf_tensor("a_mod", [P, 2 * 2 * KT], F32))
        pp = st.enter_context(nc.sbuf_tensor("pp", [P, 2 * NPP + 1], F32))
        decays = st.enter_context(nc.sbuf_tensor("decays", [P, 2 * NCH], F32))
        psum = st.enter_context(nc.psum_tensor("psum", [P, 4, 1024], F32))

        w_in = [sem(f"weights_in_{i}") for i in range(4)]
        s_cond = sem("conditions_loaded")
        s_load = sem("inputs_loaded")
        s_settled = sem("settled")
        s_par = sem("params_loaded")
        s_spill = sem("x_spilled")
        s_back = sem("x_reloaded")
        s_ya = sem("scan_output_stored")
        s_sgu = sem("sgu_params_loaded")
        s_out = sem("output_stored")

        phases, at_end = {}, []

        def phase(key, names, turns=1, lead=False, chunks=()):
            ph = {e: Steps(sem(f"{key}_{e}"), ns, turns, lead) for e, ns in names.items() if ns}
            ph["chunks"], ph["turns"] = list(chunks), turns
            phases[key] = ph
            at_end.append((key, ph))
            return ph

        for l in range(DEPTH):
            phase(f"cond{l}", dict(PE=[], A=["silu"], V=["zero"], G=[]))
            steps = [f"m{q}" for q in range(2 * KT)]
            phase(f"mod{l}", dict(PE=steps, A=[], V=[], G=[]), MOD_TURNS, chunks=steps)
            phase(f"modt{l}", dict(PE=["t"], A=[f"e{n}" for n in range(MOD_TURNS)], V=[], G=[]))
            phase(f"modv{l}", dict(PE=[], A=[], V=["mod", "a1", "a2"], G=[]))
            phase(f"norm1_{l}", names_norm())
            phase(f"lora{l}", names_lora(), chunks=["w", "a", "g", "pad"])
            for name, parts, turns in PAIR_PHASES:
                phase(f"{name}{l}", names_pair(parts)[0], turns, lead=turns > 1,
                      chunks=["zr", "zk", None, "zv"] if "prep" in parts else [])
                phases[f"{name}{l}"]["parts"] = parts
            ch = []
            for j in range(CT):
                ch += [f"cb{j}", f"ca{j}"]
            phase(f"branch{l}", names_branch(l), chunks=ch + [f"su{j}" for j in range(CT)] + [f"sv{j}" for j in range(CT)])
            ch = []
            for q in range(MERGE_TILES):
                ch += [f"g0{q}", f"p0{q}", f"g1{q}", f"g2{q}", f"p2{q}"]
            phase(f"merge{l}", names_merge(), KT // MERGE_TILES, lead=True, chunks=ch)
            phase(f"res1_{l}", names_outproj(1), 2, lead=True, chunks=["o00", "o10", "o20", "o30"])
            phase(f"norm2_{l}", names_norm())
            phase(f"ffn{l}", names_ffn(), FT // 2, lead=True, chunks=["g0", "u0", "g1", "u1"])
            phase(f"res2_{l}", names_outproj(3), 2, lead=True,
                  chunks=[f"o{q}{n}" for q in range(4) for n in range(3)])
        phase("final", dict(PE=["sum"], A=[f"sq{j}" for j in range(KT)] + ["ln", "rstd"], V= [f"xn{j}" for j in range(KT)] + [f"y{j}" for j in range(KT)], G=[]))

        order = [k for k, _ in at_end]
        for key, ph in phases.items():
            assert len(ph["chunks"]) % 4 == 0
        chunk_base, n = {}, 0
        for key in order:
            chunk_base[key] = n
            n += len(phases[key]["chunks"]) * phases[key]["turns"]
        assert n * P == w_stream.shape[0]
        w_v = w_stream.rearrange("(n p) c -> p n c", p=P)

        def enter(eng, key, own):
            k = order.index(key)
            if k:
                prev = phases[order[k - 1]]
                for e in ("PE", "A", "V", "G"):
                    if e in prev:
                        eng.wait_ge(*prev[e].end())
            if own in phases[key]:
                phases[key][own].credit(eng)
            return phases[key]

        def settle(eng):
            eng.sem_inc(s_settled, 1)

        def wait_steps(eng, turn, *steps):
            latest = {}
            for E, name, back in steps:
                if back and not E.lead:
                    continue
                if E not in latest or (-back, E.index[name]) > latest[E]:
                    latest[E] = (-back, E.index[name])
            for E, (back, k) in latest.items():
                eng.wait_ge(*E.at(E.names[k], turn, back=-back))

        def each(eng, ph, body):
            if ph["turns"] == 1:
                body(0)
            else:
                with eng.Fori(0, ph["turns"]) as i:
                    body(i)

        def slot(n, a=0, b=T):
            return arena[:, n * T + a:n * T + b]

        def slot_at(n0, turn, per, q, a=0, b=T):
            return arena[:, bass.ds((turn * per + (n0 + q)) * T + a, b - a)]

        def by_chunk(ap, c0=0):
            return ap.rearrange("p (c t) -> p c t", t=C)

        def by_half(ap):
            return ap.rearrange("p (c t) -> p c t", t=H)

        def const_b(col, n, nch=NCH):
            return const[:, None, col:col + n].to_broadcast([P, nch, n])

        def mask(name, d, nch=NCH):
            return const_b(C_MASK + (d * len(MASKS) + MASKS.index(name)) * C, C, nch)

        def mask_h(name, d):
            return const_b(C_MASK_H + (d * len(MASKS_H) + MASKS_H.index(name)) * H, H)

        def diag(x, m):
            a = {"X": (m + M_X) * T, "XT": (m + M_X) * T + NCH * H, "T": (m + M_T) * T}[x]
            return arena[:, a:a + NCH * H]

        def quarter(ap, rows, col):
            return by_chunk(ap)[rows * H:rows * H + H, :, col * H:col * H + H]

        def par_c(name, k=0, n=1):
            return par[:, PAR[name] + k:PAR[name] + k + n]

        def ppc(name):
            return pp[:, PP[name]:PP[name] + 1]

        def ppn(name):
            return pp[:, NPP + 1 + PP[name]:NPP + 2 + PP[name]]

        def eps_c(n):
            return const[:, C_EPS + n:C_EPS + n + 1]

        ident = const[:, C_ID:C_ID + P]
        ones = const[:, C_ONES:C_ONES + P]
        heads = const[:, C_HEADS:C_HEADS + P]

        def cols(l):
            return 0 if l < DEPTH - 1 else CTX

        def segs(c0):
            return ([(0, 0, CTX)] if c0 == 0 else []) + [(1, CTX, T)]

        def halves(c0, off):
            cut = 512 + off
            return [(a, b) for a, b in ((c0, min(cut, T)), (max(cut, c0), T)) if a < b]

        def project(eng, tile, lhs, rhs, c0, off):
            mm = None
            for a, b in halves(c0, off):
                for k in range(len(lhs)):
                    mm = eng.matmul(psum[0:lhs[k].shape[-1], tile, a - off:b - off], lhsT=lhs[k], rhs=rhs[k][:, a:b],
                                    start=(k == 0), stop=(k == len(lhs) - 1))
            return mm

        def chunk_blocks(n, k0=0, nk=8):
            s = n % 4
            return [ring[:, s * BW + k * P:s * BW + (k + 1) * P] for k in range(k0, k0 + nk)]

        def arrived(eng, key, turn, q):
            base = chunk_base[key] // 4
            per = len(phases[key]["chunks"]) // 4
            eng.wait_ge(w_in[q % 4], 16 * (turn * per + (base + q // 4 + 1)))

        def load_chunk(eng, q, n):
            eng.dma_start(ring[:, None, (q % 4) * BW:(q % 4 + 1) * BW], w_v[:, n, :]).then_inc(w_in[q % 4], 16)

        def up_block(n):
            return ring[:, 2 * BW + n * P:2 * BW + (n + 1) * P]

        hs = [slot(H0 + j) for j in range(KT)]
        cond = arena[:, COND * T:COND * T + KT * 32].rearrange("p (k m) -> p k m", m=32)
        sgu_w = arena[:, SGW * T:SGW * T + GROUPS * P]
        sgu_b = arena[:, SGB * T:SGB * T + CT * P]
        block = st.enter_context(nc.Block())

        @block.sync
        def _(sp):
            last = {}

            def load(q, n):
                load_chunk(sp, q, n)

            for key in order:
                ph = phases[key]
                names, turns = ph["chunks"], ph["turns"]
                if not names:
                    continue
                nq, S = len(names), ph["PE"]
                mine = range(0, nq, 2) if key.startswith("mod") else range(nq)
                for q in mine:
                    if names[q] is None and key.startswith("pairs"):
                        sp.wait_ge(*S.at("gu", 0))
                    elif q % 4 in last:
                        sp.wait_ge(*last[q % 4])
                    load(q, slice(chunk_base[key] + q, chunk_base[key] + q + 1))
                    if names[q]:
                        last[q % 4] = S.at(names[q], 0)
                if turns > 1:
                    with sp.Fori(1, turns) as i:
                        for q in mine:
                            if names[q] is None:
                                sp.wait_ge(*S.at("gu", i))
                            elif q < 4:
                                sp.wait_ge(*S.at(names[nq - 4 + q], i, back=1))
                            else:
                                sp.wait_ge(*S.at(names[q - 4], i))
                            load(q, bass.ds(i * nq + (chunk_base[key] + q), 1))
                    for q in range(nq):
                        if names[q]:
                            last[q % 4] = S.at(names[q], turns - 1)
                        else:
                            last[q % 4] = phases["last" + key[-1]]["PE"].at("gu")

        @block.tensor
        def _(pe):
            def mod_phase(l):
                key = f"mod{l}"
                ph = enter(pe, key, "PE")
                S = ph["PE"]

                def turn(i):
                    for q in range(2 * KT):
                        arrived(pe, key, i, q)
                        k = q // 2
                        for n in range(2):
                            g = 2 * (q % 2) + n
                            col = (q % 4) * BW + n * 512
                            mm = pe.matmul(psum[32 * g:32 * g + 32, i + 1, 0:512], lhsT=cond[:, k, :],
                                           rhs=ring[:, col:col + 512], start=(k == 0), stop=(k == KT - 1),
                                           skip_group_check=True)
                        mm.then_inc(*S.mark(f"m{q}"))
                for i in range(MOD_TURNS):
                    turn(i)
                ph = enter(pe, f"modt{l}", "PE")
                pick = ident.rearrange("p (g m) -> p g m", m=32)[:, :, 0:2]
                result = psum[:, 0, 0:96].rearrange("p (t g j s) -> p t g j s", t=MOD_TURNS, g=4, s=2)
                for t in range(MOD_TURNS):
                    pe.wait_ge(*ph["A"].at(f"e{t}"))
                    for j in range(4):
                        mm = pe.matmul(result[:, t, :, j, :], lhsT=slot(MODT + t, j * P, j * P + P), rhs=pick,
                                       start=True, stop=True, skip_group_check=True)
                mm.then_inc(*ph["PE"].mark("t"))

            def norm_phase(key, c0):
                ph = enter(pe, key, "PE")
                for j in range(KT):
                    pe.wait_ge(*ph["A"].at(f"sq{j}"))
                    for a, b in halves(c0, 0):
                        mm = pe.matmul(psum[:, 0, a:b], lhsT=ones, rhs=slot(H0 + j, a, b),
                                       start=(j == 0), stop=(j == KT - 1), skip_group_check=True)
                mm.then_inc(*ph["PE"].mark("sum"))

            def lora_phase(l):
                key = f"lora{l}"
                ph = enter(pe, key, "PE")
                for q, name in enumerate(["w", "a", "g"]):
                    arrived(pe, key, 0, q)
                    project(pe, q, chunk_blocks(q), hs, 0, 0).then_inc(*ph["PE"].mark(name))
                arrived(pe, key, 0, 3)
                pe.matmul(psum[:, 3, 0:2], lhsT=chunk_blocks(3)[0], rhs=hs[0][:, 0:2], start=True,
                          stop=True).then_inc(*ph["PE"].mark("pad"))

            def pair_phase(key, l):
                ph = enter(pe, key, "PE")
                S, A, V, G = (ph.get(e) for e in ("PE", "A", "V", "G"))
                parts = ph["parts"]
                prep, scan = "prep" in parts, "scan" in parts
                _, wide = names_pair(parts)
                y0 = cols(l)
                freed = {"zr": (A, "raw_r"), "zk": (A, "raw_k"), "zv": (A, "raw_v"), "gu": (A, "gz"),
                         "kkn": (V, "kkm"), "Y": (A, "y"), "mean": (V, "yc"),
                         "var": (A, "yln"), "bonus": (V, "bv")}
                for d in DIRS:
                    freed.update({f"lw{d}": (A, f"sw{d}"), f"la{d}": (A, f"sa{d}"), f"A{d}": (A, f"A{d}"),
                                  f"B{d}": (V, f"B{d}"), f"RB{d}": (V, f"RB{d}"), f"RK{d}": (V, f"RK{d}"),
                                  f"BV{d}": (A, f"BV{d}"), f"U0{d}": (A, f"U0{d}"), f"G{d}": (A, f"G{d}"),
                                  f"MT{d}": (V, f"MT{d}"), f"N{d}": (A, f"N{d}"), f"Q{d}": (V, f"Q{d}"),
                                  f"chain{d}": (V, f"c{NCH - 2}{d}"), f"T5{d}": (A, f"T5{d}"),
                                  f"U5{d}": (A, f"XT5{d}")})
                    for n in range(1, 5):
                        freed.update({f"T{n}{d}": (V, f"T{n}{d}"), f"U{n}{d}": (V, f"XT{n}{d}")})

                def turn(i):
                    def take(name, *also):
                        k = wide.index(name)
                        steps = [(*x, 0)[:3] for x in also]
                        if k >= 4:
                            steps.append((*freed[wide[k - 4]], 0))
                        else:
                            before = [n for m, n in enumerate(wide) if m % 4 == k]
                            steps.append((*freed[before[-1]], 1))
                        wait_steps(pe, i, *steps)
                        return k % 4

                    def mm64(tile, c, h, lhs, rhs, start, stop):
                        rows = slice(h * HD, h * HD + HD)
                        return pe.matmul(psum[rows, tile, c * C:c * C + C], lhsT=arena[rows, lhs:lhs + C],
                                         rhs=arena[rows, rhs:rhs + C], start=start, stop=stop, skip_group_check=True)

                    def units(tile, terms, c0=0):
                        mm = None
                        settle(pe)
                        for c in range(c0 // C, NCH):
                            for h in range(2):
                                for k, (lo, ro) in enumerate(terms):
                                    mm = mm64(tile, c, h, lo * T + c * C, ro * T + c * C,
                                              k == 0, k == len(terms) - 1)
                        return mm

                    def inputs(name, q):
                        tile = take(name)
                        arrived(pe, key, i, q)
                        project(pe, tile, chunk_blocks(q), hs, 0, 0).then_inc(*S.mark(name))

                    def small(tile, out_q, rhs, lhs):
                        for c in range(NCH):
                            for o, left, right in zip(out_q, lhs, rhs):
                                mm = pe.matmul(psum[o * H:o * H + H, tile, c * H:c * H + H], lhsT=left(c), rhs=right(c),
                                               start=True, stop=True, skip_group_check=True)
                        return mm

                    def a_block(d, row, col):
                        at = (M0_ + 11 * d + M_A) * T + col * H
                        return lambda c: arena[row * H:row * H + H, at + c * C:at + c * C + H]

                    def d_block(x, d, row):
                        ap = diag(x, M0_ + 11 * d)
                        return lambda c: ap[row * H:row * H + H, c * H:c * H + H]

                    def level(n):
                        rows = range(P // H)
                        for d in DIRS:
                            tile = take(f"T{n}{d}", (V, f"X{d}" if n == 1 else f"Xt{n - 1}{d}"), (A, f"A{d}"))
                            settle(pe)
                            small(tile, rows, [d_block("X", d, q) for q in rows],
                                  [a_block(d, q, q % 2) for q in rows]).then_inc(*S.mark(f"T{n}{d}"))
                        for d in DIRS:
                            tile = take(f"U{n}{d}", (V, f"T{n}{d}"))
                            settle(pe)
                            small(tile, rows, [d_block("XT", d, q) for q in rows],
                                  [d_block("T", d, q) for q in rows]).then_inc(*S.mark(f"U{n}{d}"))

                    def last_level():
                        early = [[2 * h + d for h in range(2)] for d in DIRS]
                        late = [[2 * h + 1 - d for h in range(2)] for d in DIRS]
                        for d in DIRS:
                            tile = take(f"T5{d}", (V, f"Xt4{d}"), (A, f"A{d}"))
                            settle(pe)
                            small(tile, late[d], [d_block("X", d, q) for q in early[d]],
                                  [a_block(d, q, 1 - d) for q in early[d]]).then_inc(*S.mark(f"T5{d}"))
                        for d in DIRS:
                            tile = take(f"U5{d}", (A, f"T5{d}"))
                            settle(pe)
                            small(tile, early[d], [d_block("XT", d, q) for q in late[d]],
                                  [d_block("T", d, q) for q in late[d]]).then_inc(*S.mark(f"U5{d}"))

                    if scan:
                        for d in DIRS:
                            f = F0 + 6 * d
                            ready = [(V, f"rP{d}", 1)] if prep else []
                            operands = [(V, f"bQ{d}", 1), (G, f"kE{d}", 1)] if prep else []
                            units(take(f"A{d}", *operands), [(f + F_B, f + F_KK)]).then_inc(*S.mark(f"A{d}"))
                            units(take(f"B{d}"), [(f + F_K, f + F_KK)]).then_inc(*S.mark(f"B{d}"))
                            units(take(f"RB{d}", *ready), [(f + F_B, f + F_R)], y0).then_inc(*S.mark(f"RB{d}"))
                            units(take(f"RK{d}"), [(f + F_K, f + F_R)], y0).then_inc(*S.mark(f"RK{d}"))
                        tile = take("bonus", (V, "bon"))
                        project(pe, tile, [heads], [slot(BN)], y0, 0).then_inc(*S.mark("bonus"))
                        tile = take("gu")
                        project(pe, tile, [up_block(4)], [slot(LG)], y0, 0).then_inc(*S.mark("gu"))
                        for d in DIRS:
                            m = M0_ + 11 * d
                            tile = take(f"BV{d}", (V, f"B{d}"))
                            units(tile, [(m + M_BT, VT)]).then_inc(*S.mark(f"BV{d}"))
                    if prep:
                        inputs("zr", 0)
                    if scan:
                        level(1)
                    if prep:
                        inputs("zk", 1)
                    if scan:
                        level(2)
                    if prep:
                        arrived(pe, key, i, 2)
                        for d in DIRS:
                            for n, (name, src) in enumerate((("lw", LW), ("la", LA))):
                                tile = take(f"{name}{d}")
                                project(pe, tile, [up_block(2 * n + d)], [slot(src)], 0, 0).then_inc(*S.mark(f"{name}{d}"))
                    if scan:
                        level(3)
                    if prep:
                        tile = take("kkn", (A, "kksq"))
                        project(pe, tile, [heads], [slot(T0)], 0, 0).then_inc(*S.mark("kkn"))
                    if scan:
                        level(4)
                        last_level()
                        for d in DIRS:
                            m = M0_ + 11 * d
                            tile = take(f"U0{d}", (V, "zero1"), (A, f"XT5{d}"))
                            units(tile, [(m + M_XT, m + M_BV)]).then_inc(*S.mark(f"U0{d}"))
                            units(take(f"G{d}"), [(m + M_XT, m + M_KKT)]).then_inc(*S.mark(f"G{d}"))
                        for d in DIRS:
                            m = M0_ + 11 * d
                            tile = take(f"MT{d}", (A, f"G{d}"))
                            units(tile, [(m + M_G, m + M_BET)]).then_inc(*S.mark(f"MT{d}"))
                            units(take(f"N{d}"), [(m + M_BET, m + M_U0), (m + M_KET, VT)]).then_inc(*S.mark(f"N{d}"))
                            units(take(f"Q{d}"), [(m + M_G, m + M_RB)], y0).then_inc(*S.mark(f"Q{d}"))
                        tiles = [take(f"chain{d}", (V, f"MT{d}"), (A, f"N{d}")) for d in DIRS]
                        ytile = take("Y")
                        free = []
                        for d in DIRS:
                            m = M0_ + 11 * d
                            free += [(c, h, lo * T + c * C, ro * T + c * C) for c in range(y0 // C, NCH) for h in range(2)
                                     for lo, ro in ((m + M_U0, m + M_RB), (VT, m + M_RK))]
                        per = -(-len(free) // (len(CHAIN) * 2))
                        opened = set()
                        for n in CHAIN:
                            for d in DIRS:
                                m, c = M0_ + 11 * d, seq(d)[n]
                                if n == 1:
                                    state = (m + M_N) * T + seq(d)[0] * C
                                else:
                                    pe.wait_ge(*V.at(f"c{n - 1}{d}", i))
                                    state = (m + M_S) * T + c * C
                                settle(pe)
                                for h in range(2):
                                    mm = mm64(tiles[d], c, h, (m + M_MT) * T + c * C, state, True, True)
                                mm.then_inc(*S.mark(f"c{n}{d}"))
                                for cc, h, lo, ro in free[:per]:
                                    bank = (cc * C // 512, h)
                                    mm64(ytile, cc, h, lo, ro, bank not in opened, False)
                                    opened.add(bank)
                                free = free[per:]
                        assert not free
                        wait_steps(pe, i, (V, f"c{NCH - 2}1", 0))
                        settle(pe)
                        for c in range(y0 // C, NCH):
                            for d in DIRS:
                                m, n = M0_ + 11 * d, seq(d).index(c)
                                if n == 0:
                                    continue
                                state = (m + M_N) * T + seq(d)[0] * C if n == 1 else (m + M_S) * T + c * C
                                for h in range(2):
                                    mm = mm64(ytile, c, h, state, (m + M_Q) * T + c * C, False, True)
                        mm.then_inc(*S.mark("Y"))
                    if prep:
                        inputs("zv", 3)
                    if scan:
                        tile = take("mean", (A, "y"))
                        project(pe, tile, [heads], [slot(PT0)], y0, 0).then_inc(*S.mark("mean"))
                        tile = take("var", (A, "ysq"))
                        project(pe, tile, [heads], [slot(PT1)], y0, 0).then_inc(*S.mark("var"))
                each(pe, ph, turn)

            def branch_phase(l):
                key = f"branch{l}"
                ph = enter(pe, key, "PE")
                S, A, V = ph["PE"], ph["A"], ph["V"]
                c0 = cols(l)
                seq_ = []
                for j in range(CT):
                    seq_ += [(f"cb{j}", A, f"cb{j}"), (f"ca{j}", V, f"u{j}")]
                seq_ += [(f"su{j}", A, f"su{j}") for j in range(CT)] + [(f"sv{j}", A, f"sv{j}") for j in range(CT)]
                for n, (name, _, _) in enumerate(seq_):
                    if n >= 4:
                        _, E, step = seq_[n - 4]
                        pe.wait_ge(*E.at(step))
                    arrived(pe, key, 0, n)
                    project(pe, n % 4, chunk_blocks(n), hs, c0, c0).then_inc(*S.mark(name))
                pe.wait_ge(*A.at(f"sv{CT - 1}"))
                for name, tile, src, E, step in (("cmean", 0, CY, V, None), ("cvar", 1, CU, A, "csq"),
                                                 ("smean", 2, SV, A, None), ("svar", 3, H1, A, "ssq")):
                    if name == "cmean":
                        pe.wait_ge(*V.at(f"y{CT - 1}_{len(conv_taps(l)) - 1}"))
                    if step:
                        pe.wait_ge(*A.at(f"{step}{CT - 1}"))
                    project(pe, tile, [ones] * CT, [slot(src + j) for j in range(CT)], c0, c0).then_inc(*S.mark(name))
                for j in range(CT):
                    pe.wait_ge(*A.at(f"sn{j}"))
                    if j == 0:
                        pe.wait_ge(*A.at("sr"))
                        pe.wait_ge(*V.at(f"sc{CT - 1}"))
                    for n in range((T - c0) // P):
                        a = c0 + n * P
                        mm = pe.matmul(psum[:, j, n * P:n * P + P], lhsT=slot(SV + j, a, a + P), rhs=ident,
                                       start=True, stop=True, skip_group_check=True)
                    mm.then_inc(*S.mark(f"tr{j}"))
                for j in range(CT):
                    pe.wait_ge(*A.at(f"tr{j}"))
                    if j == 0:
                        pe.wait_ge(s_sgu, 32 * (l + 1))
                    for n in range((T - c0) // P):
                        for g in range(2):
                            mm = pe.matmul(psum[g * HD:g * HD + HD, j, n * P:n * P + P],
                                           lhsT=arena[:, (VTK + j) * T + n * P + g * HD:(VTK + j) * T + n * P + g * HD + HD],
                                           rhs=sgu_w[:, (2 * j + g) * P:(2 * j + g + 1) * P],
                                           start=True, stop=True, skip_group_check=True)
                    mm.then_inc(*S.mark(f"sp{j}"))

            def merge_phase(l):
                key = f"merge{l}"
                ph = enter(pe, key, "PE")
                S, A, V = ph["PE"], ph["A"], ph["V"]
                c0 = cols(l)
                ya = [slot(YA0 + j) for j in range(KT)]
                cv = [slot(CY + j) for j in range(CT)]
                sg = [slot(SU + j) for j in range(CT)]

                pe.wait_ge(s_back, 32 * (l + 1))

                def turn(i):
                    flow = []
                    for q in range(MERGE_TILES):
                        flow += [(f"g0{q}", 5 * q, 0, 8, hs, A), (f"p0{q}", 5 * q + 1, 0, 8, ya, V),
                                 (f"g1{q}", 5 * q + 2, 0, 8, hs, A), (f"p1{q}", 5 * q + 4, 0, 4, cv, V),
                                 (f"g2{q}", 5 * q + 3, 0, 8, hs, A), (f"p2{q}", 5 * q + 4, 4, 4, sg, V)]
                    for n, (name, chunk, k0, nk, mov, _) in enumerate(flow):
                        if n >= 4:
                            pe.wait_ge(*flow[n - 4][5].at(flow[n - 4][0], i))
                        else:
                            pe.wait_ge(*flow[n - 4][5].at(flow[n - 4][0], i, back=1))
                        arrived(pe, key, i, chunk)
                        project(pe, n % 4, chunk_blocks(chunk, k0, nk), mov, c0, c0).then_inc(*S.mark(name))
                each(pe, ph, turn)

            def outproj_phase(key, c0, mov, per):
                ph = enter(pe, key, "PE")
                S, V = ph["PE"], ph["V"]

                def turn(i):
                    for q in range(4):
                        pe.wait_ge(*V.at(f"x{q}", i, back=1))
                        for n in range(per):
                            arrived(pe, key, i, per * q + n)
                            for k, w in zip(range(8 * n, len(mov)), chunk_blocks(per * q + n)):
                                for a, b in halves(c0, c0):
                                    mm = pe.matmul(psum[:, q, a - c0:b - c0], lhsT=w, rhs=mov[k][:, a:b],
                                                   start=(k == 0), stop=(k == len(mov) - 1), skip_group_check=True)
                            mm.then_inc(*S.mark(f"o{q}{n}"))
                each(pe, ph, turn)

            def ffn_phase(l):
                key = f"ffn{l}"
                ph = enter(pe, key, "PE")
                S, A, V = ph["PE"], ph["A"], ph["V"]
                c0 = cols(l)

                def turn(i):
                    for q, (name, E, step) in enumerate((("g0", A, "s0"), ("u0", V, "a0"), ("g1", A, "s1"), ("u1", V, "a1"))):
                        pe.wait_ge(*E.at(step, i, back=1))
                        arrived(pe, key, i, q)
                        project(pe, q, chunk_blocks(q), hs, c0, c0).then_inc(*S.mark(name))
                each(pe, ph, turn)

            for l in range(DEPTH):
                mod_phase(l)
                norm_phase(f"norm1_{l}", 0)
                lora_phase(l)
                for name, _, _ in PAIR_PHASES:
                    pair_phase(f"{name}{l}", l)
                branch_phase(l)
                merge_phase(l)
                outproj_phase(f"res1_{l}", cols(l), [slot(M0 + j) for j in range(KT)], 1)
                norm_phase(f"norm2_{l}", cols(l))
                ffn_phase(l)
                outproj_phase(f"res2_{l}", cols(l), [slot(ACT0 + j) for j in range(FT)], 3)
            norm_phase("final", CTX)

        @block.scalar
        def _(act):
            act.dma_start(cvec[:, :], c_in).then_inc(s_cond, 16)
            act.dma_start(const[:, :], const_in).then_inc(s_load, 16)
            act.dma_start(slot(SCANMASK), scanmask_in).then_inc(s_load, 16)
            act.dma_start(arena[:, X0 * T:(X0 + KT) * T], x_in).then_inc(s_load, 16)
            act.dma_start(par[:, :], par_in[0, :, :]).then_inc(s_par, 16)

            def cond_phase(l):
                ph = enter(act, f"cond{l}", "A")
                act.wait_ge(*ph["V"].at("zero"))
                act.wait_ge(s_cond, 16)
                act.activation(cond[:, :, 0:2], cvec[:, :].rearrange("p (k s) -> p k s", s=2), ACT.Silu).then_inc(*ph["A"].mark("silu"))

            def mod_phase(l):
                key = f"mod{l}"
                S = enter(act, key, "A")["PE"]
                nq = len(phases[key]["chunks"])
                for q in range(1, nq, 2):
                    if q >= 4:
                        act.wait_ge(*S.at(f"m{q - 4}", 0))
                    load_chunk(act, q, slice(chunk_base[key] + q, chunk_base[key] + q + 1))
                with act.Fori(1, phases[key]["turns"]) as i:
                    for q in range(1, nq, 2):
                        if q >= 4:
                            act.wait_ge(*S.at(f"m{q - 4}", i))
                        else:
                            act.wait_ge(*S.at(f"m{nq - 4 + q}", i, back=1))
                        load_chunk(act, q, bass.ds(i * nq + (chunk_base[key] + q), 1))
                ph = enter(act, f"modt{l}", "A")
                if l == 0:
                    act.wait_ge(s_load, 48)
                for t in range(MOD_TURNS):
                    act.activation(slot(MODT + t, 0, 512), psum[:, t + 1, 0:512], ACT.Copy).then_inc(*ph["A"].mark(f"e{t}"))

            def rsqrt(A, turn, out_, in_, scale, bias, name_ln, name_exp):
                act.activation(out_, in_, ACT.Ln, bias=bias, scale=scale).then_inc(*A.mark(name_ln))
                act.wait_ge(*A.at(name_ln, turn))
                act.activation(out_, out_, ACT.Exp, scale=-0.5).then_inc(*A.mark(name_exp))

            def norm_phase(key, c0, which, affine=True):
                ph = enter(act, key, "A")
                A, V = ph["A"], ph["V"]
                for j in range(KT):
                    act.activation(slot(H0 + j, c0), slot(X0 + j, c0), ACT.Square).then_inc(*A.mark(f"sq{j}"))
                act.wait_ge(*ph["PE"].at("sum"))
                rsqrt(A, 0, slot(NT, c0), psum[:, 0, c0:T], 1.0 / D, eps_c(0), "ln", "rstd")
                if not affine:
                    return
                for j in range(KT):
                    act.wait_ge(*V.at(f"xn{j}"))
                    for s, a, b in segs(c0):
                        shift = mod[:, 2 * (24 * which + j) + s:2 * (24 * which + j) + s + 1]
                        gain = a_mod[:, 2 * (KT * which + j) + s:2 * (KT * which + j) + s + 1]
                        ins = act.activation(slot(H0 + j, a, b), slot(H0 + j, a, b), ACT.Identity, bias=shift, scale=gain)
                    ins.then_inc(*A.mark(f"h{j}"))

            def lora_phase(l):
                ph = enter(act, f"lora{l}", "A")
                A, V, PE = ph["A"], ph["V"], ph["PE"]
                act.dma_start(spill, arena[:, X0 * T:(X0 + KT) * T]).then_inc(s_spill, 16)
                for n, name in enumerate(["w", "a", "g"]):
                    act.wait_ge(*PE.at(name))
                    act.activation(slot(T0 + n), psum[:, n, 0:T], ACT.Copy).then_inc(*A.mark(f"raw{n}"))
                act.wait_ge(*V.at("s0c"))
                act.activation(slot(LW), slot(LW), ACT.Tanh).then_inc(*A.mark("act0"))
                act.wait_ge(*V.at("s2c"))
                act.wait_ge(s_spill, 16 * (l + 1))
                act.activation(slot(LG), slot(LG), ACT.Sigmoid).then_inc(*A.mark("act2"))

            def pair_phase(key, l):
                ph = enter(act, key, "A")
                A, V, PE, G = (ph.get(e) for e in ("A", "V", "PE", "G"))
                parts = ph["parts"]
                prep, scan = "prep" in parts, "scan" in parts
                _, wide = names_pair(parts)
                y0 = cols(l)

                def turn(i):
                    def ps(name, a=0, b=T):
                        return psum[:, wide.index(name) % 4, a:b]

                    def evac(name, dst, a=0, scale=1.0):
                        act.wait_ge(*PE.at(name, i))
                        act.activation(slot(dst, a), ps(name, a), ACT.Copy, scale=scale).then_inc(*A.mark(name))

                    def raw(x, dst):
                        act.wait_ge(*PE.at(f"z{x}", i))
                        act.activation(slot(dst), ps(f"z{x}"), ACT.Copy).then_inc(*A.mark(f"raw_{x}"))

                    if scan:
                        for d in DIRS:
                            act.wait_ge(*V.at(f"X1a{d}", i))
                            evac(f"A{d}", M0_ + 11 * d + M_A)
                        act.wait_ge(*PE.at("gu", i))
                        wait_steps(act, i, (G, "yst", 1))
                        act.activation(slot(GZ, y0), ps("gu", y0), ACT.Copy).then_inc(*A.mark("gz"))
                        for d in DIRS:
                            evac(f"BV{d}", M0_ + 11 * d + M_BV)
                    if prep:
                        raw("r", T0)
                        raw("k", T1)
                        act.wait_ge(*G.at("pp", i))
                        for d in DIRS:
                            f = F0 + 6 * d
                            act.wait_ge(*PE.at(f"lw{d}", i))
                            if scan:
                                act.wait_ge(*V.at(f"bT{d}", i))
                            act.activation(slot(f + F_BE), ps(f"lw{d}"), ACT.Sigmoid, bias=ppn(f"w0{d}")).then_inc(*A.mark(f"sw{d}"))
                            act.wait_ge(*PE.at(f"la{d}", i))
                            if scan:
                                act.wait_ge(*V.at(f"kT{d}", i))
                            act.activation(slot(f + F_KE), ps(f"la{d}"), ACT.Sigmoid, bias=ppn(f"a0{d}")).then_inc(*A.mark(f"sa{d}"))
                        act.wait_ge(*V.at("kk0", i))
                        act.activation(slot(T0), slot(KK_), ACT.Square).then_inc(*A.mark("kksq"))
                        act.wait_ge(*V.at("kkm", i))
                        act.activation(slot(T1), slot(T1), ACT.Ln, scale=float(2 ** LN_SHIFT)).then_inc(*A.mark("kkl"))
                        act.wait_ge(*A.at("kkl", i))
                        act.activation(slot(T1), slot(T1), ACT.Exp, scale=-0.5, bias=eps_c(3)).then_inc(*A.mark("kke"))
                        for d in DIRS:
                            f, le, ei = F0 + 6 * d, (LE0, LE1)[d], (EI0, EI1)[d]
                            act.wait_ge(*V.at(f"L{d}", i))
                            act.wait_ge(*G.at("Le0" if d == 0 else "Li1", i))
                            act.activation(slot(ei), slot(le), ACT.Exp, scale=-KAPPA).then_inc(*A.mark(f"Ei{d}"))
                            act.activation(slot(le), slot(le), ACT.Exp, scale=KAPPA).then_inc(*A.mark(f"En{d}"))
                            act.activation(slot(f + F_KK), slot(f + F_KK), ACT.Exp, scale=-KAPPA).then_inc(*A.mark(f"Ee{d}"))
                    if scan:
                        def copy(out_, in_, scale=1.0):
                            return act.activation(out_, in_, ACT.Copy, scale=scale)

                        for d in DIRS:
                            m = M0_ + 11 * d
                            act.wait_ge(*V.at(f"XT4{d}", i))
                            for q in range(P // H):
                                ins = copy(quarter(slot(m + M_XT), q, q % 2),
                                           by_half(diag("XT", m))[q * H:q * H + H])
                            ins.then_inc(*A.mark(f"xd{d}"))
                        for d in DIRS:
                            act.wait_ge(*PE.at(f"T5{d}", i))
                            for h in range(2):
                                q = 2 * h + 1 - d
                                ins = copy(diag("T", M0_ + 11 * d)[q * H:q * H + H], ps(f"T5{d}", 0, NCH * H)[q * H:q * H + H])
                            ins.then_inc(*A.mark(f"T5{d}"))
                        for d in DIRS:
                            act.wait_ge(*PE.at(f"U5{d}", i))
                            for h in range(2):
                                q = 2 * h + d
                                ins = copy(quarter(slot(M0_ + 11 * d + M_XT), q, 1 - d),
                                           by_half(ps(f"U5{d}", 0, NCH * H))[q * H:q * H + H], -1.0)
                            ins.then_inc(*A.mark(f"XT5{d}"))
                        for d in DIRS:
                            evac(f"U0{d}", M0_ + 11 * d + M_U0, scale=-1.0)
                            evac(f"G{d}", M0_ + 11 * d + M_G, scale=-1.0)
                        for d in DIRS:
                            evac(f"N{d}", M0_ + 11 * d + M_N)
                        act.wait_ge(*PE.at("Y", i))
                        act.activation(slot(PT0, y0), ps("Y", y0), ACT.Copy).then_inc(*A.mark("y"))
                    if prep:
                        raw("v", T2)
                    if scan:
                        act.wait_ge(*V.at("yc", i))
                        act.activation(slot(PT1, y0), slot(PT0, y0), ACT.Square).then_inc(*A.mark("ysq"))
                        act.wait_ge(*PE.at("var", i))
                        rsqrt(A, i, slot(PT1, y0), ps("var", y0), 1.0 / HD, eps_c(2), "yln", "yrs")
                        act.wait_ge(*V.at("ynr", i))
                        act.wait_ge(*G.at("ppc", i))
                        act.activation(slot(PT0, y0), slot(PT0, y0), ACT.Identity, bias=ppc("gnb"), scale=ppc("gng")).then_inc(*A.mark("yn"))
                each(act, ph, turn)

            def branch_phase(l):
                ph = enter(act, f"branch{l}", "A")
                A, V, PE = ph["A"], ph["V"], ph["PE"]
                c0 = cols(l)
                n = T - c0
                act.dma_start(arena[:, YA0 * T:(YA0 + KT) * T], ya_spill).then_inc(s_back, 16)
                act.dma_start(arena[:, X0 * T:(X0 + KT) * T], spill).then_inc(s_back, 16)
                act.dma_start(sgu_w, sgu_w_in[l, :, :]).then_inc(s_sgu, 16)
                act.dma_start(sgu_b, sgu_b_in[l, :, :]).then_inc(s_sgu, 16)
                for j in range(CT):
                    act.wait_ge(*PE.at(f"cb{j}"))
                    if j >= 2:
                        act.wait_ge(*V.at(f"u{j - 2}"))
                    act.activation(slot(G0 + j % 2, c0), psum[:, (2 * j) % 4, 0:n], ACT.Sigmoid).then_inc(*A.mark(f"cb{j}"))
                for name, dst in (("su", SU), ("sv", SV)):
                    for j in range(CT):
                        act.wait_ge(*PE.at(f"{name}{j}"))
                        act.activation(slot(dst + j, c0), psum[:, j, 0:n], ACT.Gelu_apprx_tanh).then_inc(*A.mark(f"{name}{j}"))
                for j in range(CT):
                    act.wait_ge(*V.at(f"cc{j}"))
                    act.activation(slot(CU + j, c0), slot(CY + j, c0), ACT.Square).then_inc(*A.mark(f"csq{j}"))
                for j in range(CT):
                    act.wait_ge(*V.at(f"sc{j}"))
                    act.activation(slot(H1 + j, c0), slot(SV + j, c0), ACT.Square).then_inc(*A.mark(f"ssq{j}"))
                for x, tile, dst in (("c", 1, G0), ("s", 3, G0 + 1)):
                    act.wait_ge(*PE.at(f"{x}var"))
                    rsqrt(A, 0, slot(dst, c0), psum[:, tile, 0:n], 1.0 / CONV, eps_c(1), f"{x}ln", f"{x}r")
                for j in range(CT):
                    act.wait_ge(*V.at(f"cn{j}"))
                    act.activation(slot(CY + j, c0), slot(CY + j, c0), ACT.Silu, bias=par_c("clb", j), scale=par_c("clg", j)).then_inc(*A.mark(f"cs{j}"))
                for j in range(CT):
                    act.wait_ge(*V.at(f"sm{j}"))
                    act.activation(slot(SV + j, c0), slot(SV + j, c0), ACT.Identity, bias=par_c("slb", j), scale=par_c("slg", j)).then_inc(*A.mark(f"sn{j}"))
                for j in range(CT):
                    act.wait_ge(*PE.at(f"tr{j}"))
                    act.activation(slot(VTK + j, 0, n), psum[:, j, 0:n], ACT.Copy).then_inc(*A.mark(f"tr{j}"))

            def merge_phase(l):
                ph = enter(act, f"merge{l}", "A")
                A, V, PE = ph["A"], ph["V"], ph["PE"]
                c0 = cols(l)
                n = T - c0
                order_g = [(b, q) for q in range(MERGE_TILES) for b in range(3)]

                def turn(i):
                    for k, (b, q) in enumerate(order_g):
                        act.wait_ge(*PE.at(f"g{b}{q}", i))
                        if k >= 3:
                            act.wait_ge(*V.at("p%d%d" % order_g[k - 3], i))
                        else:
                            act.wait_ge(*V.at("p%d%d" % order_g[k - 3], i, back=1))
                        act.activation(slot(G0 + k % 3, c0), psum[:, (2 * k) % 4, 0:n], ACT.Sigmoid).then_inc(*A.mark(f"g{b}{q}"))
                each(act, ph, turn)

            def ffn_phase(l):
                ph = enter(act, f"ffn{l}", "A")
                A, V, PE = ph["A"], ph["V"], ph["PE"]
                c0 = cols(l)
                n = T - c0

                def turn(i):
                    for q in range(2):
                        act.wait_ge(*PE.at(f"g{q}", i))
                        act.wait_ge(*V.at(f"a{q}", i, back=1))
                        act.activation(slot(YA0 + q, c0), psum[:, 2 * q, 0:n], ACT.Silu).then_inc(*A.mark(f"s{q}"))
                each(act, ph, turn)

            for l in range(DEPTH):
                if l:
                    act.wait_ge(*phases[f"res2_{l - 1}"]["V"].end())
                    act.wait_ge(*phases[f"res2_{l - 1}"]["PE"].end())
                    act.dma_start(par[:, :], par_in[l, :, :]).then_inc(s_par, 16)
                cond_phase(l)
                mod_phase(l)
                norm_phase(f"norm1_{l}", 0, 0)
                lora_phase(l)
                for name, _, _ in PAIR_PHASES:
                    pair_phase(f"{name}{l}", l)
                branch_phase(l)
                merge_phase(l)
                norm_phase(f"norm2_{l}", cols(l), 1)
                ffn_phase(l)
            norm_phase("final", CTX, 0, affine=False)
            act.wait_ge(*phases["final"]["V"].end())
            act.dma_start(out, arena[:, H0 * T:(H0 + KT) * T].rearrange("p (j t) -> p j t", t=T)[:, :, CTX:T]).then_inc(s_out, 16)
            act.wait_ge(s_out, 16)

        @block.vector
        def _(dve):
            def modv_phase(l):
                ph = enter(dve, f"modv{l}", "V")
                V = ph["V"]
                dve.wait_ge(s_par, 16 * (l + 1))
                dve.tensor_tensor(mod[:, :].rearrange("p (j s) -> p j s", s=2),
                                  psum[:, 0, 0:96].rearrange("p (j s) -> p j s", s=2),
                                  par[:, PAR["b_mod"]:PAR["b_mod"] + 48, None].to_broadcast([P, 48, 2]),
                                  ALU.add).then_inc(*V.mark("mod"))
                dve.wait_ge(*V.at("mod"))
                for which, g, name in ((0, "n1g", "a1"), (1, "n2g", "a2")):
                    o = 2 * (24 * which + KT)
                    dve.scalar_tensor_tensor(
                        out=a_mod[:, 2 * KT * which:2 * KT * (which + 1)].rearrange("p (j s) -> p j s", s=2),
                        in0=mod[:, o:o + 2 * KT].rearrange("p (j s) -> p j s", s=2), scalar=1.0,
                        in1=par[:, PAR[g]:PAR[g] + KT, None].to_broadcast([P, KT, 2]),
                        op0=ALU.add, op1=ALU.mult).then_inc(*V.mark(name))

            def norm_phase(key, c0, final=False):
                ph = enter(dve, key, "V")
                V, A = ph["V"], ph["A"]
                dve.wait_ge(*A.at("rstd"))
                for j in range(KT):
                    dve.tensor_tensor(slot(H0 + j, c0), slot(X0 + j, c0), slot(NT, c0), ALU.mult).then_inc(*V.mark(f"xn{j}"))
                if final:
                    for j in range(KT):
                        dve.wait_ge(*V.at(f"xn{j}"))
                        dve.tensor_scalar(slot(H0 + j, c0), slot(H0 + j, c0), par_c("fin", j), None, ALU.mult).then_inc(*V.mark(f"y{j}"))

            def shift(V, i, raw, dst, w0, w1, w2, n0, n1, n2):
                dve.tensor_scalar(slot(dst), slot(raw), w1, None, ALU.mult).then_inc(*V.mark(n0))
                dve.wait_ge(*V.at(n0, i))
                for a, b in ((0, CTX), (CTX, T)):
                    ins = dve.scalar_tensor_tensor(out=slot(dst, a + 1, b), in0=slot(raw, a, b - 1), scalar=w0,
                                                   in1=slot(dst, a + 1, b), op0=ALU.mult, op1=ALU.add)
                ins.then_inc(*V.mark(n1))
                dve.wait_ge(*V.at(n1, i))
                for a, b in ((0, CTX), (CTX, T)):
                    ins = dve.scalar_tensor_tensor(out=slot(dst, a, b - 1), in0=slot(raw, a + 1, b), scalar=w2,
                                                   in1=slot(dst, a, b - 1), op0=ALU.mult, op1=ALU.add)
                ins.then_inc(*V.mark(n2))

            def lora_phase(l):
                ph = enter(dve, f"lora{l}", "V")
                A, V = ph["A"], ph["V"]
                for n in range(3):
                    dve.wait_ge(*A.at(f"raw{n}"))
                    shift(V, 0, T0 + n, LW + n, *[par_c("shift", 3 * n + t) for t in range(3)],
                          *[f"s{n}{x}" for x in "abc"])

            def pair_phase(key, l):
                ph = enter(dve, key, "V")
                A, V, PE, G = (ph.get(e) for e in ("A", "V", "PE", "G"))
                parts = ph["parts"]
                prep, scan = "prep" in parts, "scan" in parts
                _, wide = names_pair(parts)
                y0 = cols(l)
                ny = (T - y0) // C

                def turn(i):
                    def ps(name, a=0, b=T):
                        return psum[:, wide.index(name) % 4, a:b]

                    def mul(name, out_, a, b):
                        dve.tensor_tensor(slot(out_), slot(a), slot(b), ALU.mult).then_inc(*V.mark(name))

                    def shifted(x, raw, dst):
                        dve.wait_ge(*A.at(f"raw_{x}", i))
                        shift(V, i, raw, dst, ppn(f"{x}0"), ppn(f"{x}1"), ppn(f"{x}2"), f"{x}a", f"{x}b", f"{x}c")

                    def masked(name, dst, m, d, a=0):
                        dve.wait_ge(*PE.at(name, i))
                        dve.tensor_tensor(by_chunk(slot(dst, a)), by_chunk(ps(name, a)),
                                          mask(m, d, (T - a) // C), ALU.mult).then_inc(*V.mark(name))

                    def operand_t(x, d):
                        src, dst = {"kT": (F_KE, M_KET), "kkT": (F_KK, M_KKT)}[x]
                        token_major(f"{x}{d}", F0 + 6 * d + src, M0_ + 11 * d + dst)

                    def level(n):
                        for d in DIRS:
                            dve.wait_ge(*PE.at(f"T{n}{d}", i))
                            dve.tensor_tensor(by_half(diag("T", M0_ + 11 * d)), by_half(ps(f"T{n}{d}", 0, NCH * H)),
                                              mask_h(f"lv{n}", d), ALU.mult).then_inc(*V.mark(f"T{n}{d}"))
                        if n < 4:
                            operand_t(*(("kT", 0), ("kT", 1), ("kkT", 1))[n - 1])
                        for d in DIRS:
                            m = M0_ + 11 * d
                            dve.wait_ge(*PE.at(f"U{n}{d}", i))
                            dve.tensor_tensor(diag("XT", m), diag("XT", m), ps(f"U{n}{d}", 0, NCH * H), ALU.subtract).then_inc(*V.mark(f"XT{n}{d}"))
                            dve.wait_ge(*V.at(f"XT{n}{d}", i))
                            dve.transpose(diag("X", m), diag("XT", m)).then_inc(*V.mark(f"Xt{n}{d}"))

                    def token_major(name, src, dst):
                        for h in range(2):
                            for a in range(2):
                                for b in range(2):
                                    t = dve.transpose(by_chunk(slot(dst))[h * HD + b * 32:h * HD + b * 32 + 32, :, a * 32:a * 32 + 32],
                                                      by_chunk(slot(src))[h * HD + a * 32:h * HD + a * 32 + 32, :, b * 32:b * 32 + 32])
                        t.then_inc(*V.mark(name))

                    if scan:
                        dve.scalar_tensor_tensor(out=slot(BN, y0), in0=slot(R_, y0), scalar=ppn("rk"), in1=slot(K_, y0),
                                                 op0=ALU.mult, op1=ALU.mult).then_inc(*V.mark("bon"))
                        wait_steps(dve, i, (V, "ya", 1))
                        token_major("vT", V_, VT)
                        for d in DIRS:
                            m = M0_ + 11 * d
                            dve.wait_ge(*PE.at(f"A{d}", i))
                            for q in range(P // H):
                                ins = dve.tensor_tensor(by_half(diag("XT", m))[q * H:q * H + H], quarter(ps(f"A{d}"), q, q % 2),
                                                        mask_h("first", d)[q * H:q * H + H], ALU.mult)
                            ins.then_inc(*V.mark(f"X1a{d}"))
                            dve.wait_ge(*V.at(f"X1a{d}", i))
                            dve.tensor_tensor(by_half(diag("XT", m)), by_half(diag("XT", m)), const_b(C_ID_H, H), ALU.add).then_inc(*V.mark(f"X1b{d}"))
                            dve.wait_ge(*V.at(f"X1b{d}", i))
                            dve.transpose(diag("X", m), diag("XT", m)).then_inc(*V.mark(f"X{d}"))
                            masked(f"B{d}", m + M_BT, "strict", d)
                            masked(f"RB{d}", m + M_RB, "incl", d, y0)
                            masked(f"RK{d}", m + M_RK, "incl", d, y0)
                            for h in range(2):
                                ins = dve.memset(quarter(slot(m + M_XT), 2 * h + 1 - d, d), 0.0)
                            ins.then_inc(*V.mark(f"zero{d}"))
                        dve.wait_ge(*PE.at("bonus", i))
                        dve.tensor_tensor(slot(BN, y0), slot(V_, y0), ps("bonus", y0), ALU.mult).then_inc(*V.mark("bv"))
                        if prep:
                            wait_steps(dve, i, (G, "kE1", 1))
                        for d in DIRS:
                            token_major(f"bT{d}", F0 + 6 * d + F_BE, M0_ + 11 * d + M_BET)
                        level(1)
                        operand_t("kkT", 0)
                    if prep:
                        dve.wait_ge(*G.at("pp", i))
                        shifted("r", T0, R_)
                    if scan:
                        level(2)
                    if prep:
                        shifted("k", T1, K_)
                        dve.wait_ge(*V.at("kc", i))
                        dve.tensor_scalar(slot(KK_), slot(K_), ppn("kk"), None, ALU.mult).then_inc(*V.mark("kk0"))
                    if scan:
                        level(3)
                    if prep:
                        for d in DIRS:
                            dve.wait_ge(*A.at(f"sw{d}", i))
                            dve.tensor_tensor_scan(slot((LE0, LE1)[d]), slot(SCANMASK), slot(F0 + 6 * d + F_BE), 0.0,
                                                   ALU.mult, ALU.add).then_inc(*V.mark(f"L{d}"))
                        dve.wait_ge(*PE.at("kkn", i))
                        dve.tensor_scalar(slot(T1), ps("kkn"), 1e-24, None, ALU.max).then_inc(*V.mark("kkm"))
                    if scan:
                        level(4)
                    if prep:
                        dve.wait_ge(*A.at("kke", i))
                        mul("kk", KK_, KK_, T1)
                        dve.wait_ge(*V.at("kk", i))
                        for d in DIRS:
                            f, le = F0 + 6 * d, (LE0, LE1)[d]
                            mul(f"b{d}", f + F_B, KK_, f + F_KE)
                            dve.wait_ge(*A.at(f"Ee{d}", i))
                            mul(f"kkP{d}", f + F_KK, KK_, f + F_KK)
                            dve.wait_ge(*V.at(f"b{d}", i))
                            mul(f"bQ{d}", f + F_B, f + F_B, le)
                    if scan:
                        for d in DIRS:
                            m, f = M0_ + 11 * d, F0 + 6 * d
                            dve.wait_ge(*PE.at(f"MT{d}", i))
                            dve.wait_ge(*G.at(f"D{d}", i))
                            dve.tensor_tensor(slot(m + M_MT), slot(m + M_MT), ps(f"MT{d}"), ALU.add).then_inc(*V.mark(f"MT{d}"))
                            dve.wait_ge(*PE.at(f"Q{d}", i))
                            dve.tensor_tensor(slot(m + M_Q, y0), slot(f + F_R, y0), ps(f"Q{d}", y0), ALU.add).then_inc(*V.mark(f"Q{d}"))
                    if prep:
                        if scan:
                            dve.wait_ge(*V.at("Q1", i))
                        for d in DIRS:
                            mul(f"rP{d}", F0 + 6 * d + F_R, R_, (EI0, EI1)[d])
                    if scan:
                        for n in CHAIN:
                            for d in DIRS:
                                m, c, nxt = M0_ + 11 * d, seq(d)[n], seq(d)[n + 1]
                                dve.wait_ge(*PE.at(f"c{n}{d}", i))
                                if n == 1:
                                    dve.wait_ge(*A.at(f"N{d}", i))
                                dve.tensor_tensor(slot(m + M_S, nxt * C, nxt * C + C), slot(m + M_N, c * C, c * C + C),
                                                  psum[:, wide.index(f"chain{d}") % 4, c * C:c * C + C], ALU.add).then_inc(*V.mark(f"c{n}{d}"))
                        dve.wait_ge(*PE.at("mean", i))
                        dve.scalar_tensor_tensor(out=slot(PT0, y0), in0=ps("mean", y0), scalar=-1.0 / HD, in1=slot(PT0, y0),
                                                 op0=ALU.mult, op1=ALU.add).then_inc(*V.mark("yc"))
                    if prep:
                        shifted("v", T2, V_)
                    if scan:
                        dve.wait_ge(*A.at("yrs", i))
                        dve.tensor_tensor(slot(PT0, y0), slot(PT0, y0), slot(PT1, y0), ALU.mult).then_inc(*V.mark("ynr"))
                        dve.wait_ge(*A.at("yn", i))
                        dve.tensor_tensor(slot(PT0, y0), slot(PT0, y0), slot(BN, y0), ALU.add).then_inc(*V.mark("yb"))
                        dve.wait_ge(*V.at("yb", i))
                        dve.tensor_tensor(slot(GZ, y0), slot(PT0, y0), slot(GZ, y0), ALU.mult).then_inc(*V.mark("ya"))
                each(dve, ph, turn)

            def branch_phase(l):
                ph = enter(dve, f"branch{l}", "V")
                A, V, PE = ph["A"], ph["V"], ph["PE"]
                c0 = cols(l)
                n = T - c0
                taps = conv_taps(l)

                def grid(k, t, horizontal=True):
                    return slot(k, CTX).rearrange("p (r w) -> p r w", w=GRID_W)

                def tap(j, o, m):
                    w = par_c("dw", j * TAPS + 15 + o)
                    lo, hi = max(0, -o), max(0, o)
                    ins = None
                    if c0 == 0:
                        ins = dve.scalar_tensor_tensor(out=slot(CY + j, lo, CTX - hi), in0=slot(CU + j, lo + o, CTX - hi + o),
                                                       scalar=w, in1=slot(CY + j, lo, CTX - hi), op0=ALU.mult, op1=ALU.add)
                    if l % 2 == 0:
                        y, u = grid(CY + j, 0), grid(CU + j, 0)
                        ins = dve.scalar_tensor_tensor(out=y[:, :, lo:GRID_W - hi], in0=u[:, :, lo + o:GRID_W - hi + o],
                                                       scalar=w, in1=y[:, :, lo:GRID_W - hi], op0=ALU.mult, op1=ALU.add)
                    else:
                        a, b, s = CTX + lo * GRID_W, T - hi * GRID_W, o * GRID_W
                        ins = dve.scalar_tensor_tensor(out=slot(CY + j, a, b), in0=slot(CU + j, a + s, b + s),
                                                       scalar=w, in1=slot(CY + j, a, b), op0=ALU.mult, op1=ALU.add)
                    return ins

                for j in range(CT):
                    dve.wait_ge(*A.at(f"cb{j}"))
                    dve.wait_ge(*PE.at(f"ca{j}"))
                    dve.tensor_tensor(slot(CU + j, c0), psum[:, (2 * j + 1) % 4, 0:n], slot(G0 + j % 2, c0), ALU.mult).then_inc(*V.mark(f"u{j}"))
                    dve.wait_ge(*V.at(f"u{j}"))
                    for m, o in enumerate(taps):
                        if m == 0:
                            dve.tensor_scalar(slot(CY + j, c0), slot(CU + j, c0), par_c("dw", j * TAPS + 15), par_c("dwb", j),
                                              ALU.mult, ALU.add).then_inc(*V.mark(f"y{j}_0"))
                        else:
                            dve.wait_ge(*V.at(f"y{j}_{m - 1}"))
                            tap(j, o, m).then_inc(*V.mark(f"y{j}_{m}"))
                for pre, mean, dst, tile in (("cc", "cmean", CY, 0), ("sc", "smean", SV, 2)):
                    dve.wait_ge(*PE.at(mean))
                    for j in range(CT):
                        dve.scalar_tensor_tensor(out=slot(dst + j, c0), in0=psum[:, tile, 0:n], scalar=-1.0 / CONV,
                                                 in1=slot(dst + j, c0), op0=ALU.mult, op1=ALU.add).then_inc(*V.mark(f"{pre}{j}"))
                for pre, r, dst, tmp in (("c", "cn", CY, G0), ("s", "sm", SV, G0 + 1)):
                    dve.wait_ge(*A.at(f"{pre}r"))
                    for j in range(CT):
                        dve.tensor_tensor(slot(dst + j, c0), slot(dst + j, c0), slot(tmp, c0), ALU.mult).then_inc(*V.mark(f"{r}{j}"))
                for j in range(CT):
                    dve.wait_ge(*PE.at(f"sp{j}"))
                    if j == 0:
                        dve.wait_ge(s_sgu, 32 * (l + 1))
                    dve.tensor_tensor(slot(H1 + j, 0, n).rearrange("p (c t) -> p c t", t=P),
                                      psum[:, j, 0:n].rearrange("p (c t) -> p c t", t=P),
                                      sgu_b[:, None, j * P:(j + 1) * P].to_broadcast([P, n // P, P]), ALU.add).then_inc(*V.mark(f"sp{j}"))
                    dve.wait_ge(*V.at(f"sp{j}"))
                    dve.tensor_tensor(slot(SU + j, c0), slot(SU + j, c0), slot(H1 + j, 0, n), ALU.mult).then_inc(*V.mark(f"uv{j}"))

            def merge_phase(l):
                ph = enter(dve, f"merge{l}", "V")
                A, V, PE, G = ph["A"], ph["V"], ph["PE"], ph["G"]
                c0 = cols(l)
                n = T - c0

                def turn(i):
                    k = 0
                    for q in range(MERGE_TILES):
                        for b in range(3):
                            dve.wait_ge(*PE.at(f"p{b}{q}", i))
                            dve.wait_ge(*A.at(f"g{b}{q}", i))
                            if b == 0:
                                dst = slot_at(M0, i, MERGE_TILES, q, c0)
                            else:
                                dst = slot(MTMP + b - 1, c0)
                                if q:
                                    dve.wait_ge(*G.at(f"m{b}{q - 1}", i))
                                else:
                                    dve.wait_ge(*G.at(f"m{b}{MERGE_TILES - 1}", i, back=1))
                            dve.tensor_tensor(dst, psum[:, (2 * k + 1) % 4, 0:n], slot(G0 + k % 3, c0), ALU.mult).then_inc(*V.mark(f"p{b}{q}"))
                            k += 1
                each(dve, ph, turn)

            def outproj_phase(key, c0, gate):
                per = len(phases[key]["PE"].names) // 4
                ph = enter(dve, key, "V")
                V, PE = ph["V"], ph["PE"]

                def turn(i):
                    for q in range(4):
                        dve.wait_ge(*PE.at(f"o{q}{per - 1}", i))
                        for s, a, b in segs(c0):
                            x = slot_at(X0, i, 4, q, a, b)
                            ins = dve.scalar_tensor_tensor(out=x, in0=psum[:, q, a - c0:b - c0],
                                                           scalar=mod[:, bass.ds(i * 8 + (2 * (gate * KT + q) + s), 1)],
                                                           in1=x, op0=ALU.mult, op1=ALU.add)
                        ins.then_inc(*V.mark(f"x{q}"))
                each(dve, ph, turn)

            def ffn_phase(l):
                ph = enter(dve, f"ffn{l}", "V")
                A, V, PE = ph["A"], ph["V"], ph["PE"]
                c0 = cols(l)
                n = T - c0

                def turn(i):
                    for q in range(2):
                        dve.wait_ge(*PE.at(f"u{q}", i))
                        dve.wait_ge(*A.at(f"s{q}", i))
                        dve.tensor_tensor(slot_at(ACT0, i, 2, q, c0), psum[:, 2 * q + 1, 0:n], slot(YA0 + q, c0), ALU.mult).then_inc(*V.mark(f"a{q}"))
                each(dve, ph, turn)

            for l in range(DEPTH):
                start = enter(dve, f"cond{l}", "V")
                dve.memset(cond, 0.0).then_inc(*start["V"].mark("zero"))
                modv_phase(l)
                if l == 0:
                    dve.wait_ge(s_load, 48)
                norm_phase(f"norm1_{l}", 0)
                lora_phase(l)
                for name, _, _ in PAIR_PHASES:
                    pair_phase(f"{name}{l}", l)
                branch_phase(l)
                merge_phase(l)
                dve.wait_ge(s_back, 32 * (l + 1))
                outproj_phase(f"res1_{l}", cols(l), 2)
                norm_phase(f"norm2_{l}", cols(l))
                ffn_phase(l)
                outproj_phase(f"res2_{l}", cols(l), 5)
            norm_phase("final", CTX, final=True)

        @block.gpsimd
        def _(pool):
            def pair_phase(key, l):
                ph = enter(pool, key, "G")
                A, V, PE, G = (ph.get(e) for e in ("A", "V", "PE", "G"))
                parts = ph["parts"]
                prep, scan = "prep" in parts, "scan" in parts
                y0 = cols(l)

                def turn(i):
                    def tt(name, out_, a, b, op):
                        settle(pool)
                        pool.tensor_tensor(out_, a, b, op).then_inc(*G.mark(name))

                    if scan:
                        wait_steps(pool, i, (A, "yn", 1))
                        settle(pool)
                        pool.tensor_copy(pp[:, 0:NPP], pp[:, NPP + 1:2 * NPP + 1]).then_inc(*G.mark("ppc"))
                    if prep:
                        if scan:
                            pool.wait_ge(*V.at("bon", i))
                            pool.wait_ge(*G.at("ppc", i))
                        arrived(pool, key, i, 2)
                        settle(pool)
                        pool.tensor_copy(pp[:, NPP + 1:2 * NPP + 1], ring[:, 2 * BW + 5 * P:2 * BW + 5 * P + NPP]).then_inc(*G.mark("pp"))
                        pool.wait_ge(*G.at("pp", i))
                        settle(pool)
                        pool.tensor_scalar(pp[:, NPP:NPP + 1], ppn("ka"), -1.0, 1.0, ALU.mult, ALU.add).then_inc(*G.mark("omk"))
                        pool.wait_ge(*V.at("L0", i))
                        tt("Le0", slot(F0 + F_KK), slot(LE0), slot(F0 + F_BE), ALU.subtract)
                        pool.wait_ge(*V.at("L1", i))
                        f = F0 + 6
                        total = by_chunk(slot(LE1))[:, :, C - 1:C].to_broadcast([P, NCH, C])
                        tt("Le1", by_chunk(slot(f + F_KK)), total, by_chunk(slot(LE1)), ALU.subtract)
                        pool.wait_ge(*G.at("Le1", i))
                        tt("Li1", slot(LE1), slot(f + F_KK), slot(f + F_BE), ALU.add)
                        for d in DIRS:
                            f = F0 + 6 * d
                            pool.wait_ge(*A.at(f"sa{d}", i))
                            settle(pool)
                            pool.tensor_scalar(slot(f + F_K), slot(f + F_KE), ppn("ka"), pp[:, NPP:NPP + 1], ALU.mult, ALU.add).then_inc(*G.mark(f"kt{d}"))
                            pool.wait_ge(*G.at(f"kt{d}", i))
                            pool.wait_ge(*V.at("kc", i))
                            tt(f"kd{d}", slot(f + F_K), slot(f + F_K), slot(K_), ALU.mult)
                    if scan:
                        for d in DIRS:
                            pool.wait_ge(*PE.at(f"U5{d}", i))
                            tt(f"D{d}", by_chunk(slot(M0_ + 11 * d + M_MT)), const_b(C_ID64, C),
                               decays[:, d * NCH:(d + 1) * NCH, None].to_broadcast([P, NCH, C]), ALU.mult)
                    if prep:
                        for d in DIRS:
                            f, le, ei = F0 + 6 * d, (LE0, LE1)[d], (EI0, EI1)[d]
                            pool.wait_ge(*G.at(f"kd{d}", i))
                            pool.wait_ge(*A.at(f"Ee{d}", i))
                            tt(f"kQ{d}", slot(f + F_K), slot(f + F_K), slot(le), ALU.mult)
                            end = C - 1 if d == 0 else 0
                            decay = by_chunk(slot(ei))[:, :, end:end + 1].to_broadcast([P, NCH, C])
                            pool.wait_ge(*V.at(f"bQ{d}", i))
                            tt(f"bE{d}", by_chunk(slot(f + F_BE)), by_chunk(slot(f + F_B)), decay, ALU.mult)
                            pool.wait_ge(*G.at(f"kQ{d}", i))
                            tt(f"kE{d}", by_chunk(slot(f + F_KE)), by_chunk(slot(f + F_K)), decay, ALU.mult)
                        for d in DIRS:
                            end = C - 1 if d == 0 else 0
                            if scan:
                                pool.wait_ge(*G.at(f"D{d}", i))
                            settle(pool)
                            pool.tensor_copy(decays[:, d * NCH:(d + 1) * NCH, None],
                                             by_chunk(slot((EI0, EI1)[d]))[:, :, end:end + 1]).then_inc(*G.mark(f"pc{d}"))
                    if scan:
                        pool.wait_ge(*V.at("ya", i))
                        settle(pool)
                        first = KT - 1 if key.startswith("last") else i
                        pool.dma_start(ya_v[:, bass.ds(first, 1), y0:T],
                                       arena[:, None, GZ * T + y0:GZ * T + T]).then_inc(s_ya, 16)
                        pool.wait_ge(s_ya, 16 * (first + (1 + KT * l)))
                        pool.wait_ge(*G.at("pc1" if prep else "D1", i))
                        pool.sem_inc(*G.mark("yst"))
                each(pool, ph, turn)

            def merge_phase(l):
                ph = enter(pool, f"merge{l}", "G")
                V, G = ph["V"], ph["G"]
                c0 = cols(l)

                def turn(i):
                    for q in range(MERGE_TILES):
                        m = slot_at(M0, i, MERGE_TILES, q, c0)
                        for b in (1, 2):
                            pool.wait_ge(*V.at(f"p{b}{q}", i))
                            if b == 2:
                                pool.wait_ge(*G.at(f"m1{q}", i))
                            settle(pool)
                            pool.tensor_tensor(m, m, slot(MTMP + b - 1, c0), ALU.add).then_inc(*G.mark(f"m{b}{q}"))
                each(pool, ph, turn)

            for l in range(DEPTH):
                for name, _, _ in PAIR_PHASES:
                    pair_phase(f"{name}{l}", l)
                merge_phase(l)


def seq(d):
    ctx, lat = list(range(CTX_CH)), list(range(CTX_CH, NCH))
    return ctx + lat if d == 0 else ctx[::-1] + lat[::-1]


def blocks(w):
    return w.reshape(-1, P, P).transpose(1, 0, 2).reshape(P, -1)


def tiled(v):
    return v.reshape(-1, P).T


def weight_stream(x):
    out = []

    def put(w):
        if w.shape[1] < BW:
            w = np.concatenate([w, np.zeros((P, BW - w.shape[1]), np.float32)], 1)
        out.append(w)

    def tile(w, col):
        return blocks(w[:, col:col + P])

    for l in range(DEPTH):
        w_in, up = x["w_in"][l], x["ffn_w_in"][l]
        for t in range(MOD_TURNS):
            for k in range(KT):
                for n in range(2):
                    put(x["w_mod"][l][k * P:k * P + P, (2 * t + n) * BW:(2 * t + n + 1) * BW])
        for off in (OFF_W, OFF_A, OFF_G):
            put(tile(w_in, off))
        put(np.zeros((P, BW), np.float32))
        for p in range(KT):
            s = slice(p * P, p * P + P)
            put(tile(w_in, p * P))
            put(tile(w_in, OFF_K + p * P))
            taps = [x["rwkv_shift"][l][t, off + p * P:off + p * P + P] for off in (0, OFF_K, OFF_V) for t in range(3)]
            vec = taps + [x["rwkv_w0"][l][0, s], x["rwkv_w0"][l][1, s], x["rwkv_a0"][l][0, s], x["rwkv_a0"][l][1, s],
                          x["rwkv_k_k"][l][s], x["rwkv_k_a"][l][s], x["rwkv_r_k"][l][s], x["rwkv_gn_g"][l][s],
                          x["rwkv_gn_b"][l][s]]
            ups = np.zeros((P, 4 * P), np.float32)
            for n, name in enumerate(("rwkv_w_up", "rwkv_a_up")):
                for d in DIRS:
                    ups[d * HD:(d + 1) * HD, (2 * n + d) * P:(2 * n + d + 1) * P] = x[name][l][d, :, s]
            put(np.concatenate([ups, x["rwkv_g_up"][l][:, s], np.stack(vec, 1)], 1))
            put(tile(w_in, OFF_V + p * P))
        for j in range(CT):
            put(tile(w_in, OFF_CONV + CONV + j * P))
            put(tile(w_in, OFF_CONV + j * P))
        for j in range(2 * CT):
            put(tile(w_in, OFF_SGU + j * P))
        for j in range(KT):
            put(tile(w_in, OFF_GATE + j * P))
            put(tile(x["rwkv_out"][l], j * P))
            put(tile(w_in, OFF_GATE + D + j * P))
            put(tile(w_in, OFF_GATE + 2 * D + j * P))
            put(np.concatenate([tile(x["conv_out"][l], j * P), tile(x["sgu_out"][l], j * P)], 1))
        for j in range(KT):
            put(tile(x["w_merge"][l], j * P))
        for j in range(FT):
            put(tile(up, j * P))
            put(tile(up, DFF + j * P))
        for j in range(KT):
            w = np.concatenate([tile(x["ffn_w_out"][l], j * P), np.zeros((P, 3 * BW - FT * P), np.float32)], 1)
            for n in range(3):
                put(w[:, n * BW:(n + 1) * BW])
    return np.concatenate(out, 0)


def parameters(x, l):
    cols = [tiled(x["b_mod"][l]), tiled(x["norm1_g"][l]), tiled(x["norm2_g"][l])]
    cols.append(np.stack([x["rwkv_shift"][l][t, off:off + P] for off in (OFF_W, OFF_A, OFF_G) for t in range(3)], 1))
    cols.append(x["conv_dw"][l].reshape(TAPS, CT, P).transpose(2, 1, 0).reshape(P, CT * TAPS))
    cols += [tiled(x[n][l]) for n in ("conv_dw_b", "conv_ln_g", "conv_ln_b", "sgu_ln_g", "sgu_ln_b")]
    cols.append(tiled(x["final_norm_g"]))
    return np.concatenate(cols, 1)


def constants():
    out = np.zeros((P, NCONST), np.float32)
    r = np.arange(P)
    out[r, C_ID64 + r % C] = 1
    out[r, C_ID + r] = 1
    out[r, C_ID_H + r % H] = 1
    out[:, C_ONES:C_ONES + P] = 1
    out[:, C_EPS:C_EPS + len(EPS)] = EPS
    out[:, C_HEADS:C_HEADS + P] = (r[:, None] // HD == r[None, :] // HD)
    a, b = r[:, None] % C, np.arange(C)[None, :]
    for d in DIRS:
        after = (b > a) if d == 0 else (b < a)
        for name in MASKS + MASKS_H:
            if name == "strict":
                m = 1.0 * after
            elif name == "incl":
                m = 1.0 * (after | (a == b))
            elif name == "first":
                m = -1.0 * (after & (a // 2 == b // 2))
            else:
                w = 2 ** int(name[2:])
                same = a // (2 * w) == b // (2 * w)
                up, lo = a % (2 * w) >= w, b % (2 * w) < w
                m = 1.0 * (same & ((up & lo) if d == 0 else (~up & ~lo)))
            if name in MASKS:
                at = C_MASK + (d * len(MASKS) + MASKS.index(name)) * C
                out[:, at:at + C] = m
            else:
                at = C_MASK_H + (d * len(MASKS_H) + MASKS_H.index(name)) * H
                own = a // H * H + np.arange(H)[None, :]
                out[:, at:at + H] = np.take_along_axis(m, own, 1)
    mask = np.ones((P, T), np.float32)
    mask[:, ::C] = 0
    return out, mask


def kernel(**inputs):
    import concourse.bacc as _bacc
    from concourse.bass_utils import run_bass_kernel_spmd as _run

    x = {k: np.asarray(v) for k, v in inputs.items()}
    const, scanmask = constants()
    tokens = np.concatenate([x["ctx"][0], x["x"][0]], 0)
    arrays = {
        "x": tokens.reshape(T, KT, P).transpose(2, 1, 0).reshape(P, KT * T),
        "c": np.stack([x["c_ctx"], x["c"][0]], 1).reshape(KT, P, 2).transpose(1, 0, 2).reshape(P, 2 * KT),
        "w_stream": weight_stream(x),
        "par": np.stack([parameters(x, l) for l in range(DEPTH)]),
        "const": const,
        "scanmask": scanmask,
        "sgu_w": x["sgu_w"].transpose(0, 3, 1, 2).reshape(DEPTH, P, GROUPS * P),
        "sgu_b": np.repeat(x["sgu_b"].reshape(DEPTH, CT, 2, P), HD, axis=2).transpose(0, 2, 1, 3).reshape(DEPTH, P, CT * P),
    }
    arrays = {f"{k}_in": np.ascontiguousarray(v) for k, v in arrays.items()}
    nc = _bacc.Bacc("TRN2", target_bir_lowering=False, num_devices=1)
    args = [nc.dram_tensor(k, v.shape, F32, kind="ExternalInput").ap() for k, v in arrays.items()]
    out = nc.dram_tensor("out", (P, KT, LAT), F32, kind="ExternalOutput").ap()
    build(nc, *args, out)
    r = _run(nc, [arrays], core_ids=[0])
    y = r.results[0]["out"]
    return y.transpose(2, 1, 0).reshape(1, LAT, D)
```
